# Optimizing a Trainium2 kernel written in Bass

```python
import jax, jax.numpy as jnp
from jax import lax
import numpy as np
import math
import jax
import jax.numpy as jnp

D_MODEL = 1024
BATCH = 1
SEQ = 256
DEPTH = 2

GRID_W = 64
CTX_LEN = 256
EPS = 1e-6
ROPE_BASE = 10000.0

MLA_HEADS = 8
MLA_Q_RANK = D_MODEL // 4
MLA_KV_RANK = D_MODEL // 8
MLA_NOPE = 64
MLA_ROPE = 32
MLA_V = 64
MLA_IN = MLA_Q_RANK + MLA_KV_RANK + MLA_ROPE
MLA_SCALE = (MLA_NOPE + MLA_ROPE) ** -0.5
Q_BLOCK = 128

CONV_DIM = D_MODEL // 2
CONV_WIDTH = 3
EVEN_IN = MLA_IN + 3 * CONV_DIM
EVEN_MIX = MLA_HEADS * MLA_V + CONV_DIM

ML_HEADS = 4
ML_DQK = D_MODEL // 8
ML_DV = D_MODEL // 4
ML_CHUNK = 64
ML_QKVG = ML_HEADS * (2 * ML_DQK + ML_DV) + 4 * ML_HEADS
ML_MIX = ML_HEADS * ML_DV
ODD_IN = ML_QKVG + ML_MIX
F_BIAS = 3.0

PEER_HEADS = 8
PEER_NKEYS = 128
PEER_N = PEER_NKEYS * PEER_NKEYS
PEER_DKEY = 256
PEER_DHALF = PEER_DKEY // 2
PEER_TOPK = 16
PEER_BLOCK = 128


def rmsnorm(x, g):
    x32 = x.astype(jnp.float32)
    y = x32 * lax.rsqrt(jnp.mean(x32 * x32, axis=-1, keepdims=True) + EPS)
    return (y * g.astype(jnp.float32)).astype(x.dtype)

def modulate(h, shift, scale):
    return h * (1 + scale) + shift

def axial_rope(rows, dim):
    n_freq = dim // 4
    inv = ROPE_BASE ** (-jnp.arange(n_freq, dtype=jnp.float32) / n_freq)
    row = jnp.repeat(jnp.arange(rows, dtype=jnp.float32), GRID_W)
    col = jnp.tile(jnp.arange(GRID_W, dtype=jnp.float32), rows)
    ang = jnp.concatenate([row[:, None] * inv, col[:, None] * inv], axis=-1)
    return jnp.cos(ang), jnp.sin(ang)

def apply_rope(x, cos, sin):
    half = x.shape[-1] // 2
    x32 = x.astype(jnp.float32)
    x1, x2 = x32[..., :half], x32[..., half:]
    return jnp.concatenate([x1 * cos - x2 * sin, x1 * sin + x2 * cos], axis=-1).astype(x.dtype)

def mla_q(p_q, q_norm, w_uq, cos, sin):
    B, T, _ = p_q.shape
    q = (rmsnorm(p_q, q_norm) @ w_uq).reshape(B, T, MLA_HEADS, MLA_NOPE + MLA_ROPE)
    q_n, q_r = q[..., :MLA_NOPE], q[..., MLA_NOPE:]
    if cos is not None:
        q_r = apply_rope(q_r, cos[:, None, :], sin[:, None, :])
    return q_n, q_r

def mla_kv(p_kv, kv_norm, w_ukv, cos, sin):
    B, T, _ = p_kv.shape
    kv = (rmsnorm(p_kv[..., :MLA_KV_RANK], kv_norm) @ w_ukv).reshape(B, T, MLA_HEADS, MLA_NOPE + MLA_V)
    k_r = p_kv[..., MLA_KV_RANK:]
    if cos is not None:
        k_r = apply_rope(k_r, cos, sin)
    return kv[..., :MLA_NOPE], k_r, kv[..., MLA_NOPE:]

def mla_attend(q_n, q_r, k_n, k_r, v):
    s = jnp.einsum('bqhd,bkhd->bhqk', q_n, k_n) + jnp.einsum('bqhr,bkr->bhqk', q_r, k_r)
    p = jax.nn.softmax(s.astype(jnp.float32) * MLA_SCALE, axis=-1).astype(v.dtype)
    out = jnp.einsum('bhqk,bkhd->bqhd', p, v)
    return out.reshape(out.shape[0], out.shape[1], MLA_HEADS * MLA_V)

def short_conv(p, conv_w):
    T = p.shape[1]
    b_gate, c_gate, u = p[..., :CONV_DIM], p[..., CONV_DIM:2 * CONV_DIM], p[..., 2 * CONV_DIM:]
    z = jnp.pad(c_gate * u, ((0, 0), (1, 1), (0, 0)))
    y = conv_w[0] * z[:, :T] + conv_w[1] * z[:, 1:T + 1] + conv_w[2] * z[:, 2:]
    return b_gate * y

def even_mixer(nc, nl, w_in, q_norm, kv_norm, w_uq, w_ukv, conv_w, w_out, cos, sin, need_ctx):
    B, S, _ = nl.shape
    pl = nl @ w_in
    if need_ctx:
        pc = nc @ w_in
        pc_kv = pc[..., MLA_Q_RANK:MLA_IN]
    else:
        pc_kv = nc @ w_in[:, MLA_Q_RANK:MLA_IN]
    qn_l, qr_l = mla_q(pl[..., :MLA_Q_RANK], q_norm, w_uq, cos, sin)
    kn_l, kr_l, v_l = mla_kv(pl[..., MLA_Q_RANK:MLA_IN], kv_norm, w_ukv, cos, sin)
    kn_c, kr_c, v_c = mla_kv(pc_kv, kv_norm, w_ukv, None, None)
    kn = jnp.concatenate([kn_l, kn_c], axis=1)
    kr = jnp.concatenate([kr_l, kr_c], axis=1)
    vv = jnp.concatenate([v_l, v_c], axis=1)
    blocks = lambda a: jnp.moveaxis(a.reshape((B, S // Q_BLOCK, Q_BLOCK) + a.shape[2:]), 1, 0)
    ol = lax.map(lambda qb: mla_attend(qb[0], qb[1], kn, kr, vv), (blocks(qn_l), blocks(qr_l)))
    ol = jnp.moveaxis(ol, 0, 1).reshape(B, S, MLA_HEADS * MLA_V)
    yl = jnp.concatenate([ol, short_conv(pl[..., MLA_IN:], conv_w)], axis=-1) @ w_out
    yc = None
    if need_ctx:
        qn_c, qr_c = mla_q(pc[..., :MLA_Q_RANK], q_norm, w_uq, None, None)
        oc = mla_attend(qn_c, qr_c, kn_c, kr_c, v_c)
        yc = jnp.concatenate([oc, short_conv(pc[..., MLA_IN:], conv_w)], axis=-1) @ w_out
    return yc, yl

def mlstm_inputs(p, gate_b):
    B, T, _ = p.shape
    qk, vd = ML_HEADS * ML_DQK, ML_HEADS * ML_DV
    heads = lambda a, d: a.reshape(B, T, ML_HEADS, d).transpose(0, 2, 1, 3)
    q = heads(p[..., :qk], ML_DQK) * (ML_DQK ** -0.5)
    k = heads(p[..., qk:2 * qk], ML_DQK)
    v = heads(p[..., 2 * qk:2 * qk + vd], ML_DV)
    g = p[..., 2 * qk + vd:ML_QKVG].astype(jnp.float32) + gate_b.astype(jnp.float32)
    g = g.reshape(B, T, 4, ML_HEADS).transpose(2, 0, 3, 1)
    return q, k, v, g

def mlstm_scan(q, k, v, ig, lf, state, with_output):
    B, H, T, _ = q.shape
    L = ML_CHUNK
    nc = T // L
    chunks = lambda a: jnp.moveaxis(a.reshape(a.shape[:2] + (nc, L) + a.shape[3:]), 2, 0)
    xs = (chunks(q), chunks(k), chunks(v), chunks(ig), chunks(lf))
    causal = jnp.tril(jnp.ones((L, L), dtype=bool))

    def step(carry, xc):
        C, n, m = carry
        qc, kc, vc, ic, fc = xc
        b = jnp.cumsum(fc, axis=-1)
        b_end = b[..., -1]
        a = ic + b_end[..., None] - b
        m_new = jnp.maximum(b_end + m, jnp.max(a, axis=-1))
        w_s = jnp.exp(a - m_new[..., None])
        decay = jnp.exp(b_end + m - m_new)
        C_new = decay[..., None, None] * C + jnp.einsum('bhs,bhsk,bhsv->bhkv', w_s, kc, vc)
        n_new = decay[..., None] * n + jnp.einsum('bhs,bhsk->bhk', w_s, kc)
        if with_output:
            dmat = jnp.where(causal, b[..., :, None] - b[..., None, :] + ic[..., None, :], -jnp.inf)
            m_t = jnp.maximum(b + m[..., None], jnp.max(dmat, axis=-1))
            inter = jnp.exp(b + m[..., None] - m_t)
            sc = jnp.einsum('bhtk,bhsk->bhts', qc, kc) * jnp.exp(dmat - m_t[..., None])
            num = jnp.einsum('bhts,bhsv->bhtv', sc, vc) + inter[..., None] * jnp.einsum('bhtk,bhkv->bhtv', qc, C)
            den = jnp.sum(sc, axis=-1) + inter * jnp.einsum('bhtk,bhk->bht', qc, n)
            h = num / jnp.maximum(jnp.abs(den), jnp.exp(-m_t))[..., None]
        else:
            h = None
        return (C_new, n_new, m_new), h

    state, hs = lax.scan(step, state, xs)
    if with_output:
        hs = jnp.moveaxis(hs, 0, 2).reshape(B, H, T, ML_DV)
    return state, hs

def odd_mixer(nc, nl, w_in, gate_b, head_g, w_out, need_ctx):
    pc = nc @ (w_in if need_ctx else w_in[:, :ML_QKVG])
    pl = nl @ w_in
    qc, kc, vc, gc = mlstm_inputs(pc, gate_b)
    ql, kl, vl, gl = mlstm_inputs(pl, gate_b)
    B = nl.shape[0]
    zero = (jnp.zeros((B, ML_HEADS, ML_DQK, ML_DV), jnp.float32),
            jnp.zeros((B, ML_HEADS, ML_DQK), jnp.float32),
            jnp.zeros((B, ML_HEADS), jnp.float32))
    flip = lambda a: jnp.flip(a, axis=2)
    h_c, h_l = None, None
    for d in range(2):
        ctx_seq = (qc, kc, vc, gc[2 * d], jax.nn.log_sigmoid(gc[2 * d + 1]))
        lat_seq = (ql, kl, vl, gl[2 * d], jax.nn.log_sigmoid(gl[2 * d + 1]))
        if d == 1:
            ctx_seq = tuple(flip(a) for a in ctx_seq)
            lat_seq = tuple(flip(a) for a in lat_seq)
        state, hc_d = mlstm_scan(*ctx_seq, zero, need_ctx)
        _, hl_d = mlstm_scan(*lat_seq, state, True)
        if d == 1:
            hl_d = flip(hl_d)
            hc_d = flip(hc_d) if need_ctx else None
        h_l = hl_d if h_l is None else h_l + hl_d
        if need_ctx:
            h_c = hc_d if h_c is None else h_c + hc_d

    def readout(h, p):
        Bh, _, T, _ = h.shape
        h = h.transpose(0, 2, 1, 3).astype(p.dtype)
        h = rmsnorm(h, head_g.reshape(ML_HEADS, ML_DV)).reshape(Bh, T, ML_MIX)
        return (jax.nn.sigmoid(p[..., ML_QKVG:]) * h) @ w_out

    yl = readout(h_l, pl)
    yc = readout(h_c, pc) if need_ctx else None
    return yc, yl

def peer(h, w_q, subkeys, u, v):
    B, T, D = h.shape
    tok = h.reshape(-1, PEER_BLOCK, D)

    def block(xb):
        q = (xb @ w_q).reshape(PEER_BLOCK, PEER_HEADS, 2, PEER_DHALF)
        s = jnp.einsum('thpd,hpkd->thpk', q, subkeys).astype(jnp.float32)
        s1, i1 = lax.top_k(s[:, :, 0], PEER_TOPK)
        s2, i2 = lax.top_k(s[:, :, 1], PEER_TOPK)
        cand = (s1[..., :, None] + s2[..., None, :]).reshape(PEER_BLOCK, PEER_HEADS, PEER_TOPK * PEER_TOPK)
        cidx = (i1[..., :, None] * PEER_NKEYS + i2[..., None, :]).reshape(PEER_BLOCK, PEER_HEADS, PEER_TOPK * PEER_TOPK)
        top, pos = lax.top_k(cand, PEER_TOPK)
        idx = jnp.take_along_axis(cidx, pos, axis=-1)
        g = jax.nn.softmax(top, axis=-1)
        ue, ve = u[idx], v[idx]
        act = jax.nn.gelu(jnp.einsum('td,thkd->thk', xb, ue).astype(jnp.float32), approximate=False)
        return jnp.einsum('thk,thkd->td', (g * act).astype(xb.dtype), ve)

    return lax.map(block, tok).reshape(B, T, D)

def first_inputs(seed: int = 0) -> dict:
    key = jax.random.key(seed)
    ks = iter(jax.random.split(key, 32))
    nrm = lambda shape, s: jax.random.normal(next(ks), shape, jnp.float32) * s
    n_even = (DEPTH + 1) // 2
    n_odd = DEPTH // 2
    D = D_MODEL
    gate_b = (nrm((n_odd, 4, ML_HEADS), 0.1)
              + jnp.array([0.0, F_BIAS, 0.0, F_BIAS], jnp.float32)[:, None]).reshape(n_odd, 4 * ML_HEADS)
    return {
        'x': nrm((BATCH, SEQ, D), 1.0),
        'c': nrm((BATCH, D), 1.0),
        'ctx': nrm((BATCH, CTX_LEN, D), 1.0),
        'c_ctx': nrm((D,), 1.0),
        'norm1_g': 1.0 + nrm((DEPTH, D), 0.02),
        'norm2_g': 1.0 + nrm((DEPTH, D), 0.02),
        'w_mod': nrm((DEPTH, D, 6 * D), 0.5 * D ** -0.5),
        'b_mod': nrm((DEPTH, 6 * D), 0.02),
        'even_w_in': nrm((n_even, D, EVEN_IN), D ** -0.5),
        'mla_q_norm': 1.0 + nrm((n_even, MLA_Q_RANK), 0.02),
        'mla_kv_norm': 1.0 + nrm((n_even, MLA_KV_RANK), 0.02),
        'mla_w_uq': nrm((n_even, MLA_Q_RANK, MLA_HEADS * (MLA_NOPE + MLA_ROPE)), MLA_Q_RANK ** -0.5),
        'mla_w_ukv': nrm((n_even, MLA_KV_RANK, MLA_HEADS * (MLA_NOPE + MLA_V)), MLA_KV_RANK ** -0.5),
        'conv_w': nrm((n_even, CONV_WIDTH, CONV_DIM), CONV_WIDTH ** -0.5),
        'even_w_out': nrm((n_even, EVEN_MIX, D), EVEN_MIX ** -0.5),
        'odd_w_in': nrm((n_odd, D, ODD_IN), D ** -0.5),
        'mlstm_gate_b': gate_b,
        'mlstm_head_g': 1.0 + nrm((n_odd, ML_MIX), 0.02),
        'odd_w_out': nrm((n_odd, ML_MIX, D), ML_MIX ** -0.5),
        'peer_w_q': nrm((DEPTH, D, PEER_HEADS * PEER_DKEY), D ** -0.5),
        'peer_subkeys': nrm((DEPTH, PEER_HEADS, 2, PEER_NKEYS, PEER_DHALF), PEER_DHALF ** -0.5),
        'peer_u': nrm((DEPTH, PEER_N, D), D ** -0.5),
        'peer_v': nrm((DEPTH, PEER_N, D), PEER_HEADS ** -0.5),
        'norm_f_g': 1.0 + nrm((D,), 0.02),
    }

def first_block(x, c, ctx, c_ctx, norm1_g, norm2_g, w_mod, b_mod,
              even_w_in, mla_q_norm, mla_kv_norm, mla_w_uq, mla_w_ukv, conv_w, even_w_out,
              odd_w_in, mlstm_gate_b, mlstm_head_g, odd_w_out,
              peer_w_q, peer_subkeys, peer_u, peer_v, norm_f_g):
    B, S, D = x.shape
    rows = S // GRID_W
    cos, sin = axial_rope(rows, MLA_ROPE)
    hl, hc = x, ctx
    n_ctx = ctx.shape[1]
    for i in range(DEPTH):
        last = i == DEPTH - 1
        j = i // 2
        mod_l = [m[:, None, :] for m in jnp.split(jax.nn.silu(c) @ w_mod[i] + b_mod[i], 6, axis=-1)]
        mod_c = jnp.split(jax.nn.silu(c_ctx) @ w_mod[i] + b_mod[i], 6, axis=-1)
        nl = modulate(rmsnorm(hl, norm1_g[i]), mod_l[0], mod_l[1])
        nc = modulate(rmsnorm(hc, norm1_g[i]), mod_c[0], mod_c[1])
        if i % 2 == 0:
            yc, yl = even_mixer(nc, nl, even_w_in[j], mla_q_norm[j], mla_kv_norm[j], mla_w_uq[j],
                                mla_w_ukv[j], conv_w[j], even_w_out[j], cos, sin, not last)
        else:
            yc, yl = odd_mixer(nc, nl, odd_w_in[j], mlstm_gate_b[j], mlstm_head_g[j], odd_w_out[j], not last)
        hl = hl + mod_l[2] * yl
        nl = modulate(rmsnorm(hl, norm2_g[i]), mod_l[3], mod_l[4])
        if last:
            hl = hl + mod_l[5] * peer(nl, peer_w_q[i], peer_subkeys[i], peer_u[i], peer_v[i])
        else:
            hc = hc + mod_c[2] * yc
            nc = modulate(rmsnorm(hc, norm2_g[i]), mod_c[3], mod_c[4])
            ff = peer(jnp.concatenate([nc, nl], axis=1), peer_w_q[i], peer_subkeys[i], peer_u[i], peer_v[i])
            hc = hc + mod_c[5] * ff[:, :n_ctx]
            hl = hl + mod_l[5] * ff[:, n_ctx:]
    return rmsnorm(hl, norm_f_g)


PLE_DIM = 256
D_FF = 2816
NORM_EPS = 1e-6
NEG_INF = -1e30
NUM_BUCKETS = 32
MAX_DISTANCE = 128
A_HEADS = 4
A_HEAD_DIM = 64
A_QBLOCK = 128
B_HEADS = 8
B_GROUPS = 2
B_REP = B_HEADS // B_GROUPS
B_HEAD_DIM = 64
B_CMP_LEN = 32
B_CMP_STRIDE = 16
B_CMP_HIDDEN = 256
B_SEL_BLOCK = 64
B_SEL_TOPK = 16
B_WINDOW = 512
B_QBLOCK = 64
B_SEL_FORCE = 1e6
C_HEADS = 8
C_GROUPS = 2
C_REP = C_HEADS // C_GROUPS
C_HEAD_DIM = 64
C_WINDOW = 128
C_QBLOCK = 128

A_WIDTH = A_HEADS * 2 * A_HEAD_DIM
B_WIDTH = B_HEADS * B_HEAD_DIM
B_KV = B_GROUPS * B_HEAD_DIM
C_WIDTH = C_HEADS * C_HEAD_DIM
C_KV = C_GROUPS * C_HEAD_DIM
N_BIAS_HEADS = A_HEADS + B_HEADS + C_HEADS
IN_SPLITS = (A_WIDTH, A_WIDTH, A_WIDTH,
             B_WIDTH, B_KV, B_KV, B_KV, B_KV, B_KV, B_KV, 3 * B_HEADS,
             C_WIDTH, C_KV, C_KV,
             D_MODEL, D_MODEL, D_MODEL)
D_IN = 3 * A_WIDTH + B_WIDTH + 6 * B_KV + 3 * B_HEADS + C_WIDTH + 2 * C_KV + 3 * D_MODEL


def rms_norm(x, g):
    xf = x.astype(jnp.float32)
    y = xf * lax.rsqrt(jnp.mean(xf * xf, axis=-1, keepdims=True) + NORM_EPS)
    return (y * g.astype(jnp.float32)).astype(x.dtype)

def swiglu(x, wi, wo):
    gate, up = jnp.split(x @ wi, 2, axis=-1)
    return (jax.nn.silu(gate) * up) @ wo

def split_cols(z, sizes):
    outs, start = [], 0
    for s in sizes:
        outs.append(z[..., start:start + s])
        start += s
    return outs

def rel_bucket(dist):
    n = jnp.maximum(dist, 0)
    max_exact = NUM_BUCKETS // 2
    nf = jnp.maximum(n, 1).astype(jnp.float32)
    large = max_exact + (jnp.log(nf / max_exact) / math.log(MAX_DISTANCE / max_exact)
                         * (NUM_BUCKETS - max_exact)).astype(jnp.int32)
    large = jnp.minimum(large, NUM_BUCKETS - 1)
    return jnp.where(n < max_exact, n, large)

def head_bias(table, dist):
    return jnp.moveaxis(table[rel_bucket(dist)].astype(jnp.float32), -1, 0)

def grouped_head_bias(table, dist, groups, rep):
    b = head_bias(table, dist)
    return b.reshape((groups, rep) + dist.shape)

def masked_softmax(s, mask):
    return jax.nn.softmax(jnp.where(mask, s, NEG_INF), axis=-1) * mask

def diff_attention(q, k, v, bias_table, lam, lam_init, subln_g):
    bsz, seq = q.shape[:2]
    nblk = seq // A_QBLOCK
    scale = A_HEAD_DIM ** -0.5
    qb = q.reshape(bsz, nblk, A_QBLOCK, A_HEADS, 2, A_HEAD_DIM).swapaxes(0, 1)
    kpos = jnp.arange(seq)

    def block(args):
        i, qi = args
        qpos = i * A_QBLOCK + jnp.arange(A_QBLOCK)
        dist = qpos[:, None] - kpos[None, :]
        s = jnp.einsum('bqhcd,bkhcd->bchqk', qi, k, preferred_element_type=jnp.float32) * scale
        s = s + head_bias(bias_table, dist)[None, None]
        pr = masked_softmax(s, dist >= 0)
        attn = pr[:, 0] - lam * pr[:, 1]
        return jnp.einsum('bhqk,bkhe->bqhe', attn.astype(v.dtype), v)

    o = lax.map(block, (jnp.arange(nblk), qb))
    o = o.swapaxes(0, 1).reshape(bsz, seq, A_HEADS, 2 * A_HEAD_DIM)
    o = rms_norm(o, subln_g) * (1.0 - lam_init)
    return o.reshape(bsz, seq, A_WIDTH)

def nsa_attention(q, kc, vc, ks, vs, kw, vw, gates, bias_table, cmp_pos, cmp_w1, cmp_w2):
    bsz, seq = q.shape[:2]
    scale = B_HEAD_DIM ** -0.5
    n_chunk = seq // B_CMP_STRIDE
    n_cmp = n_chunk - 1
    n_sel = seq // B_SEL_BLOCK
    top_k = min(B_SEL_TOPK, n_sel)
    nblk = seq // B_QBLOCK

    def compress(t, pos, w1, w2):
        c = t.reshape(bsz, n_chunk, B_CMP_STRIDE, B_GROUPS, B_HEAD_DIM)
        blk = jnp.concatenate([c[:, :-1], c[:, 1:]], axis=2) + pos[None, None, :, None, :]
        blk = blk.transpose(0, 1, 3, 2, 4).reshape(bsz, n_cmp, B_GROUPS, B_CMP_LEN * B_HEAD_DIM)
        return jax.nn.gelu(blk @ w1) @ w2

    k_cmp = compress(kc, cmp_pos[0], cmp_w1[0], cmp_w2[0])
    v_cmp = compress(vc, cmp_pos[1], cmp_w1[1], cmp_w2[1])
    cmp_start = jnp.arange(n_cmp) * B_CMP_STRIDE
    cmp_end = cmp_start + B_CMP_LEN - 1
    sel_start = jnp.arange(n_sel) * B_SEL_BLOCK
    overlap = ((cmp_start[:, None] < sel_start[None, :] + B_SEL_BLOCK)
               & (cmp_start[:, None] + B_CMP_LEN > sel_start[None, :])).astype(jnp.float32)
    ks_blk = ks.reshape(bsz, n_sel, B_SEL_BLOCK, B_GROUPS, B_HEAD_DIM).transpose(0, 3, 1, 2, 4)
    vs_blk = vs.reshape(bsz, n_sel, B_SEL_BLOCK, B_GROUPS, B_HEAD_DIM).transpose(0, 3, 1, 2, 4)
    kw_pad = jnp.pad(kw, ((0, 0), (B_WINDOW, 0), (0, 0), (0, 0)))
    vw_pad = jnp.pad(vw, ((0, 0), (B_WINDOW, 0), (0, 0), (0, 0)))
    tbg = bias_table.reshape(NUM_BUCKETS, B_GROUPS, B_REP).transpose(1, 0, 2)
    b_idx = jnp.arange(bsz)[:, None, None, None]
    g_idx = jnp.arange(B_GROUPS)[None, :, None, None]
    blk_id = jnp.arange(n_sel)
    qb = q.reshape(bsz, nblk, B_QBLOCK, B_GROUPS, B_REP, B_HEAD_DIM).swapaxes(0, 1)
    gb = gates.reshape(bsz, nblk, B_QBLOCK, B_GROUPS, B_REP, 3).swapaxes(0, 1)

    def block(args):
        i, qi, gi = args
        qpos = i * B_QBLOCK + jnp.arange(B_QBLOCK)
        dist_c = qpos[:, None] - cmp_end[None, :]
        s_c = jnp.einsum('bqgrd,bngd->bgrqn', qi, k_cmp, preferred_element_type=jnp.float32) * scale
        s_c = s_c + grouped_head_bias(bias_table, dist_c, B_GROUPS, B_REP)
        p_c = masked_softmax(s_c, dist_c >= 0)
        o_c = jnp.einsum('bgrqn,bngd->bqgrd', p_c.astype(v_cmp.dtype), v_cmp)
        imp = jnp.einsum('bgrqn,nm->bgqm', p_c, overlap)
        cur = qpos // B_SEL_BLOCK
        forced = (blk_id[None, :] == 0) | (blk_id[None, :] == cur[:, None]) | (blk_id[None, :] == cur[:, None] - 1)
        future = blk_id[None, :] > cur[:, None]
        imp = jnp.where(forced, B_SEL_FORCE, jnp.where(future, -B_SEL_FORCE, imp))
        _, idx = lax.top_k(imp, top_k)
        n_keys = top_k * B_SEL_BLOCK
        k_sel = ks_blk[b_idx, g_idx, idx].reshape(bsz, B_GROUPS, B_QBLOCK, n_keys, B_HEAD_DIM)
        v_sel = vs_blk[b_idx, g_idx, idx].reshape(bsz, B_GROUPS, B_QBLOCK, n_keys, B_HEAD_DIM)
        kpos_s = (idx[..., None] * B_SEL_BLOCK + jnp.arange(B_SEL_BLOCK)).reshape(bsz, B_GROUPS, B_QBLOCK, n_keys)
        dist_s = qpos[None, None, :, None] - kpos_s
        bias_s = tbg[g_idx, rel_bucket(dist_s)].astype(jnp.float32).transpose(0, 1, 4, 2, 3)
        s_s = jnp.einsum('bqgrd,bgqld->bgrql', qi, k_sel, preferred_element_type=jnp.float32) * scale + bias_s
        p_s = masked_softmax(s_s, (dist_s >= 0)[:, :, None])
        o_s = jnp.einsum('bgrql,bgqld->bqgrd', p_s.astype(v_sel.dtype), v_sel)
        start = i * B_QBLOCK
        k_win = lax.dynamic_slice_in_dim(kw_pad, start, B_WINDOW + B_QBLOCK, axis=1)
        v_win = lax.dynamic_slice_in_dim(vw_pad, start, B_WINDOW + B_QBLOCK, axis=1)
        kpos_w = start - B_WINDOW + jnp.arange(B_WINDOW + B_QBLOCK)
        dist_w = qpos[:, None] - kpos_w[None, :]
        mask_w = (dist_w >= 0) & (dist_w < B_WINDOW) & (kpos_w >= 0)[None, :]
        s_w = jnp.einsum('bqgrd,bkgd->bgrqk', qi, k_win, preferred_element_type=jnp.float32) * scale
        s_w = s_w + grouped_head_bias(bias_table, dist_w, B_GROUPS, B_REP)
        p_w = masked_softmax(s_w, mask_w)
        o_w = jnp.einsum('bgrqk,bkgd->bqgrd', p_w.astype(v_win.dtype), v_win)
        return gi[..., 0:1] * o_c + gi[..., 1:2] * o_s + gi[..., 2:3] * o_w

    o = lax.map(block, (jnp.arange(nblk), qb, gb))
    return o.swapaxes(0, 1).reshape(bsz, seq, B_WIDTH)

def swa_sink_attention(q, k, v, bias_table, sinks):
    bsz, seq = q.shape[:2]
    scale = C_HEAD_DIM ** -0.5
    nblk = seq // C_QBLOCK
    k_pad = jnp.pad(k, ((0, 0), (C_WINDOW, 0), (0, 0), (0, 0)))
    v_pad = jnp.pad(v, ((0, 0), (C_WINDOW, 0), (0, 0), (0, 0)))
    qb = q.reshape(bsz, nblk, C_QBLOCK, C_GROUPS, C_REP, C_HEAD_DIM).swapaxes(0, 1)
    sink = jnp.broadcast_to(sinks.astype(jnp.float32).reshape(C_GROUPS, C_REP, 1, 1),
                            (bsz, C_GROUPS, C_REP, C_QBLOCK, 1))

    def block(args):
        i, qi = args
        start = i * C_QBLOCK
        qpos = start + jnp.arange(C_QBLOCK)
        kb = lax.dynamic_slice_in_dim(k_pad, start, C_WINDOW + C_QBLOCK, axis=1)
        vb = lax.dynamic_slice_in_dim(v_pad, start, C_WINDOW + C_QBLOCK, axis=1)
        kpos = start - C_WINDOW + jnp.arange(C_WINDOW + C_QBLOCK)
        dist = qpos[:, None] - kpos[None, :]
        mask = (dist >= 0) & (dist < C_WINDOW) & (kpos >= 0)[None, :]
        s = jnp.einsum('bqgrd,bkgd->bgrqk', qi, kb, preferred_element_type=jnp.float32) * scale
        s = jnp.where(mask, s + grouped_head_bias(bias_table, dist, C_GROUPS, C_REP), NEG_INF)
        pr = jax.nn.softmax(jnp.concatenate([s, sink], axis=-1), axis=-1)[..., :-1]
        return jnp.einsum('bgrqk,bkgd->bqgrd', pr.astype(vb.dtype), vb)

    o = lax.map(block, (jnp.arange(nblk), qb))
    return o.swapaxes(0, 1).reshape(bsz, seq, C_WIDTH)

def second_inputs(seed: int = 0) -> dict:
    key = jax.random.key(seed)
    ks = jax.random.split(key, 20)

    def nrm(k, shape, scale):
        return jax.random.normal(k, shape, jnp.float32) * scale

    return {
        'x': nrm(ks[0], (BATCH, SEQ, D_MODEL), 1.0),
        'p': nrm(ks[1], (DEPTH, BATCH, SEQ, PLE_DIM), 1.0),
        'norm_g': 1.0 + nrm(ks[2], (DEPTH, 4, D_MODEL), 0.05),
        'ffn1_wi': nrm(ks[3], (DEPTH, D_MODEL, 2 * D_FF), D_MODEL ** -0.5),
        'ffn1_wo': nrm(ks[4], (DEPTH, D_FF, D_MODEL), D_FF ** -0.5),
        'w_in': nrm(ks[5], (DEPTH, D_MODEL, D_IN), D_MODEL ** -0.5),
        'diff_lambda': nrm(ks[6], (DEPTH, 4, A_HEAD_DIM), 0.1),
        'diff_subln': 1.0 + nrm(ks[7], (DEPTH, 2 * A_HEAD_DIM), 0.05),
        'nsa_cmp_pos': nrm(ks[8], (DEPTH, 2, B_CMP_LEN, B_HEAD_DIM), 0.1),
        'nsa_cmp_w1': nrm(ks[9], (DEPTH, 2, B_CMP_LEN * B_HEAD_DIM, B_CMP_HIDDEN), (B_CMP_LEN * B_HEAD_DIM) ** -0.5),
        'nsa_cmp_w2': nrm(ks[10], (DEPTH, 2, B_CMP_HIDDEN, B_HEAD_DIM), B_CMP_HIDDEN ** -0.5),
        'swa_sinks': nrm(ks[11], (DEPTH, C_HEADS), 0.5),
        'w_branch': nrm(ks[12], (DEPTH, 3, A_WIDTH, D_MODEL), A_WIDTH ** -0.5),
        'w_out': nrm(ks[13], (DEPTH, D_MODEL, D_MODEL), D_MODEL ** -0.5),
        'ffn2_wi': nrm(ks[14], (DEPTH, D_MODEL, 2 * D_FF), D_MODEL ** -0.5),
        'ffn2_wo': nrm(ks[15], (DEPTH, D_FF, D_MODEL), D_FF ** -0.5),
        'w_ple': nrm(ks[16], (DEPTH, PLE_DIM, D_MODEL), PLE_DIM ** -0.5),
        'w_ple_gate': nrm(ks[17], (DEPTH, D_MODEL, D_MODEL), D_MODEL ** -0.5),
        'rel_bias': nrm(ks[18], (NUM_BUCKETS, N_BIAS_HEADS), 0.5),
        'final_norm': 1.0 + nrm(ks[19], (D_MODEL,), 0.05),
    }

def second_block(x, p, norm_g, ffn1_wi, ffn1_wo, w_in, diff_lambda, diff_subln, nsa_cmp_pos,
              nsa_cmp_w1, nsa_cmp_w2, swa_sinks, w_branch, w_out, ffn2_wi, ffn2_wo,
              w_ple, w_ple_gate, rel_bias, final_norm):
    bsz, seq, _ = x.shape
    bias_a = rel_bias[:, :A_HEADS]
    bias_b = rel_bias[:, A_HEADS:A_HEADS + B_HEADS]
    bias_c = rel_bias[:, A_HEADS + B_HEADS:]
    h = x
    for i in range(DEPTH):
        h = h + 0.5 * swiglu(rms_norm(h, norm_g[i, 0]), ffn1_wi[i], ffn1_wo[i])
        n = rms_norm(h, norm_g[i, 1])
        (aq, ak, av, bq, bkc, bvc, bks, bvs, bkw, bvw, bgate,
         cq, ck, cv, ga, gb, gc) = split_cols(n @ w_in[i], IN_SPLITS)
        lam_init = 0.8 - 0.6 * math.exp(-0.3 * i)
        lp = diff_lambda[i].astype(jnp.float32)
        lam = jnp.exp(jnp.sum(lp[0] * lp[1])) - jnp.exp(jnp.sum(lp[2] * lp[3])) + lam_init
        ya = diff_attention(aq.reshape(bsz, seq, A_HEADS, 2, A_HEAD_DIM),
                            ak.reshape(bsz, seq, A_HEADS, 2, A_HEAD_DIM),
                            av.reshape(bsz, seq, A_HEADS, 2 * A_HEAD_DIM),
                            bias_a, lam, lam_init, diff_subln[i])
        kvb = lambda t: t.reshape(bsz, seq, B_GROUPS, B_HEAD_DIM)
        yb = nsa_attention(bq.reshape(bsz, seq, B_GROUPS, B_REP, B_HEAD_DIM),
                           kvb(bkc), kvb(bvc), kvb(bks), kvb(bvs), kvb(bkw), kvb(bvw),
                           jax.nn.sigmoid(bgate.reshape(bsz, seq, B_GROUPS, B_REP, 3)),
                           bias_b, nsa_cmp_pos[i], nsa_cmp_w1[i], nsa_cmp_w2[i])
        yc = swa_sink_attention(cq.reshape(bsz, seq, C_GROUPS, C_REP, C_HEAD_DIM),
                                ck.reshape(bsz, seq, C_GROUPS, C_HEAD_DIM),
                                cv.reshape(bsz, seq, C_GROUPS, C_HEAD_DIM),
                                bias_c, swa_sinks[i])
        merged = (jax.nn.sigmoid(ga) * (ya @ w_branch[i, 0])
                  + jax.nn.sigmoid(gb) * (yb @ w_branch[i, 1])
                  + jax.nn.sigmoid(gc) * (yc @ w_branch[i, 2]))
        h = h + merged @ w_out[i]
        h = h + 0.5 * swiglu(rms_norm(h, norm_g[i, 2]), ffn2_wi[i], ffn2_wo[i])
        h = h + jax.nn.sigmoid(rms_norm(h, norm_g[i, 3]) @ w_ple_gate[i]) * (p[i] @ w_ple[i])
    return rms_norm(h, final_norm)


def setup_inputs(seed=0):
    out = dict(first_inputs(seed))
    for name, value in second_inputs(seed + 1).items():
        if name != "x":
            out[name + "_2"] = value
    return out


def reference(
    x, c, ctx, c_ctx, norm1_g, norm2_g, w_mod, b_mod, even_w_in, mla_q_norm, mla_kv_norm,
    mla_w_uq, mla_w_ukv, conv_w, even_w_out, odd_w_in, mlstm_gate_b, mlstm_head_g, odd_w_out,
    peer_w_q, peer_subkeys, peer_u, peer_v, norm_f_g, p_2, norm_g_2, ffn1_wi_2, ffn1_wo_2,
    w_in_2, diff_lambda_2, diff_subln_2, nsa_cmp_pos_2, nsa_cmp_w1_2, nsa_cmp_w2_2, swa_sinks_2,
    w_branch_2, w_out_2, ffn2_wi_2, ffn2_wo_2, w_ple_2, w_ple_gate_2, rel_bias_2, final_norm_2,
):
    x = first_block(
        x, c, ctx, c_ctx, norm1_g, norm2_g, w_mod, b_mod, even_w_in, mla_q_norm, mla_kv_norm,
        mla_w_uq, mla_w_ukv, conv_w, even_w_out, odd_w_in, mlstm_gate_b, mlstm_head_g,
        odd_w_out, peer_w_q, peer_subkeys, peer_u, peer_v, norm_f_g,
    )
    return second_block(
        x, p_2, norm_g_2, ffn1_wi_2, ffn1_wo_2, w_in_2, diff_lambda_2, diff_subln_2,
        nsa_cmp_pos_2, nsa_cmp_w1_2, nsa_cmp_w2_2, swa_sinks_2, w_branch_2, w_out_2, ffn2_wi_2,
        ffn2_wo_2, w_ple_2, w_ple_gate_2, rel_bias_2, final_norm_2,
    )


_drawn_inputs = setup_inputs


def setup_inputs(seed=0):
    import zlib

    import numpy as np

    out = dict(_drawn_inputs(seed))
    spreads = {}
    factors = {'norm1_g': 2.951,
     'norm2_g': 15.647,
     'mla_q_norm': 8.0,
     'mla_kv_norm': 8.0,
     'mlstm_head_g': 64.0,
     'diff_subln_2': 2.725,
     'nsa_cmp_pos_2': 2.758,
     'swa_sinks_2': 8.0}
    for name, (base, spread) in spreads.items():
        noise = np.random.default_rng([zlib.crc32(name.encode()), seed]).standard_normal(out[name].shape)
        drawn = base * np.exp(spread * noise) if base else spread * noise
        out[name] = jnp.asarray(drawn.astype(out[name].dtype))
    for name, factor in factors.items():
        out[name] = (out[name] * factor).astype(out[name].dtype)
    return out
```

```python
import math
from contextlib import ExitStack, contextmanager

import numpy as np

import concourse.bass as bass
from concourse import mybir

F32 = mybir.dt.float32
U32 = mybir.dt.uint32
ALU = mybir.AluOpType
ACT = mybir.ActivationFunctionType
X_AXIS = mybir.AxisListType.X

P = 128
D = 1024
KD = D // P
T = 256
LAT, CTX = 0, 1
RING = 8
TILE = 1024
EPS = 1e-6
NEG = -1e30

MLA_HEADS, MLA_NOPE, MLA_ROPE, MLA_V = 8, 64, 32, 64
MLA_SCALE = (MLA_NOPE + MLA_ROPE) ** -0.5
ML_HEADS, ML_DV = 4, 256
ML_SCALE = 128 ** -0.5
PH, NKEYS, TOPK = 8, 128, 16
PEER_TILES = 2 * NKEYS
D_FF = 2816
FC = D_FF // P
N_BIAS = 20
N_CMP = 15


def stream_plan():
    def route(layer):
        return [("peer_q%d" % layer, 16, "w"), ("subkeys%d" % layer, 2, "w"), ("experts%d" % layer, PEER_TILES, "peer")]

    plan = [("mod", 96, "w"), ("even_in", 16, "w"), ("uq", 2, "w"), ("ukv", 1, "w"), ("even_out", 8, "w")]
    plan += route(0) + route(0)
    plan += [("odd_qk", 9, "w"), ("odd_v", 8, "w"), ("odd_gate", 8, "w"), ("odd_out", 8, "w")] + route(1)
    for i in range(2):
        plan += [(name + str(i), n, "w") for name, n in (
            ("ffn1_", 3 * FC), ("in_cols", 21), ("in_rows", 8), ("cmp", 9), ("gates", 24), ("branch", 12),
            ("out", 8), ("ffn2_", 3 * FC), ("ple_w", 2), ("ple_gate", 8))]
    return plan


def tile_bases():
    bases, nxt = {}, {"w": 0, "peer": 0}
    for name, n, source in stream_plan():
        if name not in bases:
            bases[name] = nxt[source]
            nxt[source] += n
    return bases, nxt


COLS = [("norm1", 16), ("norm2", 16), ("b_mod", 96), ("q_norm", 2), ("kv_norm", 1), ("conv", 12), ("head_g", 8),
        ("norm_f", 8), ("norms", 64), ("subln", 2), ("final", 8), ("gate_b", 1), ("pos", 64), ("lam", 512),
        ("sinks", 16), ("valid", 1)]


def col_at(name):
    at = 0
    for n, w in COLS:
        if n == name:
            return at
        at += w
    raise KeyError(name)


N_COLS = sum(w for _, w in COLS)
N_CONST = 3 * P + 16


class Weights:

    def __init__(self, nc, w_tiles, peer_tiles):
        self.sources = {"w": w_tiles, "peer": peer_tiles}
        self.ring = nc.alloc_sbuf_tensor("weight_ring", [P, RING, TILE], F32)
        self.arrived = [nc.alloc_semaphore("tile_arrived%d" % i) for i in range(RING)]
        self.used = nc.alloc_semaphore("tiles_used")
        self.plan = stream_plan()
        bases, _ = tile_bases()
        self.tiles = []
        for name, n, source in self.plan:
            self.tiles += [(source, bases[name] + i) for i in range(n)]
        self.at = 0
        self.seg = 0

    def take(self, name):
        got, n, _ = self.plan[self.seg]
        assert got == name, (got, name)
        first = self.at
        self.at += n
        self.seg += 1
        return first

    def slot(self, g):
        return self.ring[:, g % RING, :]

    def wait(self, pe, g):
        pe.wait_ge(self.arrived[g % RING], 16 * (g // RING + 1))

    def load(self, sync, g):
        source, i = self.tiles[g]
        sync.dma_start(self.slot(g), self.sources[source][i * P:(i + 1) * P, :]).then_inc(self.arrived[g % RING], 16)

    def prime(self, sync):
        for g in range(RING):
            self.load(sync, g)

    def feed(self, sync, first, n):
        for g in range(first + RING, min(first + n + RING, len(self.tiles))):
            sync.wait_ge(self.used, g - RING + 1)
            self.load(sync, g)


class Stage:
    def __init__(self, nc, name, ctx):
        self.nc, self.name, self.ctx = nc, name, ctx

    def sem(self, name):
        return self.nc.alloc_semaphore("%s_%s" % (self.name, name))

    def sb(self, name, shape, dt=F32):
        return self.ctx.enter_context(self.nc.sbuf_tensor("%s_%s" % (self.name, name), shape, dt))

    def ps(self, name, shape):
        return self.ctx.enter_context(self.nc.psum_tensor("%s_%s" % (self.name, name), shape, F32))

    def block(self):
        return self.ctx.enter_context(self.nc.Block())


STAGES = [0]


@contextmanager
def stage(nc, name):
    STAGES[0] += 1
    with nc.cleanup_on_exit():
        with ExitStack() as ctx:
            yield Stage(nc, "%s_%d" % (name, STAGES[0]), ctx)


class Chain:

    def __init__(self, eng, sem):
        self.eng, self.sem, self.n = eng, sem, 0

    def __call__(self, ins):
        self.n += 1
        ins.then_inc(self.sem, 1)
        self.eng.wait_ge(self.sem, self.n)


class Job:

    def __init__(self, g, mms, m, last_of_tile):
        self.g, self.mms, self.m, self.last_of_tile = g, mms, m, last_of_tile


def column_jobs(W, first, n_chunks, K, N, x, m=P):
    per = KD // K
    jobs = []
    for c in range(n_chunks):
        g, at = first + c // per, (c % per) * K * P
        tile = W.slot(g)
        mms = [((0, N), tile[:, at + k * P:at + k * P + m], x(k), k == 0, k == K - 1) for k in range(K)]
        jobs.append(Job(g, mms, m, (c + 1) % per == 0 or c == n_chunks - 1))
    return jobs


def products(nc, W, name, first, n_tiles, jobs, evacuate, who, prepare=None, const_load=None, pe_const=False,
             evacuated_out=None, banks=4):
    with stage(nc, name) as S:
        acc = S.ps("acc", [P, banks, 512])
        part_done = S.sem("part_done")
        evacuated = S.sem("evacuated")
        ordered = S.sem("ordered")
        const_in = S.sem("const_in")
        if evacuated_out is not None:
            evacuated_out.append(evacuated)
        ready, parts = [], 0
        for j in jobs:
            if j.last_of_tile:
                ready.append((W.used, j.g + 1))
            else:
                parts += 1
                ready.append((part_done, parts))
        block = S.block()

        @block.sync
        def _(sync):
            if const_load is not None:
                for dst, src in const_load:
                    sync.dma_start(dst, src).then_inc(const_in, 16)
            W.feed(sync, first, n_tiles)

        @block.tensor
        def _(pe):
            if pe_const:
                pe.wait_ge(const_in, 16 * len(const_load))
            for c, j in enumerate(jobs):
                if c >= banks:
                    pe.wait_ge(evacuated, c - banks + 1)
                W.wait(pe, j.g)
                for (lo, hi), lhsT, rhs, start, stop in j.mms:
                    last = pe.matmul(acc[0:j.m, c % banks, lo:hi], lhsT, rhs, start=start, stop=stop)
                last.then_inc(W.used if j.last_of_tile else part_done, 1)

        def read_out(eng):
            chain = Chain(eng, ordered)
            if const_load is not None:
                eng.wait_ge(const_in, 16 * len(const_load))
            if prepare is not None:
                prepare(eng, chain)
            for c in range(len(jobs)):
                eng.wait_ge(*ready[c])
                evacuate(eng, chain, c, acc[:, c % banks, :]).then_inc(evacuated, 1)

        if who == "scalar":
            @block.scalar
            def _(act):
                read_out(act)
        else:
            @block.vector
            def _(dve):
                read_out(dve)


def row_products(nc, W, name, first, halves, x, n_tt, evacuate):
    with stage(nc, name) as S:
        acc = S.ps("acc", [P, halves * n_tt, 512])
        block = S.block()

        @block.sync
        def _(sync):
            W.feed(sync, first, 4 * halves)

        @block.tensor
        def _(pe):
            for half in range(halves):
                for t4 in range(4):
                    g = first + 4 * half + t4
                    W.wait(pe, g)
                    for kk in range(2):
                        k = 2 * t4 + kk
                        for tt in range(n_tt):
                            last = pe.matmul(acc[:, half * n_tt + tt, :], x(k, tt),
                                             W.slot(g)[:, kk * 512:(kk + 1) * 512],
                                             start=(k == 0), stop=(k == KD - 1))
                    last.then_inc(W.used, 1)

        @block.scalar
        def _(act):
            for half in range(halves):
                act.wait_ge(W.used, first + 4 * half + 4)
                for tt in range(n_tt):
                    evacuate(act, half, tt, acc[:, half * n_tt + tt, :])


def norm(nc, name, src, dst, K, N, ones, scale, groups=1, post=1.0, shift=None, mul=None, ranges=None):
    ranges = ranges or [(0, N, 0)]
    n_chunks = K * groups
    with stage(nc, name) as S:
        sq = S.sb("sq", [P, n_chunks, N])
        root = S.sb("root", [P, groups, N])
        rstd = S.sb("rstd", [P, groups, N])
        total = S.ps("total", [P, groups, N])
        squared, summed, meaned, rooted, ordered, scaled = (
            S.sem(n) for n in ("squared", "summed", "meaned", "rooted", "ordered", "scaled"))
        block = S.block()

        @block.scalar
        def _(act):
            for c in range(n_chunks):
                act.activation(sq[:, c, :], src(c), ACT.Square).then_inc(squared, 1)
            act.wait_ge(meaned, 1)
            act.activation(root[:, :, :], root[:, :, :], ACT.Sqrt).then_inc(rooted, 1)
            if shift is not None:
                for c in range(n_chunks):
                    act.wait_ge(scaled, c + 1)
                    for lo, hi, s in ranges:
                        act.activation(dst(c)[:, lo:hi], dst(c)[:, lo:hi], ACT.Identity, bias=shift(c, s))

        @block.tensor
        def _(pe):
            for c in range(n_chunks):
                pe.wait_ge(squared, c + 1)
                last = pe.matmul(total[:, c // K, :], ones, sq[:, c, :], start=(c % K == 0), stop=(c % K == K - 1))
            last.then_inc(summed, 1)

        @block.vector
        def _(dve):
            chain = Chain(dve, ordered)
            dve.wait_ge(summed, 1)
            dve.tensor_scalar(root[:, :, :], total[:, :, :], 1.0 / (K * P * post * post), EPS / (post * post),
                              ALU.mult, ALU.add).then_inc(meaned, 1)
            dve.wait_ge(rooted, 1)
            chain(dve.reciprocal(rstd[:, :, :], root[:, :, :]))
            for c in range(n_chunks):
                for lo, hi, s in ranges:
                    last = dve.scalar_tensor_tensor(out=dst(c)[:, lo:hi], in0=src(c)[:, lo:hi], scalar=scale(c, s),
                                                    in1=rstd[:, c // K, lo:hi], op0=ALU.mult, op1=ALU.mult)
                last.then_inc(scaled, 1)
                if mul is not None:
                    dve.wait_ge(scaled, c + 1)
                    dve.tensor_tensor(dst(c), dst(c), mul(c), ALU.mult)


class Unit:

    def __init__(self, q, k, v, nk, scale, bias=None, sink=None, weight=None, end=True, first=True, out=None):
        self.q, self.k, self.v, self.nk, self.scale = q, k, v, nk, scale
        self.bias, self.sink, self.weight = bias, sink, weight
        self.first, self.end, self.out = first, end, out


def attention(nc, name, units, ident):
    U = len(units)
    width = max(u.nk for u in units)
    group, groups = [], 0
    for u in units:
        group.append(groups)
        groups += u.end
    with stage(nc, name) as S:
        raw = S.ps("raw", [P, 3, 512])
        turned = S.ps("turned", [P, 2, 512])
        out = S.ps("out", [P, 2, 512])
        biased = S.sb("biased", [P, 3, width])
        prob = S.sb("prob", [P, 3, width])
        probT = S.sb("probT", [P, 2, width])
        low = S.sb("low", [P, 3, 4])
        scored, shifted, exped, normed, transposed, copied, summed, evacuated, v_ordered, a_ordered = (
            S.sem(n) for n in ("scored", "shifted", "exped", "normed", "transposed", "copied", "summed",
                               "evacuated", "v_ordered", "a_ordered"))
        block = S.block()

        @block.tensor
        def _(pe):
            for u in range(U + 2):
                if u < U:
                    x = units[u]
                    if u >= 3:
                        pe.wait_ge(exped, u - 2)
                    pe.matmul(raw[:, u % 3, 0:x.nk], x.q, x.k, start=True, stop=True).then_inc(scored, 1)
                if 1 <= u <= U:
                    w, x = u - 1, units[u - 1]
                    pe.wait_ge(normed, w + 1)
                    if w >= 2:
                        pe.wait_ge(copied, w - 1)
                    for b in range(x.nk // P):
                        last = pe.transpose(turned[:, w % 2, b * P:(b + 1) * P], prob[:, w % 3, b * P:(b + 1) * P], ident)
                    last.then_inc(transposed, 1)
                if u >= 2:
                    w, x = u - 2, units[u - 2]
                    pe.wait_ge(copied, w + 1)
                    if x.first and group[w] >= 2:
                        pe.wait_ge(evacuated, group[w] - 1)
                    nb = x.nk // P
                    for b in range(nb):
                        last = pe.matmul(out[:, group[w] % 2, 0:P], x.v(b), probT[:, w % 2, b * P:(b + 1) * P],
                                         start=(x.first and b == 0), stop=(x.end and b == nb - 1))
                    last.then_inc(summed, 1)

        @block.vector
        def _(dve):
            chain = Chain(dve, v_ordered)
            for u in range(U + 1):
                if u < U:
                    x, i = units[u], u % 3
                    dve.wait_ge(scored, u + 1)
                    if u >= 3:
                        dve.wait_ge(exped, u - 2)
                    src = raw[:, i, 0:x.nk]
                    if x.bias is not None:
                        chain(dve.scalar_tensor_tensor(out=biased[:, i, 0:x.nk], in0=src, scalar=x.scale,
                                                       in1=x.bias, op0=ALU.mult, op1=ALU.add))
                        src = biased[:, i, 0:x.nk]
                    chain(dve.tensor_reduce(low[:, i, 0:1], src, X_AXIS, ALU.max))
                    factor = -1.0 if x.bias is not None else -x.scale
                    if x.sink is None:
                        dve.tensor_scalar(low[:, i, 0:1], low[:, i, 0:1], factor, None, ALU.mult).then_inc(shifted, 1)
                    else:
                        chain(dve.tensor_scalar(low[:, i, 0:1], low[:, i, 0:1], x.sink, factor, ALU.max, ALU.mult))
                        dve.tensor_tensor(low[:, i, 3:4], x.sink, low[:, i, 0:1], ALU.add).then_inc(shifted, 1)
                if u >= 1:
                    w, x, i = u - 1, units[u - 1], (u - 1) % 3
                    dve.wait_ge(exped, w + 1)
                    if x.sink is not None:
                        chain(dve.tensor_tensor(low[:, i, 1:2], low[:, i, 1:2], low[:, i, 3:4], ALU.add))
                    chain(dve.reciprocal(low[:, i, 2:3], low[:, i, 1:2]))
                    if x.weight is None:
                        ins = dve.tensor_scalar(prob[:, i, 0:x.nk], prob[:, i, 0:x.nk], low[:, i, 2:3], None, ALU.mult)
                    else:
                        ins = dve.tensor_scalar(prob[:, i, 0:x.nk], prob[:, i, 0:x.nk], low[:, i, 2:3], x.weight,
                                                ALU.mult, ALU.mult)
                    ins.then_inc(normed, 1)

        @block.scalar
        def _(act):
            chain = Chain(act, a_ordered)
            for u in range(U + 2):
                if u < U:
                    x, i = units[u], u % 3
                    act.wait_ge(shifted, u + 1)
                    if u >= 3:
                        act.wait_ge(transposed, u - 2)
                    src, scale = (raw[:, i, 0:x.nk], x.scale) if x.bias is None else (biased[:, i, 0:x.nk], 1.0)
                    if x.sink is not None:
                        chain(act.activation(low[:, i, 3:4], low[:, i, 3:4], ACT.Exp))
                    act.activation(prob[:, i, 0:x.nk], src, ACT.Exp, bias=low[:, i, 0:1], scale=scale,
                                   accum_out=low[:, i, 1:2]).then_inc(exped, 1)
                if 1 <= u <= U:
                    w, x = u - 1, units[u - 1]
                    act.wait_ge(transposed, w + 1)
                    if w >= 2:
                        act.wait_ge(summed, w - 1)
                    act.activation(probT[:, w % 2, 0:x.nk], turned[:, w % 2, 0:x.nk], ACT.Copy).then_inc(copied, 1)
                if u >= 2 and units[u - 2].end:
                    w = u - 2
                    act.wait_ge(summed, w + 1)
                    lo, hi, dst = units[w].out
                    act.activation(dst, out[lo:hi, group[w] % 2, 0:P], ACT.Copy).then_inc(evacuated, 1)


def feed_forward(nc, W, seg, x, h):
    first = W.take(seg)
    order = [("gate", 0), ("up", 0)]
    for c in range(FC):
        if c + 1 < FC:
            order += [("gate", c + 1), ("up", c + 1)]
        order.append(("down", c))
    number = {key: first + i for i, key in enumerate(order)}
    with stage(nc, seg) as S:
        acc = S.ps("acc", [P, KD, T])
        gu = S.ps("gu", [P, 2, 2, 512])
        silu = S.sb("silu", [P, 2, T])
        hid = S.sb("hid", [P, 2, T])
        silu_done, hidden = S.sem("silu_done"), S.sem("hidden")
        block = S.block()

        @block.sync
        def _(sync):
            W.feed(sync, first, 3 * FC)

        @block.tensor
        def _(pe):
            for kind, c in order:
                g = number[kind, c]
                W.wait(pe, g)
                tile = W.slot(g)
                if kind == "down":
                    pe.wait_ge(hidden, c + 1)
                    for n in range(KD):
                        last = pe.matmul(acc[:, n, :], tile[:, n * P:(n + 1) * P], hid[:, c % 2, :],
                                         start=(c == 0 and n % 2 == 0), stop=(c == FC - 1), skip_group_check=True)
                else:
                    j = ("gate", "up").index(kind)
                    if c >= 2 and j == 0:
                        pe.wait_ge(hidden, c - 1)
                    for k in range(KD):
                        last = pe.matmul(gu[:, c % 2, j, 0:T], tile[:, k * P:(k + 1) * P], x[:, k, :],
                                         start=(k == 0), stop=(k == KD - 1))
                last.then_inc(W.used, 1)

        @block.scalar
        def _(act):
            for c in range(FC):
                act.wait_ge(W.used, number["gate", c] + 1)
                if c >= 2:
                    act.wait_ge(hidden, c - 1)
                act.activation(silu[:, c % 2, :], gu[:, c % 2, 0, 0:T], ACT.Silu).then_inc(silu_done, 1)

        @block.vector
        def _(dve):
            for c in range(FC):
                dve.wait_ge(W.used, number["up", c] + 1)
                dve.wait_ge(silu_done, c + 1)
                if c >= 2:
                    dve.wait_ge(W.used, number["down", c - 2] + 1)
                dve.tensor_tensor(hid[:, c % 2, :], silu[:, c % 2, :], gu[:, c % 2, 1, 0:T], ALU.mult).then_inc(hidden, 1)
            dve.wait_ge(W.used, first + 3 * FC)
            for n in range(KD):
                dve.scalar_tensor_tensor(out=h[:, n, 0:T], in0=acc[:, n, :], scalar=0.5, in1=h[:, n, 0:T],
                                         op0=ALU.mult, op1=ALU.add)


def peer_topk(nc, name, scores, route, const):
    ident, iota16 = const[:, 0:P], const[:, 3 * P:3 * P + 16]
    HC = PH * TOPK
    with stage(nc, name) as S:
        rest = S.sb("rest", [P, 2 * PH, NKEYS])
        best = S.sb("best", [P, 2 * PH, TOPK])
        index = S.sb("index", [P, 2 * PH, TOPK], U32)
        indexf = S.sb("indexf", [P, 2 * PH, TOPK])
        cand = S.sb("cand", [P, PH, TOPK * TOPK])
        cand2 = S.sb("cand2", [P, PH, TOPK * TOPK])
        top = S.sb("top", [P, PH, TOPK])
        where = S.sb("where", [P, PH, TOPK], U32)
        part = S.sb("part", [P, 2, HC], U32)
        partf = S.sb("partf", [P, 2, HC])
        hit = S.sb("hit", [P, HC, TOPK])
        total = S.sb("total", [P, PH])
        chosen = S.sb("chosen", [P, 2, 3, HC])
        turned = S.ps("turned", [P, 2, 512])
        ordered, exp_in, exped, ready, transposed = (
            S.sem(n) for n in ("ordered", "exp_in", "exped", "ready", "transposed"))
        block = S.block()

        @block.vector
        def _(dve):
            chain = Chain(dve, ordered)
            for tt in range(2):
                for i in range(2 * PH):
                    last = dve.max(best[:, i, 0:8], scores[:, tt, i, :])
                chain(last)
                for i in range(2 * PH):
                    dve.match_replace(out=rest[:, i, :], in_to_replace=best[:, i, 0:8], in_values=scores[:, tt, i, :],
                                      imm_value=-3e38)
                    last = dve.max_index(index[:, i, 0:8], best[:, i, 0:8], scores[:, tt, i, :])
                chain(last)
                for i in range(2 * PH):
                    last = dve.max(best[:, i, 8:16], rest[:, i, :])
                chain(last)
                for i in range(2 * PH):
                    last = dve.max_index(index[:, i, 8:16], best[:, i, 8:16], rest[:, i, :])
                chain(last)
                dve.tensor_copy(indexf[:, :, :], index[:, :, :])
                halves = best[:, :, :].rearrange("p (h two) a -> p h two a", two=2)
                chain(dve.tensor_tensor(
                    cand[:, :, :].rearrange("p h (a b) -> p h a b", a=TOPK),
                    halves[:, :, 0, :].unsqueeze(3).to_broadcast([P, PH, TOPK, TOPK]),
                    halves[:, :, 1, :].unsqueeze(2).to_broadcast([P, PH, TOPK, TOPK]), ALU.add))
                for h in range(PH):
                    last = dve.max(top[:, h, 0:8], cand[:, h, :])
                chain(last)
                for h in range(PH):
                    dve.match_replace(out=cand2[:, h, :], in_to_replace=top[:, h, 0:8], in_values=cand[:, h, :],
                                      imm_value=-3e38)
                    last = dve.max_index(where[:, h, 0:8], top[:, h, 0:8], cand[:, h, :])
                chain(last)
                for h in range(PH):
                    last = dve.max(top[:, h, 8:16], cand2[:, h, :])
                chain(last)
                for h in range(PH):
                    last = dve.max_index(where[:, h, 8:16], top[:, h, 8:16], cand2[:, h, :])
                chain(last)
                g = chosen[:, tt, 2, :].rearrange("p (h s) -> p h s", h=PH)
                dve.tensor_tensor(g, top[:, :, :], top[:, :, 0:1].to_broadcast([P, PH, TOPK]),
                                  ALU.subtract).then_inc(exp_in, 1)
                flat = where[:, :, :].rearrange("p h s -> p (h s)")
                dve.tensor_scalar(part[:, 0, :], flat, 4, None, ALU.logical_shift_right)
                chain(dve.tensor_scalar(part[:, 1, :], flat, 15, None, ALU.bitwise_and))
                chain(dve.tensor_copy(partf[:, :, :], part[:, :, :]))
                both = indexf[:, :, :].rearrange("p (h two) a -> p h two a", two=2)
                for half in range(2):
                    chain(dve.tensor_tensor(hit[:, :, :], partf[:, half, :].unsqueeze(2).to_broadcast([P, HC, TOPK]),
                                            iota16.unsqueeze(1).to_broadcast([P, HC, TOPK]), ALU.is_equal))
                    hits = hit[:, :, :].rearrange("p (h s) a -> p h s a", h=PH)
                    chain(dve.tensor_tensor(hits, hits, both[:, :, half, :].unsqueeze(2).to_broadcast([P, PH, TOPK, TOPK]),
                                            ALU.mult))
                    chain(dve.tensor_reduce(chosen[:, tt, half, :], hit[:, :, :], X_AXIS, ALU.add))
                dve.wait_ge(exped, tt + 1)
                chain(dve.tensor_reduce(total[:, :], g, X_AXIS, ALU.add))
                chain(dve.reciprocal(total[:, :], total[:, :]))
                dve.tensor_tensor(g, g, total[:, :].unsqueeze(2).to_broadcast([P, PH, TOPK]), ALU.mult).then_inc(ready, 1)
                dve.wait_ge(ready, tt + 1)

        @block.scalar
        def _(act):
            for tt in range(2):
                act.wait_ge(exp_in, tt + 1)
                act.activation(chosen[:, tt, 2, :], chosen[:, tt, 2, :], ACT.Exp).then_inc(exped, 1)
            for tt in range(2):
                act.wait_ge(transposed, tt + 1)
                for j in range(3):
                    act.activation(route[:, j, tt * P:(tt + 1) * P], turned[:, tt, j * P:(j + 1) * P], ACT.Copy)

        @block.tensor
        def _(pe):
            for tt in range(2):
                pe.wait_ge(ready, tt + 1)
                for j in range(3):
                    last = pe.transpose(turned[:, tt, j * P:(j + 1) * P], chosen[:, tt, j, :], ident)
                last.then_inc(transposed, 1)


GROUP = 4


def peer_spread(nc, name, route, G, const):
    iota = const[:, 2 * P:3 * P]
    steps = T // GROUP
    with stage(nc, name) as S:
        cur = S.sb("cur", [P, 2, 3, GROUP])
        first = S.sb("first", [P, 2, GROUP, P])
        second = S.sb("second", [P, 2, GROUP, P])
        product = S.ps("product", [P, 2, GROUP, P])
        picked, onehots, multiplied, stored = (S.sem(n) for n in ("picked", "onehots", "multiplied", "stored"))
        block = S.block()

        @block.scalar
        def _(act):
            for b in range(2):
                act.activation(cur[:, b, :, :], route[:, :, b * GROUP:(b + 1) * GROUP], ACT.Copy).then_inc(picked, 1)

            def store(at, b, done):
                act.wait_ge(multiplied, done)
                act.activation(G[:, :, bass.ds(at, GROUP)], product[:, b, :, :].rearrange("p t j -> p j t"),
                               ACT.Copy).then_inc(stored, 1)

            with act.Fori(0, steps // 2 - 1) as i:
                for b in range(2):
                    store(i * (2 * GROUP) + b * GROUP, b, i * 2 + (b + 1))
                    act.activation(cur[:, b, :, :], route[:, :, bass.ds(i * (2 * GROUP) + (b + 2) * GROUP, GROUP)],
                                   ACT.Copy).then_inc(picked, 1)
            for b in range(2):
                store(T + (b - 2) * GROUP, b, steps - 1 + b)

        @block.vector
        def _(dve):
            with dve.Fori(0, steps // 2) as i:
                for b in range(2):
                    dve.wait_ge(picked, i * 2 + (b + 1))
                    for t in range(GROUP):
                        dve.tensor_scalar(first[:, b, t, :], iota, cur[:, b, 0, t:t + 1], None, ALU.is_equal)
                        last = dve.tensor_scalar(second[:, b, t, :], iota, cur[:, b, 1, t:t + 1], cur[:, b, 2, t:t + 1],
                                                 ALU.is_equal, ALU.mult)
                    last.then_inc(onehots, 1)

        @block.tensor
        def _(pe):
            with pe.Fori(0, steps // 2) as i:
                for b in range(2):
                    pe.wait_ge(onehots, i * 2 + (b + 1))
                    for t in range(GROUP):
                        last = pe.matmul(product[:, b, t, :], first[:, b, t, :], second[:, b, t, :], start=True, stop=True)
                    last.then_inc(multiplied, 1)


def peer_experts(nc, W, seg, x, G, h, gate):
    first = W.take(seg)
    at0 = first % RING
    per = RING // 2
    turns = (NKEYS - 1) // per
    with stage(nc, seg) as S:
        acc = S.ps("acc", [P, KD, T])
        dot = S.ps("dot", [P, 2, 512])
        act_out = S.sb("act_out", [P, 2, T])
        coef = S.sb("coef", [P, 2, T])
        zero = S.sb("zero", [P, 512])
        zeroed, dotted, gelued, weighted, finished = (
            S.sem(n) for n in ("zeroed", "dotted", "gelued", "weighted", "finished"))
        block = S.block()

        def slot(pos):
            return W.ring[:, (at0 + pos) % RING, :]

        def arrived_at(pos, i):
            return 16 * ((first + pos) // RING + 1) + i * 16

        @block.sync
        def _(sync):
            base = tile_bases()[0][seg] * P
            with sync.Fori(0, PEER_TILES // RING - 1) as i:
                for s in range(RING):
                    sync.wait_ge(W.used, i * RING + (first + s + 1))
                    sync.dma_start(slot(s), W.sources["peer"][bass.ds(i * (RING * P) + (base + (RING + s) * P), P), :]
                                   ).then_inc(W.arrived[(at0 + s) % RING], 16)
            W.feed(sync, first + PEER_TILES - RING, RING)

        @block.gpsimd
        def _(pool):
            pool.memset(zero[:, :], 0.0).then_inc(zeroed, 1)

        @block.tensor
        def _(pe):
            def dots(pos, i, j):
                pe.wait_ge(W.arrived[(at0 + pos) % RING], arrived_at(pos, i))
                for k in range(KD):
                    last = pe.matmul(dot[:, j % 2, 0:T], slot(pos)[:, k * P:(k + 1) * P], x[:, k, :],
                                     start=(k == 0), stop=(k == KD - 1))
                last.then_inc(W.used, 1)

            def sums(pos, i, j, count):
                pe.wait_ge(W.arrived[(at0 + pos) % RING], arrived_at(pos, i))
                pe.wait_ge(weighted, count)
                for n in range(KD):
                    last = pe.matmul(acc[:, n, :], slot(pos)[:, n * P:(n + 1) * P], coef[:, j % 2, :],
                                     start=False, stop=False, skip_group_check=True)
                last.then_inc(W.used, 1)

            pe.wait_ge(zeroed, 1)
            for b in range(KD // 2):
                pe.matmul(acc[:, 2 * b:2 * b + 2, :].rearrange("p a t -> p (a t)"), zero[:, 0:P], zero[:, :], start=True, stop=False,
                          skip_group_check=True)
            dots(0, 0, 0)
            with pe.Fori(0, turns) as i:
                for q in range(per):
                    dots(2 * q + 1, i, q + 1)
                    sums(2 * q + 2, i, q, i * per + (q + 1))
            for j in range(turns * per, NKEYS):
                if j + 1 < NKEYS:
                    dots(2 * j + 1, 0, j + 1)
                    sums(2 * j + 2, 0, j, j + 1)
                else:
                    sums(2 * j + 1, 0, j, j + 1)
            for b in range(KD // 2):
                last = pe.matmul(acc[:, 2 * b:2 * b + 2, :].rearrange("p a t -> p (a t)"), zero[:, 0:P], zero[:, :], start=False, stop=True,
                                 skip_group_check=True)
            last.then_inc(finished, 1)

        @block.scalar
        def _(act):
            def gelu(b, done):
                act.wait_ge(W.used, done)
                act.activation(act_out[:, b, :], dot[:, b, 0:T], ACT.Gelu).then_inc(gelued, 1)

            gelu(0, first + 1)
            with act.Fori(0, NKEYS // 2 - 1) as i:
                for b in range(2):
                    gelu(1 - b, i * 4 + (first + 2 * b + 2))
            gelu(1, first + 2 * (NKEYS - 2) + 2)

        @block.vector
        def _(dve):
            with dve.Fori(0, NKEYS // 2) as i:
                for b in range(2):
                    dve.wait_ge(gelued, i * 2 + (b + 1))
                    dve.tensor_tensor(coef[:, b, :], act_out[:, b, :],
                                      G[:, bass.ds(i * 2 + b, 1), :].rearrange("p o t -> p (o t)"),
                                      ALU.mult).then_inc(weighted, 1)
            dve.wait_ge(finished, 1)
            for n in range(KD):
                dve.scalar_tensor_tensor(out=h[:, n, :], in0=acc[:, n, :], scalar=gate(n), in1=h[:, n, :],
                                         op0=ALU.mult, op1=ALU.add)


def peer(nc, W, layer, stream, h, scale, shift, gate, const):
    name = "peer%d%d" % (layer, stream)
    with nc.sbuf_tensor(name + "_x", [P, KD, T], F32) as x, nc.sbuf_tensor(name + "_route", [P, 3, T], F32) as route:
        norm(nc, name + "n", lambda c: h[:, c, :], lambda c: x[:, c, :], KD, T, const[:, P:2 * P],
             lambda c, s: scale(c), shift=lambda c, s: shift(c))
        with nc.sbuf_tensor(name + "_q", [P, 2 * PH, T], F32) as q, \
                nc.sbuf_tensor(name + "_s", [P, 2, 2 * PH, NKEYS], F32) as scores:
            first = W.take("peer_q%d" % layer)
            products(nc, W, name + "q", first, 16, column_jobs(W, first, 16, KD, T, lambda k: x[:, k, :]),
                     lambda eng, chain, c, ps: eng.activation(q[:, c, :], ps[:, 0:T], ACT.Copy), "scalar")
            first = W.take("subkeys%d" % layer)
            jobs, place = [], []
            for t in range(2):
                for tt in range(2):
                    for quad in range(2):
                        mms = []
                        for j in range(4):
                            i = 4 * quad + j
                            mms.append(((j * NKEYS, (j + 1) * NKEYS), q[:, 8 * t + i, tt * P:(tt + 1) * P],
                                        W.slot(first + t)[:, i * P:(i + 1) * P], True, True))
                        jobs.append(Job(first + t, mms, P, tt == 1 and quad == 1))
                        place.append((tt, 8 * t + 4 * quad))
            products(nc, W, name + "s", first, 2, jobs,
                     lambda eng, chain, c, ps: eng.activation(
                         scores[:, place[c][0], place[c][1]:place[c][1] + 4, :].rearrange("p a k -> p (a k)"),
                         ps[:, :], ACT.Copy), "scalar")
            peer_topk(nc, name + "t", scores, route, const)
        with nc.sbuf_tensor(name + "_G", [P, NKEYS, T], F32) as G:
            peer_spread(nc, name + "g", route, G, const)
            peer_experts(nc, W, "experts%d" % layer, x, G, h, gate)


def even_mixer(nc, W, h, modulation, scales, cols, const, rope_dram):
    TT = 2 * T
    ones, ident = const[:, P:2 * P], const[:, 0:P]
    streams = [(0, T, LAT), (T, TT, CTX)]
    with ExitStack() as ctx:
        def sb(name, shape):
            return ctx.enter_context(nc.sbuf_tensor("even_" + name, shape, F32))

        mix = sb("mix", [P, KD, TT])
        with ExitStack() as inner:
            def tmp_sb(name, shape):
                return inner.enter_context(nc.sbuf_tensor("even_" + name, shape, F32))

            pq = tmp_sb("pq", [P, 2, TT])
            pkv = tmp_sb("pkv", [P, TT])
            kr = tmp_sb("kr", [P, TT])
            rope = tmp_sb("rope", [P, TT])
            with nc.sbuf_tensor("even_x", [P, KD, TT], F32) as x:
                norm(nc, "even_n", lambda c: h[:, c, :], lambda c: x[:, c, :], KD, TT, ones,
                     lambda c, s: scales[:, 0, 0, s, c:c + 1], ranges=streams,
                     shift=lambda c, s: modulation[:, 0, c, s:s + 1])
                first = W.take("even_in")
                with nc.sbuf_tensor("even_c", [P, TT], F32) as c_gate, nc.sbuf_tensor("even_z", [P, 2, T + 2], F32) as z, \
                        nc.sbuf_tensor("even_y", [P, 2, T], F32) as y, nc.sbuf_tensor("even_t", [P, TT], F32) as turn:
                    def prepare(dve, chain):
                        chain(dve.memset(z[:, :, :], 0.0))

                    def evacuate(dve, chain, c, ps):
                        if c < 2:
                            return dve.tensor_copy(pq[:, c, :], ps)
                        if c == 2:
                            return dve.tensor_copy(pkv[:, :], ps)
                        if c == 3:
                            chain(dve.tensor_tensor(turn[64:96, :], ps[96:128, :], rope[96:128, :], ALU.mult))
                            chain(dve.tensor_tensor(kr[64:96, :], ps[64:96, :], rope[64:96, :], ALU.mult))
                            return dve.tensor_tensor(kr[64:96, :], kr[64:96, :], turn[64:96, :], ALU.add)
                        j, kind = (c - 4) // 3, (c - 4) % 3
                        two = ps.rearrange("p (s t) -> p s t", s=2)
                        if kind == 0:
                            return dve.tensor_copy(c_gate[:, :], ps)
                        if kind == 1:
                            dve.wait_ge(*done_before(c))
                            return dve.tensor_tensor(z[:, :, 1:T + 1], two,
                                                     c_gate[:, :].rearrange("p (s t) -> p s t", s=2), ALU.mult)

                        def tap(i):
                            at = col_at("conv") + 4 * i + j
                            return cols[:, at:at + 1]

                        dve.wait_ge(*done_before(c))
                        chain(dve.tensor_scalar(y[:, :, :], z[:, :, 0:T], tap(0), None, ALU.mult))
                        for i in (1, 2):
                            chain(dve.scalar_tensor_tensor(out=y[:, :, :], in0=z[:, :, i:T + i], scalar=tap(i),
                                                           in1=y[:, :, :], op0=ALU.mult, op1=ALU.add))
                        return dve.tensor_tensor(mix[:, 4 + j, :].rearrange("p (s t) -> p s t", s=2), two, y[:, :, :],
                                                 ALU.mult)

                    done = []

                    def done_before(c):
                        return done[0], c

                    products(nc, W, "even_in", first, 16, column_jobs(W, first, 16, KD, TT, lambda k: x[:, k, :]),
                             evacuate, "vector", prepare=prepare, const_load=[(rope[:, :], rope_dram)],
                             evacuated_out=done)

            q = tmp_sb("q", [P, MLA_HEADS, TT])
            k = tmp_sb("k", [P, MLA_HEADS, TT])
            v = tmp_sb("v", [P, 4, 512])
            at = col_at("q_norm")
            norm(nc, "even_qn", lambda c: pq[:, c, :], lambda c: pq[:, c, :], 2, TT, ones,
                 lambda c, s: cols[:, at + c:at + c + 1])
            at_kv = col_at("kv_norm")
            norm(nc, "even_kvn", lambda c: pkv[:, :], lambda c: pkv[:, :], 1, TT, ones,
                 lambda c, s: cols[:, at_kv:at_kv + 1])
            first = W.take("uq")
            with nc.sbuf_tensor("even_t2", [P, 2, TT], F32) as turn:
                def rotate(dve, chain, c, ps):
                    chain(dve.tensor_tensor(turn[64:96, c % 2, :], ps[96:128, :], rope[96:128, :], ALU.mult))
                    chain(dve.tensor_tensor(q[64:96, c, :], ps[64:96, :], rope[64:96, :], ALU.mult))
                    dve.tensor_copy(q[0:64, c, :], ps[0:64, :])
                    return dve.tensor_tensor(q[64:96, c, :], q[64:96, c, :], turn[64:96, c % 2, :], ALU.add)

                products(nc, W, "even_uq", first, 2, column_jobs(W, first, MLA_HEADS, 2, TT, lambda kk: pq[:, kk, :]),
                         rotate, "vector")
            first = W.take("ukv")
            jobs = []
            for head in range(MLA_HEADS):
                w = W.slot(first)[:, head * MLA_NOPE:(head + 1) * MLA_NOPE]
                jobs.append(Job(first, [((0, TT), w, pkv[:, :], True, True)], MLA_NOPE, False))
            for tt in range(4):
                jobs.append(Job(first, [((0, 512), pkv[:, tt * P:(tt + 1) * P], W.slot(first)[:, 512:1024], True, True)],
                                P, tt == 3))

            def keys_values(dve, chain, c, ps):
                if c < MLA_HEADS:
                    dve.tensor_copy(k[64:96, c, :], kr[64:96, :])
                    return dve.tensor_copy(k[0:64, c, :], ps[0:64, :])
                return dve.tensor_copy(v[:, c - MLA_HEADS, :], ps)

            products(nc, W, "even_ukv", first, 1, jobs, keys_values, "vector")
            units = []
            for head in range(MLA_HEADS):
                for tt in range(4):
                    lo = 0 if tt < 2 else 2
                    units.append(Unit(
                        q[0:96, head, tt * P:(tt + 1) * P], k[0:96, head, lo * P:TT],
                        lambda b, head=head, lo=lo: v[:, lo + b, (head // 2) * P:(head // 2 + 1) * P],
                        (4 - lo) * P, MLA_SCALE,
                        out=(64 * (head % 2), 64 * (head % 2) + 64,
                             mix[64 * (head % 2):64 * (head % 2) + 64, head // 2, tt * P:(tt + 1) * P])))
            attention(nc, "mla", units, ident)
        first = W.take("even_out")

        def residual(dve, chain, c, ps):
            for lo, hi, s in streams:
                last = dve.scalar_tensor_tensor(out=h[:, c, lo:hi], in0=ps[:, lo:hi], scalar=modulation[:, 0, 16 + c, s:s + 1],
                                                in1=h[:, c, lo:hi], op0=ALU.mult, op1=ALU.add)
            return last

        products(nc, W, "even_out", first, 8, column_jobs(W, first, 8, KD, TT, lambda kk: mix[:, kk, :]),
                 residual, "vector")


def mlstm(nc, name, gx, q, k, v, out, const, sel_dram, mask_dram):
    TT = 2 * T
    ident = const[:, 0:P]
    with stage(nc, name) as S:
        F = S.sb("F", [P, TT])
        r = S.sb("r", [P, TT])
        M = S.sb("M", [P, TT])
        neg_m = S.sb("neg_m", [P, TT])
        sel = S.sb("sel", [P, ML_HEADS, P])
        mask = S.sb("mask", [P, 2, 2, T])
        colM = S.sb("colM", [P, 2, P])
        guard = S.sb("guard", [P, 2, P])
        s_sb = S.sb("scores", [P, TT])
        w = S.sb("w", [P, 2, TT])
        sc = S.sb("sc", [P, 2, TT])
        den = S.sb("den", [P, 2, 2])
        scT = S.sb("scT", [P, 4, P])
        raw = S.ps("raw", [P, TT])
        row = S.ps("row", [P, 2, TT])
        turned = S.ps("turned", [P, 2, 512])
        o = S.ps("o", [P, 2, 512])
        (loaded, rows_ready, cols_done, guarded, scored, scores_out, row_done, shifted, exped, masked, combined,
         transposed, copied, summed, evacuated, ordered, cols_out) = (
            S.sem(n) for n in ("loaded", "rows_ready", "cols_done", "guarded", "scored", "scores_out", "row_done",
                               "shifted", "exped", "masked", "combined", "transposed", "copied", "summed",
                               "evacuated", "ordered", "cols_out"))
        steps = [(head, tt) for head in range(ML_HEADS) for tt in range(2)]
        lanes = (slice(32, 36), slice(96, 100))
        block = S.block()

        @block.sync
        def _(sync):
            sync.dma_start(sel[:, :, :].rearrange("p h m -> p (h m)"), sel_dram).then_inc(loaded, 16)
            sync.dma_start(mask[:, :, :, :].rearrange("p a b t -> p (a b t)"), mask_dram).then_inc(loaded, 16)

        @block.gpsimd
        def _(pool):
            pool.wait_ge(loaded, 32)
            for n, (head, tt) in enumerate(steps):
                for d in range(2):
                    pool.wait_ge(exped, 2 * n + d + 1)
                    pool.tensor_tensor(w[:, d, 0:T], w[:, d, 0:T], mask[:, d, tt, :], ALU.mult).then_inc(masked, 1)

        @block.vector
        def _(dve):
            chain = Chain(dve, ordered)
            for buf in (F, r, M):
                last = dve.memset(buf[:, :], 0.0)
            chain(last)
            for d, lane in enumerate(lanes):
                src = slice(64 * d, 64 * d + 4)
                dve.tensor_copy(r[lane, :], gx[src, :])
                if d == 0:
                    one, two = slice(T, TT), slice(0, T)
                    ends = (TT - 1, T - 1)
                else:
                    one, two = slice(TT - 1, T - 1, -1), slice(T - 1, None, -1)
                    ends = (T, 0)
                chain(dve.tensor_tensor_scan(F[lane, one], gx[lane, one], gx[lane, one], 0.0, ALU.add, ALU.bypass))
                chain(dve.tensor_tensor_scan(F[lane, two], gx[lane, two], gx[lane, two],
                                             F[lane, ends[0]:ends[0] + 1], ALU.add, ALU.bypass))
                chain(dve.tensor_tensor(r[lane, :], r[lane, :], F[lane, :], ALU.subtract))
                chain(dve.tensor_tensor_scan(M[lane, one], r[lane, one], r[lane, one], 0.0, ALU.max, ALU.bypass))
                chain(dve.tensor_tensor_scan(M[lane, two], r[lane, two], r[lane, two],
                                             M[lane, ends[0]:ends[0] + 1], ALU.max, ALU.bypass))
            dve.scalar_tensor_tensor(out=neg_m[:, :], in0=F[:, :], scalar=-1.0, in1=M[:, :],
                                     op0=ALU.mult, op1=ALU.subtract).then_inc(rows_ready, 1)
            dve.wait_ge(cols_done, 1)
            dve.tensor_copy(colM[:, :, :], turned[:, 0, 0:2 * P].rearrange("p (a b) -> p a b", a=2)).then_inc(cols_out, 1)
            dve.wait_ge(cols_out, 1)
            dve.wait_ge(guarded, 1)
            for n, (head, tt) in enumerate(steps):
                for d in range(2):
                    lane = 32 + 64 * d + head
                    dve.wait_ge(row_done, 2 * n + d + 1)
                    if n:
                        dve.wait_ge(combined, n)
                    dve.tensor_scalar(w[:, d, :], row[:, d, :], colM[:, tt, lane:lane + 1], 0.0,
                                      ALU.subtract, ALU.min).then_inc(shifted, 1)
                if n >= 1:
                    dve.wait_ge(transposed, n)
                dve.wait_ge(scores_out, n + 1)
                for d in range(2):
                    lane = 32 + 64 * d + head
                    dve.wait_ge(masked, 2 * n + d + 1)
                    chain(dve.tensor_tensor_reduce(sc[:, d, :], w[:, d, :], s_sb[:, :], 1.0, 0.0, ALU.mult, ALU.add,
                                                   den[:, d, 0:1]))
                    chain(dve.tensor_scalar(den[:, d, 1:2], den[:, d, 0:1], -1.0, den[:, d, 0:1], ALU.mult, ALU.max))
                    chain(dve.tensor_tensor(den[:, d, 1:2], den[:, d, 1:2], guard[:, tt, lane:lane + 1], ALU.max))
                    chain(dve.reciprocal(den[:, d, 1:2], den[:, d, 1:2]))
                chain(dve.tensor_scalar(sc[:, 0, :], sc[:, 0, :], den[:, 0, 1:2], None, ALU.mult))
                dve.scalar_tensor_tensor(out=sc[:, 1, :], in0=sc[:, 1, :], scalar=den[:, 1, 1:2], in1=sc[:, 0, :],
                                         op0=ALU.mult, op1=ALU.add).then_inc(combined, 1)

        @block.tensor
        def _(pe):
            pe.wait_ge(rows_ready, 1)
            for tt in range(2):
                pe.transpose(turned[:, 0, tt * P:(tt + 1) * P], M[:, tt * P:(tt + 1) * P], ident)
                last = pe.transpose(turned[:, 1, tt * P:(tt + 1) * P], neg_m[:, tt * P:(tt + 1) * P], ident)
            last.then_inc(cols_done, 1)
            pe.wait_ge(loaded, 32)

            def score(n):
                head, tt = steps[n]
                if n:
                    pe.wait_ge(scores_out, n)
                pe.matmul(raw[:, :], q[:, head, tt * P:(tt + 1) * P], k[:, head, :], start=True, stop=True).then_inc(scored, 1)
                for d, lane in enumerate(lanes):
                    if n:
                        pe.wait_ge(shifted, 2 * (n - 1) + d + 1)
                    pe.matmul(row[:, d, :], sel[lane, head, :], r[lane, :], start=True, stop=True,
                              tile_position=(lane.start, 0)).then_inc(row_done, 1)

            score(0)
            for n, (head, tt) in enumerate(steps):
                if n + 1 < len(steps):
                    score(n + 1)
                pe.wait_ge(combined, n + 1)
                if n == 0:
                    pe.wait_ge(cols_out, 1)
                    pe.wait_ge(guarded, 1)
                if n >= 2:
                    pe.wait_ge(copied, n - 1)
                for b in range(4):
                    last = pe.transpose(turned[:, n % 2, b * P:(b + 1) * P], sc[:, 1, b * P:(b + 1) * P], ident)
                last.then_inc(transposed, 1)
                pe.wait_ge(copied, n + 1)
                if n >= 2:
                    pe.wait_ge(evacuated, n - 1)
                for c in range(2):
                    for b in range(4):
                        at = head * ML_DV + c * P
                        last = pe.matmul(o[:, n % 2, c * P:(c + 1) * P], v[:, b, at:at + P], scT[:, b, :],
                                         start=(b == 0), stop=(b == 3))
                last.then_inc(summed, 1)

        @block.scalar
        def _(act):
            act.wait_ge(cols_done, 1)
            act.activation(guard[:, :, :], turned[:, 1, 0:2 * P].rearrange("p (a b) -> p a b", a=2),
                           ACT.Exp).then_inc(guarded, 1)
            for n, (head, tt) in enumerate(steps):
                act.wait_ge(scored, n + 1)
                if n:
                    act.wait_ge(combined, n)
                act.activation(s_sb[:, :], raw[:, :], ACT.Copy, scale=ML_SCALE).then_inc(scores_out, 1)
                for d in range(2):
                    act.wait_ge(shifted, 2 * n + d + 1)
                    act.activation(w[:, d, :], w[:, d, :], ACT.Exp).then_inc(exped, 1)
                act.wait_ge(transposed, n + 1)
                if n:
                    act.wait_ge(summed, n)
                act.activation(scT[:, :, :].rearrange("p b t -> p (b t)"), turned[:, n % 2, :], ACT.Copy).then_inc(copied, 1)
                act.wait_ge(summed, n + 1)
                act.activation(out[:, 2 * head:2 * head + 2, tt * P:(tt + 1) * P],
                               o[:, n % 2, 0:2 * P].rearrange("p (c t) -> p c t", c=2), ACT.Copy).then_inc(evacuated, 1)


def log_forget(nc, name, gx):
    with stage(nc, name) as S:
        e = S.sb("e", [P, 2 * T])
        mn = S.sb("mn", [P, 2 * T])
        exped, plus, ln_done = S.sem("exped"), S.sem("plus"), S.sem("ln_done")
        a_ordered = S.sem("a_ordered")
        block = S.block()

        @block.scalar
        def _(act):
            chain = Chain(act, a_ordered)
            chain(act.activation(e[:, :], gx[:, :], ACT.Abs))
            act.activation(e[:, :], e[:, :], ACT.Exp, scale=-1.0).then_inc(exped, 1)
            act.wait_ge(plus, 1)
            act.activation(e[:, :], e[:, :], ACT.Ln).then_inc(ln_done, 1)

        @block.vector
        def _(dve):
            dve.wait_ge(exped, 1)
            dve.tensor_scalar(mn[:, :], gx[:, :], 0.0, None, ALU.min)
            dve.tensor_scalar(e[:, :], e[:, :], 1.0, None, ALU.add).then_inc(plus, 1)
            dve.wait_ge(plus, 1)
            dve.wait_ge(ln_done, 1)
            for lo in (32, 96):
                dve.tensor_tensor(gx[lo:lo + 4, :], mn[lo:lo + 4, :], e[lo:lo + 4, :], ALU.subtract)


def odd_mixer(nc, W, h, modulation, scales, cols, const, sel_dram, mask_dram):
    TT = 2 * T
    ones = const[:, P:2 * P]
    with ExitStack() as ctx:
        def sb(name, shape):
            return ctx.enter_context(nc.sbuf_tensor("odd_" + name, shape, F32))

        gate = sb("gate", [P, KD, T])
        y = sb("y", [P, KD, T])
        with ExitStack() as inner:
            def tmp_sb(name, shape):
                return inner.enter_context(nc.sbuf_tensor("odd_" + name, shape, F32))

            x = tmp_sb("x", [P, KD, TT])
            q = tmp_sb("q", [P, ML_HEADS, T])
            k = tmp_sb("k", [P, ML_HEADS, TT])
            v = tmp_sb("v", [P, 4, 1024])
            gx = tmp_sb("gx", [P, TT])
            norm(nc, "odd_n", lambda c: h[:, c, :], lambda c: x[:, c, :], KD, TT, ones,
                 lambda c, s: scales[:, 1, 0, s, c:c + 1], ranges=[(0, T, LAT), (T, TT, CTX)],
                 shift=lambda c, s: modulation[:, 1, c, s:s + 1])
            first = W.take("odd_qk")
            at = col_at("gate_b")

            def heads(act, chain, c, ps):
                if c < 4:
                    return act.activation(q[:, c, :], ps[:, 0:T], ACT.Copy)
                if c < 8:
                    return act.activation(k[:, c - 4, :], ps[:, :], ACT.Copy)
                return act.activation(gx[:, :], ps[:, :], ACT.Identity, bias=cols[:, at:at + 1])

            jobs = column_jobs(W, first, 4, KD, T, lambda kk: x[:, kk, 0:T])
            jobs += column_jobs(W, first + 4, 5, KD, TT, lambda kk: x[:, kk, :])
            products(nc, W, "odd_qk", first, 9, jobs, heads, "scalar")
            log_forget(nc, "odd_lf", gx)
            first = W.take("odd_v")
            row_products(nc, W, "odd_v", first, 2, lambda kk, tt: x[:, kk, tt * P:(tt + 1) * P], 4,
                         lambda act, half, tt, ps: act.activation(v[:, tt, half * 512:(half + 1) * 512], ps, ACT.Copy))
            first = W.take("odd_gate")
            products(nc, W, "odd_g", first, 8, column_jobs(W, first, 8, KD, T, lambda kk: x[:, kk, 0:T]),
                     lambda act, chain, c, ps: act.activation(gate[:, c, :], ps[:, 0:T], ACT.Sigmoid), "scalar")
            mlstm(nc, "mlstm", gx, q, k, v, y, const, sel_dram, mask_dram)
        at_g = col_at("head_g")
        norm(nc, "odd_hn", lambda c: y[:, c, :], lambda c: y[:, c, :], 2, T, ones,
             lambda c, s: cols[:, at_g + c:at_g + c + 1], groups=ML_HEADS, mul=lambda c: gate[:, c, :])
        first = W.take("odd_out")
        products(nc, W, "odd_out", first, 8, column_jobs(W, first, 8, KD, T, lambda kk: y[:, kk, :]),
                 lambda dve, chain, c, ps: dve.scalar_tensor_tensor(
                     out=h[:, c, 0:T], in0=ps[:, 0:T], scalar=modulation[:, 1, 16 + c, LAT:LAT + 1],
                     in1=h[:, c, 0:T], op0=ALU.mult, op1=ALU.add), "vector")


def modulation_stage(nc, W, h, modulation, scales, cols, const, dram):
    first = W.take("mod")
    with stage(nc, "mod") as S:
        c_in = S.sb("c", [P, KD, 2])
        c_act = S.sb("c_act", [P, KD, 2])
        acc = S.ps("acc", [P, 2 * 96])
        loaded, silu_done, ordered, h_loaded = S.sem("loaded"), S.sem("silu_done"), S.sem("ordered"), S.sem("h_loaded")
        block = S.block()

        @block.sync
        def _(sync):
            W.prime(sync)
            W.feed(sync, first, 96)

        @block.scalar
        def _(act):
            act.dma_start(c_in[:, :, :].rearrange("p k s -> p (k s)"), dram["c_cols"]).then_inc(loaded, 16)
            act.dma_start(cols[:, :], dram["cols"]).then_inc(loaded, 16)
            act.dma_start(const[:, :], dram["const"]).then_inc(loaded, 16)
            act.dma_start(h[:, :, :].rearrange("p k t -> p (k t)"), dram["tokens"]).then_inc(h_loaded, 16)
            act.wait_ge(loaded, 48)
            act.activation(c_act[:, :, :], c_in[:, :, :], ACT.Silu).then_inc(silu_done, 1)
            act.wait_ge(h_loaded, 16)

        @block.tensor
        def _(pe):
            pe.wait_ge(silu_done, 1)
            for c in range(96):
                W.wait(pe, first + c)
                for k in range(KD):
                    last = pe.matmul(acc[:, 2 * c:2 * c + 2], W.slot(first + c)[:, k * P:(k + 1) * P], c_act[:, k, :],
                                     start=(k == 0), stop=(k == KD - 1))
                last.then_inc(W.used, 1)

        @block.vector
        def _(dve):
            chain = Chain(dve, ordered)
            dve.wait_ge(loaded, 48)
            dve.wait_ge(W.used, first + 96)
            at = col_at("b_mod")
            chain(dve.tensor_tensor(modulation[:, :, :, :], acc[:, :].rearrange("p (l c s) -> p l c s", l=2, s=2),
                                    cols[:, at:at + 96].rearrange("p (l c) -> p l c", l=2).unsqueeze(3)
                                    .to_broadcast([P, 2, 48, 2]), ALU.add))
            for layer in range(2):
                for n in range(2):
                    at = col_at("norm%d" % (n + 1)) + 8 * layer
                    for s in range(2):
                        lo = 8 + 24 * n
                        dve.scalar_tensor_tensor(out=scales[:, layer, n, s, :], in0=modulation[:, layer, lo:lo + 8, s],
                                                 scalar=1.0, in1=cols[:, at:at + 8], op0=ALU.add, op1=ALU.mult)


C_HEAD0, B_HEAD0 = 12, 4


def bias_stage(nc, bias, cmp_bias, neg_lam, cols, dram):
    PER = 16
    with stage(nc, "bias") as S:
        onehot = S.sb("onehot", [34, 4 * P])
        table = S.sb("table", [34, N_BIAS])
        acc = S.ps("acc", [P, 4, 512])
        prod = S.sb("prod", [P, 2, 2, 64])
        dots = S.sb("dots", [P, 2, 2])
        loaded, filled, copied, ordered, dotted, exped = (
            S.sem(n) for n in ("loaded", "filled", "copied", "ordered", "dotted", "exped"))
        rounds = T // PER
        block = S.block()

        @block.sync
        def _(sync):
            sync.dma_start(onehot[:, :], dram["onehot"]).then_inc(loaded, 16)
            sync.dma_start(table[0:32, :], dram["rel_bias"]).then_inc(loaded, 16)
            sync.dma_start(table[32:34, :], dram["masked"]).then_inc(loaded, 16)

        @block.tensor
        def _(pe):
            pe.wait_ge(loaded, 48)
            for r in range(rounds + 2):
                if r >= 4:
                    pe.wait_ge(copied, r - 3)
                for j in range(PER if r < rounds else N_CMP):
                    x0 = 384 - (r * PER + j) if r < rounds else 225 + P * (r - rounds) - 16 * j
                    last = pe.matmul(acc[:, r % 4, j * N_BIAS:(j + 1) * N_BIAS], onehot[:, x0:x0 + P], table[:, :],
                                     start=True, stop=True)
                last.then_inc(filled, 1)

        @block.scalar
        def _(act):
            for r in range(rounds):
                act.wait_ge(filled, r + 1)
                act.activation(bias[:, :, r * PER:(r + 1) * PER],
                               acc[:, r % 4, 0:PER * N_BIAS].rearrange("p (c h) -> p h c", h=N_BIAS),
                               ACT.Copy).then_inc(copied, 1)
            act.wait_ge(ordered, 1)
            for tt in range(2):
                act.wait_ge(filled, rounds + tt + 1)
                act.activation(cmp_bias[:, tt, :, 0:N_CMP],
                               acc[:, (rounds + tt) % 4, 0:N_CMP * N_BIAS].rearrange("p (c h) -> p h c", h=N_BIAS)
                               [:, B_HEAD0:B_HEAD0 + 8, :], ACT.Copy).then_inc(copied, 1)
            act.wait_ge(dotted, 1)
            act.activation(dots[:, :, :], dots[:, :, :], ACT.Exp).then_inc(exped, 1)

        @block.vector
        def _(dve):
            chain = Chain(dve, ordered)
            chain(dve.memset(cmp_bias[:, :, :, :], NEG))
            at = col_at("lam")
            lam = cols[:, at:at + 512].rearrange("p (l a b d) -> p l a b d", l=2, a=2, b=2)
            for layer in range(2):
                last = dve.tensor_tensor(prod[:, layer, :, :], lam[:, layer, :, 0, :], lam[:, layer, :, 1, :], ALU.mult)
            chain(last)
            dve.tensor_reduce(dots[:, :, :], prod[:, :, :, :], X_AXIS, ALU.add).then_inc(dotted, 1)
            dve.wait_ge(exped, 1)
            for layer in range(2):
                init = 0.8 - 0.6 * math.exp(-0.3 * layer)
                dve.tensor_scalar(neg_lam[:, layer:layer + 1], dots[:, layer, 1:2], dots[:, layer, 0:1], -init,
                                  ALU.subtract, ALU.add)


def compress_stage(nc, W, layer, X, kc, vc, cols):
    first = W.take("cmp%d" % layer)
    with nc.sbuf_tensor("cmp%d_hid" % layer, [P, 2, 2, 2 * N_CMP], F32) as hid:
        with stage(nc, "cmp1") as S:
            acc = S.ps("acc", [P, 2, 2, 2, 512])
            pos_sum = S.sb("pos_sum", [P, 2, 2])
            pos_out = S.sem("pos_out")
            block = S.block()
            at = col_at("pos") + 32 * layer

            @block.sync
            def _(sync):
                W.feed(sync, first, 8)

            @block.tensor
            def _(pe):
                for kv in range(2):
                    for pp in range(16):
                        g = first + 4 * kv + pp // 4
                        W.wait(pe, g)
                        for hc in range(2):
                            lhsT = W.slot(g)[:, (pp % 4) * 256 + hc * P:(pp % 4) * 256 + (hc + 1) * P]
                            blocks = X[:, kv, :, 2 * pp:2 * pp + 16 * (N_CMP - 1) + 1:16]
                            pe.matmul(acc[:, kv, hc, 0, 0:2 * N_CMP], lhsT, blocks, start=(pp == 0), stop=(pp == 15))
                            last = pe.matmul(acc[:, kv, hc, 1, 0:1], lhsT, cols[:, at + 16 * kv + pp:at + 16 * kv + pp + 1],
                                             start=(pp == 0), stop=(pp == 15))
                        if pp % 4 == 3:
                            last.then_inc(W.used, 1)

            @block.vector
            def _(dve):
                for kv in range(2):
                    dve.wait_ge(W.used, first + 4 * kv + 4)
                    dve.tensor_copy(pos_sum[:, kv, :], acc[:, kv, :, 1, 0]).then_inc(pos_out, 1)

            @block.scalar
            def _(act):
                for kv in range(2):
                    act.wait_ge(pos_out, kv + 1)
                    act.wait_ge(W.used, first + 4 * kv + 4)
                    for hc in range(2):
                        act.activation(hid[:, kv, hc, :], acc[:, kv, hc, 0, 0:2 * N_CMP], ACT.Gelu_apprx_tanh,
                                       bias=pos_sum[:, kv, hc:hc + 1])

        with stage(nc, "cmp2") as S:
            acc = S.ps("acc", [P, 2, 512])
            cleared = S.sem("cleared")
            block = S.block()
            g = first + 8

            @block.sync
            def _(sync):
                W.feed(sync, g, 1)

            @block.tensor
            def _(pe):
                W.wait(pe, g)
                tile = W.slot(g)
                for hc in range(2):
                    pe.matmul(acc[:, 0, 0:2 * N_CMP], tile[:, hc * P:(hc + 1) * P], hid[:, 0, hc, :],
                              start=(hc == 0), stop=(hc == 1))
                for grp in range(2):
                    for hc in range(2):
                        last = pe.matmul(acc[0:N_CMP, 1, grp * P:(grp + 1) * P],
                                         hid[:, 1, hc, grp * N_CMP:(grp + 1) * N_CMP],
                                         tile[:, (2 + hc) * P:(3 + hc) * P], start=(hc == 0), stop=(hc == 1))
                last.then_inc(W.used, 1)

            @block.vector
            def _(dve):
                dve.memset(kc[:, :], 0.0)
                dve.memset(vc[:, :, :], 0.0).then_inc(cleared, 1)
                dve.wait_ge(cleared, 1)
                dve.wait_ge(W.used, g + 1)
                for grp in range(2):
                    dve.tensor_copy(kc[64 * grp:64 * grp + 64, 0:N_CMP],
                                    acc[64 * grp:64 * grp + 64, 0, grp * N_CMP:(grp + 1) * N_CMP])
                dve.tensor_copy(vc[0:N_CMP, :, :], acc[0:N_CMP, 1, 0:2 * P].rearrange("p (g d) -> p g d", g=2))


def small_gates(nc, name, rows, gates, cmp_gates, valid):
    with stage(nc, name) as S:
        done = S.sem("done")
        block = S.block()

        @block.scalar
        def _(act):
            act.activation(gates[:, :, :], rows[:, :, 384:408], ACT.Sigmoid).then_inc(done, 1)

        @block.vector
        def _(dve):
            dve.wait_ge(done, 1)
            by = gates[:, :, :].rearrange("p t (h b) -> p t h b", b=3)
            dve.tensor_scalar(cmp_gates[:, 0, :], by[:, 0, :, 0], valid, None, ALU.mult)
            dve.tensor_copy(cmp_gates[:, 1, :], by[:, 1, :, 0])


def causal_units(q, k, v, bias, tt, **more):
    nk = P * (tt + 1)
    return Unit(q[:, tt * P:(tt + 1) * P], k[:, 0:nk], v, nk, 64 ** -0.5, bias=bias[:, 2 * P - nk:2 * P], **more)


def second_layer(nc, W, layer, h, bias, cmp_bias, neg_lam, cols, const, dram):
    ones, ident = const[:, P:2 * P], const[:, 0:P]
    n = str(layer)

    def norm_to(dst, which, name):
        at = col_at("norms") + 32 * layer + 8 * which
        norm(nc, name, lambda c: h[:, c, 0:T], lambda c: dst[:, c, :], KD, T, ones, lambda c, s: cols[:, at + c:at + c + 1])

    with ExitStack() as ctx:
        def sb(name, shape):
            return ctx.enter_context(nc.sbuf_tensor("second%d_%s" % (layer, name), shape, F32))

        x = sb("x", [P, KD, T])
        norm_to(x, 0, "ffn1n")
        feed_forward(nc, W, "ffn1_" + n, x, h)
        norm_to(x, 1, "attn_n")
        merged = sb("merged", [P, KD, T])
        with ExitStack() as inner:
            def tmp_sb(name, shape):
                return inner.enter_context(nc.sbuf_tensor("second%d_%s" % (layer, name), shape, F32))

            y = tmp_sb("y", [P, 3, 4, T])
            with ExitStack() as attn:
                def at_sb(name, shape):
                    return attn.enter_context(nc.sbuf_tensor("second%d_%s" % (layer, name), shape, F32))

                heads = at_sb("heads", [P, 19, T])
                X = at_sb("X", [P, 2, 2, T])
                av = at_sb("av", [P, 2, 512])
                rows = at_sb("rows", [P, 2, 512])
                kc = at_sb("kc", [P, P])
                vc = at_sb("vc", [P, 2, P])
                gates = at_sb("gates", [P, 2, 24])
                cmp_gates = at_sb("cmp_gates", [P, 2, 8])
                first = W.take("in_cols" + n)

                def evacuate(act, chain, c, ps):
                    if c < 19:
                        return act.activation(heads[:, c, :], ps[:, 0:T], ACT.Copy)
                    for g in range(2):
                        act.activation(X[0:64, c - 19, g, :], ps[64 * g:64 * g + 64, 0:T], ACT.Copy)
                        last = act.activation(X[64:128, c - 19, g, 0:T - 1], ps[64 * g:64 * g + 64, 1:T], ACT.Copy)
                    return last

                products(nc, W, "in_cols", first, 21, column_jobs(W, first, 21, KD, T, lambda k: x[:, k, :]),
                         evacuate, "scalar")
                first = W.take("in_rows" + n)
                row_products(nc, W, "in_rows", first, 2, lambda k, tt: x[:, k, tt * P:(tt + 1) * P], 2,
                             lambda act, half, tt, ps: act.activation((av, rows)[half][:, tt, :], ps, ACT.Copy))
                small_gates(nc, "small_gates", rows, gates, cmp_gates, cols[:, col_at("valid"):col_at("valid") + 1])
                compress_stage(nc, W, layer, X, kc, vc, cols)

                units = []
                for head in range(4):
                    for tt in range(2):
                        for c in range(2):
                            half = slice(64 * c, 64 * c + 64)
                            units.append(causal_units(
                                heads[half, head, :], heads[half, 4 + head, :],
                                lambda b, head=head: av[:, b, head * P:(head + 1) * P], bias[:, head, :], tt,
                                weight=neg_lam[:, layer:layer + 1] if c else None, first=c == 0, end=c == 1,
                                out=(0, P, y[:, 0, head, tt * P:(tt + 1) * P])))
                for g in range(2):
                    half = slice(64 * g, 64 * g + 64)
                    for r in range(4):
                        head = 4 * g + r
                        for tt in range(2):
                            tok = slice(tt * P, (tt + 1) * P)
                            out = (64 * g, 64 * g + 64, y[half, 1, r, tok])
                            units.append(Unit(heads[half, 8 + r, tok], kc[half, :], lambda b, g=g: vc[:, g, :], P,
                                              64 ** -0.5, bias=cmp_bias[:, tt, head, :],
                                              weight=cmp_gates[:, tt, head:head + 1], first=True, end=False))
                            for br in (1, 2):
                                gate = gates[:, tt, 3 * head + br:3 * head + br + 1]
                                units.append(causal_units(
                                    heads[half, 8 + r, :], heads[half, 11 + br, :],
                                    lambda b, br=br: rows[:, b, (br - 1) * P:br * P], bias[:, B_HEAD0 + head, :], tt,
                                    weight=gate, first=False, end=br == 2, out=out))
                    for r in range(4):
                        head = 4 * g + r
                        at = col_at("sinks") + 8 * layer + head
                        for tt in range(2):
                            units.append(causal_units(
                                heads[half, 14 + r, :], heads[half, 18, :], lambda b: rows[:, b, 2 * P:3 * P],
                                bias[:, C_HEAD0 + head, :], tt, sink=cols[:, at:at + 1],
                                out=(64 * g, 64 * g + 64, y[half, 2, r, tt * P:(tt + 1) * P])))
                attention(nc, "attn", units, ident)
            at = col_at("subln") + layer
            norm(nc, "subln", lambda c: y[:, 0, c, :], lambda c: y[:, 0, c, :], 1, T, ones, lambda c, s: cols[:, at:at + 1],
                 groups=4, post=0.2 + 0.6 * math.exp(-0.3 * layer))
            sig = tmp_sb("sig", [P, 3, KD, T])
            term = tmp_sb("term", [P, 2, T])
            first = W.take("gates" + n)
            products(nc, W, "gates", first, 24, column_jobs(W, first, 24, KD, T, lambda k: x[:, k, :]),
                     lambda act, chain, c, ps: act.activation(sig[:, c // 8, c % 8, :], ps[:, 0:T], ACT.Sigmoid), "scalar")
            first = W.take("branch" + n)
            jobs = []
            for br in range(3):
                jobs += column_jobs(W, first + 4 * br, 8, 4, T, lambda k, br=br: y[:, br, k, :])

            def merge(dve, chain, c, ps):
                br, j = c // 8, c % 8
                if br == 0:
                    return dve.tensor_tensor(merged[:, j, :], ps[:, 0:T], sig[:, br, j, :], ALU.mult)
                chain(dve.tensor_tensor(term[:, c % 2, :], ps[:, 0:T], sig[:, br, j, :], ALU.mult))
                return dve.tensor_tensor(merged[:, j, :], merged[:, j, :], term[:, c % 2, :], ALU.add)

            products(nc, W, "branch", first, 12, jobs, merge, "vector")
        first = W.take("out" + n)
        products(nc, W, "out", first, 8, column_jobs(W, first, 8, KD, T, lambda k: merged[:, k, :]),
                 lambda dve, chain, c, ps: dve.tensor_tensor(h[:, c, 0:T], h[:, c, 0:T], ps[:, 0:T], ALU.add), "vector")
        norm_to(x, 2, "ffn2n")
        feed_forward(nc, W, "ffn2_" + n, x, h)
        norm_to(x, 3, "ple_n")
        p_in = sb("p", [P, 2, T])
        pw = sb("pw", [P, KD, T])
        first = W.take("ple_w" + n)
        products(nc, W, "ple_w", first, 2, column_jobs(W, first, 8, 2, T, lambda k: p_in[:, k, :]),
                 lambda act, chain, c, ps: act.activation(pw[:, c, :], ps[:, 0:T], ACT.Copy), "scalar",
                 const_load=[(p_in[:, :, :].rearrange("p k t -> p (k t)"), dram["p" + n])], pe_const=True)
        first = W.take("ple_gate" + n)
        products(nc, W, "ple_gate", first, 8, column_jobs(W, first, 8, KD, T, lambda k: x[:, k, :]),
                 lambda act, chain, c, ps: act.activation(merged[:, c, :], ps[:, 0:T], ACT.Sigmoid), "scalar")
        with stage(nc, "ple_add") as S:
            done = S.sem("done")
            block = S.block()

            @block.vector
            def _(dve):
                dve.tensor_tensor(pw[:, :, :], pw[:, :, :], merged[:, :, :], ALU.mult).then_inc(done, 1)
                dve.wait_ge(done, 1)
                dve.tensor_tensor(h[:, :, 0:T], h[:, :, 0:T], pw[:, :, :], ALU.add)


def store_stage(nc, y, out):
    with stage(nc, "store") as S:
        stored = S.sem("stored")
        block = S.block()

        @block.sync
        def _(sync):
            sync.dma_start(out, y[:, :, :].rearrange("p k t -> p (k t)")).then_inc(stored, 16)
            sync.wait_ge(stored, 16)


def build(nc, dram, out, debug=None, upto=99):
    def dump(name, ap):
        if debug is not None:
            debug(name, ap)

    STAGES[0] = 0
    cols = nc.alloc_sbuf_tensor("cols_sb", [P, N_COLS], F32)
    const = nc.alloc_sbuf_tensor("const_sb", [P, N_CONST], F32)
    modulation = nc.alloc_sbuf_tensor("modulation", [P, 2, 48, 2], F32)
    scales = nc.alloc_sbuf_tensor("scales", [P, 2, 2, 2, KD], F32)
    h = nc.alloc_sbuf_tensor("h", [P, KD, 2 * T], F32)
    W = Weights(nc, dram["w_tiles"], dram["peer_tiles"])
    modulation_stage(nc, W, h, modulation, scales, cols, const, dram)
    even_mixer(nc, W, h, modulation, scales, cols, const, dram["rope"])
    dump("h_even", h)
    if upto <= 1:
        return
    for s in (LAT, CTX):
        peer(nc, W, 0, s, h[:, :, s * T:(s + 1) * T], lambda c, s=s: scales[:, 0, 1, s, c:c + 1],
             lambda c, s=s: modulation[:, 0, 24 + c, s:s + 1], lambda c, s=s: modulation[:, 0, 40 + c, s:s + 1], const)
        if upto <= 2:
            dump("h_peer", h)
            return
    dump("h_peer0", h)
    odd_mixer(nc, W, h, modulation, scales, cols, const, dram["select"], dram["masks"])
    dump("h_odd", h)
    peer(nc, W, 1, LAT, h[:, :, 0:T], lambda c: scales[:, 1, 1, LAT, c:c + 1],
         lambda c: modulation[:, 1, 24 + c, LAT:LAT + 1], lambda c: modulation[:, 1, 40 + c, LAT:LAT + 1], const)
    ones = const[:, P:2 * P]
    at = col_at("norm_f")
    norm(nc, "norm_f", lambda c: h[:, c, 0:T], lambda c: h[:, c, 0:T], KD, T, ones, lambda c, s: cols[:, at + c:at + c + 1])
    dump("h_first", h)
    with nc.sbuf_tensor("bias_sb", [P, N_BIAS, T], F32) as bias, nc.sbuf_tensor("cmp_bias", [P, 2, 8, P], F32) as cmp_bias, \
            nc.sbuf_tensor("neg_lam", [P, 2], F32) as neg_lam:
        bias_stage(nc, bias, cmp_bias, neg_lam, cols, dram)
        for layer in range(2):
            second_layer(nc, W, layer, h, bias, cmp_bias, neg_lam, cols, const, dram)
            dump("h_second%d" % layer, h)
    with nc.sbuf_tensor("y_out", [P, KD, T], F32) as y:
        at2 = col_at("final")
        norm(nc, "final", lambda c: h[:, c, 0:T], lambda c: y[:, c, :], KD, T, ones,
             lambda c, s: cols[:, at2 + c:at2 + c + 1])
        store_stage(nc, y, out)


def column_tiles(w):
    k = w.shape[0] // P
    per = KD // k
    n = -(-w.shape[1] // (P * per)) * per
    full = np.zeros((k * P, n * P), w.dtype)
    full[:, :w.shape[1]] = w
    a = full.reshape(k, P, n // per, per, P).transpose(2, 1, 3, 0, 4)
    return a.reshape(n // per, P, TILE)


def row_tiles(w):
    n = -(-w.shape[1] // 512)
    full = np.zeros((w.shape[0], n * 512), w.dtype)
    full[:, :w.shape[1]] = w
    return full.reshape(4, 2, P, n, 512).transpose(3, 0, 2, 1, 4).reshape(4 * n, P, TILE)


def padded_tile(a):
    a = a.reshape(P, -1)
    out = np.zeros((1, P, TILE), a.dtype)
    out[0, :, :a.shape[1]] = a
    return out


def swapped_rope(w):
    return np.concatenate([w[..., 16:32], w[..., 0:16]], axis=-1)


def pair_heads(w, axis):
    w = np.moveaxis(w, axis, 0)
    rest = w.shape[1:]
    w = w.reshape((2, 4, 64) + rest).transpose((1, 0, 2) + tuple(range(3, 3 + len(rest)))).reshape((512,) + rest)
    return np.moveaxis(w, 0, axis)


def feed_forward_tiles(wi, wo):
    gate, up = column_tiles(wi[:, :D_FF]), column_tiles(wi[:, D_FF:])
    down = wo.reshape(FC, P, D)
    out = [gate[0], up[0]]
    for c in range(FC):
        if c + 1 < FC:
            out += [gate[c + 1], up[c + 1]]
        out.append(down[c])
    return np.stack(out)


def layout_weights(a):
    f = {}
    f["mod"] = np.concatenate([column_tiles(a["w_mod"][i]) for i in range(2)])
    w = a["even_w_in"][0]
    kr = w[:, 384:416]
    conv = [w[:, 416 + 512 * i:928 + 512 * i].reshape(D, 4, P) for i in range(3)]
    triples = np.stack([conv[1], conv[2], conv[0]], axis=2).reshape(D, 1536)
    f["even_in"] = column_tiles(np.concatenate([w[:, :384], np.zeros((D, 64), w.dtype), kr, swapped_rope(kr), triples], 1))
    uq = a["mla_w_uq"][0].reshape(256, MLA_HEADS, 96)
    f["uq"] = column_tiles(np.concatenate([uq, swapped_rope(uq[..., 64:])], -1).reshape(256, 1024))
    f["ukv"] = a["mla_w_ukv"][0].reshape(P, MLA_HEADS, 2, 64).transpose(0, 2, 1, 3).reshape(1, P, TILE)
    f["even_out"] = column_tiles(a["even_w_out"][0])
    for layer in range(2):
        f["peer_q%d" % layer] = column_tiles(a["peer_w_q"][layer])
        f["subkeys%d" % layer] = a["peer_subkeys"][layer].reshape(2, 8, P, P).transpose(0, 3, 1, 2).reshape(2, P, TILE)
    w = a["odd_w_in"][0]
    gates = np.zeros((D, 4, 32), w.dtype)
    gates[:, :, :4] = w[:, 2048:2064].reshape(D, 4, 4)
    f["odd_qk"] = column_tiles(np.concatenate([w[:, :1024], gates.reshape(D, P)], 1))
    f["odd_v"] = row_tiles(w[:, 1024:2048])
    f["odd_gate"] = column_tiles(w[:, 2064:])
    f["odd_out"] = column_tiles(a["odd_w_out"][0])
    for i in range(2):
        w, n = a["w_in_2"][i], str(i)
        f["ffn1_" + n] = feed_forward_tiles(a["ffn1_wi_2"][i], a["ffn1_wo_2"][i])
        f["ffn2_" + n] = feed_forward_tiles(a["ffn2_wi_2"][i], a["ffn2_wo_2"][i])
        f["in_cols" + n] = column_tiles(np.concatenate([
            w[:, 0:1024], pair_heads(w[:, 1536:2048], 1), w[:, 2304:2432], w[:, 2560:2688],
            pair_heads(w[:, 2840:3352], 1), w[:, 3352:3480], w[:, 2048:2304]], 1))
        f["in_rows" + n] = row_tiles(np.concatenate([
            w[:, 1024:1536], w[:, 2432:2560], w[:, 2688:2816], w[:, 3480:3608], w[:, 2816:2840]], 1))
        w1 = a["nsa_cmp_w1_2"][i].reshape(2, 4, 4, P, 256).transpose(0, 1, 3, 2, 4).reshape(8, P, TILE)
        w2 = a["nsa_cmp_w2_2"][i].reshape(2, 2, P, 64)
        w2 = np.concatenate([w2, w2], -1).transpose(2, 0, 1, 3)
        f["cmp" + n] = np.concatenate([w1, padded_tile(w2)])
        f["gates" + n] = column_tiles(w[:, 3608:])
        wb = a["w_branch_2"][i]
        f["branch" + n] = np.concatenate([column_tiles(x) for x in (wb[0], pair_heads(wb[1], 0), pair_heads(wb[2], 0))])
        f["out" + n] = column_tiles(a["w_out_2"][i])
        f["ple_w" + n] = column_tiles(a["w_ple_2"][i])
        f["ple_gate" + n] = column_tiles(a["w_ple_gate_2"][i])
    bases, size = tile_bases()
    out = np.empty((size["w"], P, TILE), np.float32)
    for name, n, source in stream_plan():
        if source == "w":
            assert f[name].shape == (n, P, TILE), (name, f[name].shape)
            out[bases[name]:bases[name] + n] = f[name]
    return out.reshape(-1, TILE)


def layout_experts(u, v):
    out = np.empty((2, PEER_TILES, P, TILE), u.dtype)
    for layer in range(2):
        ut = u[layer].reshape(NKEYS, NKEYS, KD, P).transpose(1, 3, 2, 0).reshape(NKEYS, P, TILE)
        vt = v[layer].reshape(NKEYS, NKEYS, D).transpose(1, 0, 2)
        out[layer, 0] = ut[0]
        out[layer, 1:-1:2] = ut[1:]
        out[layer, 2:-1:2] = vt[:-1]
        out[layer, -1] = vt[-1]
    return out.reshape(-1, TILE)


def features(v):
    return np.ascontiguousarray(v.reshape(-1, P).T)


def spread(v):
    return np.broadcast_to(v.reshape(1, -1), (P, v.size))


def layout_columns(a):
    gate_b = np.zeros((4, 32), np.float32)
    gate_b[:, :4] = a["mlstm_gate_b"][0].reshape(4, 4)
    pos = a["nsa_cmp_pos_2"].reshape(4, 16, P)
    parts = {
        "norm1": features(a["norm1_g"]), "norm2": features(a["norm2_g"]), "b_mod": features(a["b_mod"]),
        "q_norm": features(a["mla_q_norm"]), "kv_norm": features(a["mla_kv_norm"]), "conv": features(a["conv_w"]),
        "head_g": features(a["mlstm_head_g"]), "norm_f": features(a["norm_f_g"]), "norms": features(a["norm_g_2"]),
        "subln": features(a["diff_subln_2"]), "final": features(a["final_norm_2"]), "gate_b": gate_b.reshape(P, 1),
        "pos": pos.reshape(64, P).T, "lam": spread(a["diff_lambda_2"]), "sinks": spread(a["swa_sinks_2"]),
        "valid": (np.arange(P) >= 31).astype(np.float32).reshape(P, 1),
    }
    for name, width in COLS:
        assert parts[name].shape == (P, width), (name, parts[name].shape)
    return np.concatenate([parts[name] for name, _ in COLS], 1)


def constants():
    const = np.concatenate([np.eye(P), np.ones((P, P)), np.tile(np.arange(P), (P, 1)), np.tile(np.arange(16), (P, 1))],
                           1).astype(np.float32)
    inv = np.float32(10000.0) ** (-np.arange(8, dtype=np.float32) / np.float32(8))
    t = np.arange(T)
    ang = np.concatenate([(t // 64).astype(np.float32)[:, None] * inv, (t % 64).astype(np.float32)[:, None] * inv], -1)
    cos, sin = np.cos(ang).T, np.sin(ang).T
    rope = np.zeros((P, 2 * T), np.float32)
    rope[64:96, T:] = 1.0
    rope[64:96, :T] = np.concatenate([cos, cos])
    rope[96:128, :T] = np.concatenate([-sin, sin])
    dist = np.arange(512) - 256
    n = np.maximum(dist, 0)
    nf = np.maximum(n, 1).astype(np.float32)
    large = 16 + (np.log(nf / 16) / np.float32(math.log(8)) * 16).astype(np.int32)
    bucket = np.where(n < 16, n, np.minimum(large, 31))
    onehot = np.zeros((34, 512), np.float32)
    seen = dist >= 0
    onehot[bucket[seen], np.nonzero(seen)[0]] = 1.0
    onehot[32] = ~seen
    onehot[33] = dist >= 128
    masked = np.zeros((2, N_BIAS), np.float32)
    masked[0] = NEG
    masked[1, C_HEAD0:] = NEG
    select = np.zeros((P, ML_HEADS, P), np.float32)
    for hd in range(ML_HEADS):
        select[32 + hd, hd] = select[96 + hd, hd] = 1.0
    q = np.arange(T).reshape(2, P).T[:, :, None]
    s = np.arange(T)[None, None, :]
    masks = np.stack([s <= q, s >= q], 1).astype(np.float32)
    return {"const": const, "rope": rope, "onehot": onehot, "masked": masked, "select": select.reshape(P, -1),
            "masks": masks.reshape(P, -1)}


def layout(inputs):
    a = {k: np.asarray(v) for k, v in inputs.items()}

    def tokens(x):
        return x.T.reshape(-1, P, x.shape[0]).transpose(1, 0, 2)

    arrays = constants()
    arrays["w_tiles"] = layout_weights(a)
    arrays["peer_tiles"] = layout_experts(a["peer_u"], a["peer_v"])
    arrays["cols"] = layout_columns(a)
    arrays["tokens"] = np.concatenate([tokens(a["x"][0]), tokens(a["ctx"][0])], 2).reshape(P, -1)
    arrays["c_cols"] = np.stack([features(a["c"][0]), features(a["c_ctx"])], 2).reshape(P, -1)
    arrays["rel_bias"] = a["rel_bias_2"]
    for i in range(2):
        arrays["p%d" % i] = tokens(a["p_2"][i, 0]).reshape(P, -1)
    return {k: np.ascontiguousarray(v) for k, v in arrays.items()}


def kernel(**inputs):
    import concourse.bacc as bacc
    from concourse.bass_utils import run_bass_kernel_spmd

    arrays = layout(inputs)
    nc = bacc.Bacc("TRN2", target_bir_lowering=False, num_devices=1)
    dram = {name: nc.dram_tensor("in_" + name, x.shape, mybir.dt.from_np(x.dtype), kind="ExternalInput").ap()
            for name, x in arrays.items()}
    out = nc.dram_tensor("out_y", (P, KD * T), F32, kind="ExternalOutput").ap()
    build(nc, dram, out)
    r = run_bass_kernel_spmd(nc, [{"in_" + name: x for name, x in arrays.items()}], core_ids=[0])
    y = r.results[0]["out_y"].reshape(P, KD, T)
    return y.transpose(2, 1, 0).reshape(1, T, D)
```

```python
import math
from contextlib import ExitStack, contextmanager

import numpy as np

import concourse.bass as bass
from concourse import mybir

F32 = mybir.dt.float32
U32 = mybir.dt.uint32
F32R = mybir.dt.float32r
ALU = mybir.AluOpType
ACT = mybir.ActivationFunctionType
X_AXIS = mybir.AxisListType.X

P = 128
D = 1024
KD = D // P
T = 256
LAT, CTX = 0, 1
RING = 4
TILE = 1024
PARTS = 4
PART = TILE // 2
EPS = 1e-6
NEG = -1e30

MLA_HEADS, MLA_NOPE, MLA_ROPE, MLA_V = 8, 64, 32, 64
MLA_SCALE = (MLA_NOPE + MLA_ROPE) ** -0.5
ML_HEADS, ML_DV = 4, 256
ML_SCALE = 128 ** -0.5
PH, NKEYS, TOPK = 8, 128, 16
PEER_TILES = 2 * NKEYS
D_FF = 2816
FC = D_FF // P
N_BIAS = 20
N_CMP = 15
XT = T + 16


def stream_plan():
    def route(layer):
        return [("peer_q%d" % layer, 16, "w"), ("experts%d" % layer, PEER_TILES, "peer")]

    plan = [("mod", 96, "w"), ("even_in", 16, "w"), ("uq", 2, "w"), ("ukv", 1, "w"), ("even_out", 8, "w")]
    plan += route(0) + route(0)
    plan += [("odd_qk", 9, "w"), ("odd_v", 8, "w"), ("odd_gate", 8, "w"), ("odd_out", 8, "w")] + route(1)
    for i in range(2):
        plan += [(name + str(i), n, "w") for name, n in (
            ("ffn1_", 3 * FC), ("in_cols", 21), ("in_rows", 8), ("cmp", 9), ("gates", 24), ("branch", 12),
            ("out", 8), ("ffn2_", 3 * FC), ("ple_w", 2), ("ple_gate", 8))]
    return plan


def tile_bases():
    bases, nxt = {}, {"w": 0, "peer": 0}
    for name, n, source in stream_plan():
        if name not in bases:
            bases[name] = nxt[source]
            nxt[source] += n
    return bases, nxt


COLS = [("norm1", 16), ("norm2", 16), ("b_mod", 96), ("q_norm", 2), ("kv_norm", 1), ("conv", 12), ("head_g", 8),
        ("norm_f", 8), ("gate_b", 1)]
COLS2 = [("norms", 64), ("subln", 2), ("final", 8), ("pos", 64), ("lam", 512), ("sinks", 16), ("valid", 1)]


def col_at(name):
    for columns in (COLS, COLS2):
        at = 0
        for n, w in columns:
            if n == name:
                return at
            at += w
    raise KeyError(name)


N_COLS = sum(w for _, w in COLS)
N_COLS2 = sum(w for _, w in COLS2)
N_CONST = 3 * P + 16


class Weights:

    def __init__(self, nc, w_tiles, peer_tiles):
        self.sources = {"w": w_tiles, "peer": peer_tiles}
        self.ring = nc.alloc_sbuf_tensor("weight_ring", [P, RING, TILE], F32)
        self.hi = nc.alloc_sbuf_tensor("weight_hi", [P, PARTS, PART], F32R)
        self.lo = nc.alloc_sbuf_tensor("weight_lo", [P, PARTS, PART], F32R)
        self.arrived = [nc.alloc_semaphore("tile_arrived%d" % i) for i in range(RING)]
        self.hi_done = nc.alloc_semaphore("parts_hi_done")
        self.lo_done = nc.alloc_semaphore("parts_lo_done")
        self.used = nc.alloc_semaphore("parts_used")
        self.plan = stream_plan()
        bases, _ = tile_bases()
        self.tiles = []
        for name, n, source in self.plan:
            self.tiles += [(source, bases[name] + i) for i in range(n)]
        self.at = 0
        self.seg = 0

    def take(self, name):
        got, n, _ = self.plan[self.seg]
        assert got == name, (got, name)
        first = self.at
        self.at += n
        self.seg += 1
        return first

    def wait(self, pe, part):
        pe.wait_ge(self.lo_done, part + 1)

    def load(self, sync, g):
        source, i = self.tiles[g]
        sync.dma_start(self.ring[:, g % RING, :], self.sources[source][i * P:(i + 1) * P, :]
                       ).then_inc(self.arrived[g % RING], 16)

    def prime(self, sync):
        for g in range(RING):
            self.load(sync, g)

    def feed(self, sync, first, n):
        for g in range(first + RING, min(first + n + RING, len(self.tiles))):
            sync.wait_ge(self.lo_done, 2 * (g - RING) + 2)
            self.load(sync, g)

    def write_hi(self, act, part):
        if part < 2 * len(self.tiles):
            g = part // 2
            act.wait_ge(self.arrived[g % RING], 16 * (g // RING + 1))
            act.activation(self.hi[:, part % PARTS, :], self.ring[:, g % RING, (part % 2) * PART:(part % 2 + 1) * PART],
                           ACT.Copy).then_inc(self.hi_done, 1)

    def write_lo(self, dve, part):
        if part < 2 * len(self.tiles):
            g = part // 2
            dve.wait_ge(self.hi_done, part + 1)
            dve.tensor_tensor(self.lo[:, part % PARTS, :], self.ring[:, g % RING, (part % 2) * PART:(part % 2 + 1) * PART],
                              self.hi[:, part % PARTS, :].bitcast(F32), ALU.subtract).then_inc(self.lo_done, 1)

    def next_hi(self, act, part):
        act.wait_ge(self.used, part + 1)
        self.write_hi(act, part + PARTS)

    def next_lo(self, dve, part):
        self.write_lo(dve, part + PARTS)

    def stationary(self, part, at, x):
        w_hi, w_lo = (w[:, part % PARTS, at:at + P] for w in (self.hi, self.lo))
        return [(w_hi, x[0]), (w_hi, x[1]), (w_lo, x[0])]

    def moving(self, part, x):
        w_hi, w_lo = (w[:, part % PARTS, :] for w in (self.hi, self.lo))
        return [(x[0], w_hi), (x[0], w_lo), (x[1], w_hi)]


def run_passes(pe, out, passes, start, stop, **more):
    for i, (lhsT, rhs) in enumerate(passes):
        last = pe.matmul(out, lhsT, rhs, start=start and i == 0, stop=stop and i == len(passes) - 1, **more)
    return last


def split_pair(hi, lo):
    return lambda k: (hi[:, k, :], lo[:, k, :])


class Stage:
    def __init__(self, nc, name, ctx):
        self.nc, self.name, self.ctx = nc, name, ctx

    def sem(self, name):
        return self.nc.alloc_semaphore("%s_%s" % (self.name, name))

    def sb(self, name, shape, dt=F32):
        return self.ctx.enter_context(self.nc.sbuf_tensor("%s_%s" % (self.name, name), shape, dt))

    def ps(self, name, shape):
        return self.ctx.enter_context(self.nc.psum_tensor("%s_%s" % (self.name, name), shape, F32))

    def block(self):
        return self.ctx.enter_context(self.nc.Block())


STAGES = [0]


@contextmanager
def stage(nc, name):
    STAGES[0] += 1
    with nc.cleanup_on_exit():
        with ExitStack() as ctx:
            yield Stage(nc, "%s_%d" % (name, STAGES[0]), ctx)


class Chain:

    def __init__(self, eng, sem):
        self.eng, self.sem, self.n = eng, sem, 0

    def __call__(self, ins):
        self.n += 1
        ins.then_inc(self.sem, 1)
        self.eng.wait_ge(self.sem, self.n)


class Job:

    def __init__(self, mms):
        self.mms = mms
        self.part = mms[-1][1]


def column_jobs(W, first, n_chunks, K, N, x):
    jobs = []
    for c in range(n_chunks):
        mms = []
        for k in range(K):
            at = (c * K + k) * P
            part = 2 * first + at // PART
            mms.append(((0, N), part, W.stationary(part, at % PART, x(k)), k == 0, k == K - 1))
        jobs.append(Job(mms))
    return jobs


def products(nc, W, name, first, n_tiles, jobs, evacuate, who, prepare=None, const_load=None,
             evacuated_out=None, banks=4):
    with stage(nc, name) as S:
        acc = S.ps("acc", [P, banks, 512])
        job_done = S.sem("job_done")
        evacuated = S.sem("evacuated")
        ordered = S.sem("ordered")
        const_in = S.sem("const_in")
        if evacuated_out is not None:
            evacuated_out.append(evacuated)
        last_mm = {mm[1]: (c, i) for c, j in enumerate(jobs) for i, mm in enumerate(j.mms)}
        ready, within = [], 0
        for c, j in enumerate(jobs):
            if last_mm[j.part] == (c, len(j.mms) - 1):
                ready.append((W.used, j.part + 1))
            else:
                within += 1
                ready.append((job_done, within))
        parts = range(2 * first, 2 * (first + n_tiles))
        assert sorted(last_mm) == list(parts)
        block = S.block()

        @block.sync
        def _(sync):
            if const_load is not None:
                for dst, src in const_load:
                    sync.dma_start(dst, src).then_inc(const_in, 16)
            W.feed(sync, first, n_tiles)

        @block.tensor
        def _(pe):
            seen = None
            for c, j in enumerate(jobs):
                if c >= banks:
                    pe.wait_ge(evacuated, c - banks + 1)
                for i, ((lo, hi), part, passes, start, stop) in enumerate(j.mms):
                    if part != seen:
                        W.wait(pe, part)
                        seen = part
                    last = run_passes(pe, acc[:, c % banks, lo:hi], passes, start, stop)
                    if last_mm[part] == (c, i):
                        last.then_inc(W.used, 1)
                    elif i == len(j.mms) - 1:
                        last.then_inc(job_done, 1)

        def read_out(eng, chain, part):
            for c, j in enumerate(jobs):
                if j.part == part:
                    eng.wait_ge(*ready[c])
                    evacuate(eng, chain, c, acc[:, c % banks, :]).then_inc(evacuated, 1)

        def start(eng):
            chain = Chain(eng, ordered)
            if const_load is not None:
                eng.wait_ge(const_in, 16 * len(const_load))
            if prepare is not None:
                prepare(eng, chain)
            return chain

        @block.scalar
        def _(act):
            chain = start(act) if who == "scalar" else None
            for part in parts:
                W.next_hi(act, part)
                if who == "scalar":
                    read_out(act, chain, part)

        @block.vector
        def _(dve):
            chain = start(dve) if who == "vector" else None
            for part in parts:
                W.next_lo(dve, part)
                if who == "vector":
                    read_out(dve, chain, part)


def row_products(nc, W, name, first, halves, x, n_tt, evacuate):
    with stage(nc, name) as S:
        acc = S.ps("acc", [P, halves * n_tt, 512])
        block = S.block()

        @block.sync
        def _(sync):
            W.feed(sync, first, 4 * halves)

        @block.tensor
        def _(pe):
            for half in range(halves):
                for k in range(KD):
                    part = 2 * first + KD * half + k
                    W.wait(pe, part)
                    for tt in range(n_tt):
                        last = run_passes(pe, acc[:, half * n_tt + tt, :], W.moving(part, x(k, tt)), k == 0, k == KD - 1)
                    last.then_inc(W.used, 1)

        @block.vector
        def _(dve):
            for k in range(KD * halves):
                W.next_lo(dve, 2 * first + k)

        @block.scalar
        def _(act):
            for half in range(halves):
                for k in range(KD):
                    W.next_hi(act, 2 * first + KD * half + k)
                for tt in range(n_tt):
                    evacuate(act, half, tt, acc[:, half * n_tt + tt, :])


def split_stage(nc, name, src, hi, lo, load=None, pieces=4):
    n = src.shape[1] // pieces
    with stage(nc, name) as S:
        hi_done, loaded = S.sem("hi_done"), S.sem("loaded")
        block = S.block()
        if load is not None:
            @block.sync
            def _(sync):
                sync.dma_start(src, load).then_inc(loaded, 16)

        @block.scalar
        def _(act):
            if load is not None:
                act.wait_ge(loaded, 16)
            for i in range(pieces):
                act.activation(hi[:, i * n:(i + 1) * n], src[:, i * n:(i + 1) * n], ACT.Copy).then_inc(hi_done, 1)

        @block.vector
        def _(dve):
            if load is not None:
                dve.wait_ge(loaded, 16)
            for i in range(pieces):
                dve.wait_ge(hi_done, i + 1)
                dve.tensor_tensor(lo[:, i * n:(i + 1) * n], src[:, i * n:(i + 1) * n],
                                  hi[:, i * n:(i + 1) * n].bitcast(F32), ALU.subtract)


def norm(nc, name, src, dst, K, N, ones, scale, groups=1, post=1.0, shift=None, mul=None, ranges=None, pair=None):
    ranges = ranges or [(0, N, 0)]
    n_chunks = K * groups
    with stage(nc, name) as S:
        sq = S.sb("sq", [P, n_chunks, N])
        root = S.sb("root", [P, groups, N])
        rstd = S.sb("rstd", [P, groups, N])
        total = S.ps("total", [P, groups, N])
        squared, summed, meaned, rooted, ordered, scaled, multiplied, hi_done = (
            S.sem(n) for n in ("squared", "summed", "meaned", "rooted", "ordered", "scaled", "multiplied", "hi_done"))
        value = dst if dst is not None else (lambda c: sq[:, c, :])
        valued = multiplied if mul is not None else scaled
        block = S.block()

        @block.scalar
        def _(act):
            for c in range(n_chunks):
                act.activation(sq[:, c, :], src(c), ACT.Square).then_inc(squared, 1)
            act.wait_ge(meaned, 1)
            act.activation(root[:, :, :], root[:, :, :], ACT.Sqrt).then_inc(rooted, 1)
            if pair is not None:
                for c in range(n_chunks):
                    act.wait_ge(valued, c + 1)
                    for lo, hi, s in ranges:
                        if shift is not None:
                            last = act.activation(pair(c)[0][:, lo:hi], value(c)[:, lo:hi], ACT.Identity, bias=shift(c, s))
                        else:
                            last = act.activation(pair(c)[0][:, lo:hi], value(c)[:, lo:hi], ACT.Copy)
                    last.then_inc(hi_done, 1)

        @block.tensor
        def _(pe):
            for c in range(n_chunks):
                pe.wait_ge(squared, c + 1)
                last = pe.matmul(total[:, c // K, :], ones, sq[:, c, :], start=(c % K == 0), stop=(c % K == K - 1))
            last.then_inc(summed, 1)

        @block.vector
        def _(dve):
            chain = Chain(dve, ordered)
            dve.wait_ge(summed, 1)
            dve.tensor_scalar(root[:, :, :], total[:, :, :], 1.0 / (K * P * post * post), EPS / (post * post),
                              ALU.mult, ALU.add).then_inc(meaned, 1)
            dve.wait_ge(rooted, 1)
            chain(dve.reciprocal(rstd[:, :, :], root[:, :, :]))
            for c in range(n_chunks):
                for lo, hi, s in ranges:
                    last = dve.scalar_tensor_tensor(out=value(c)[:, lo:hi], in0=src(c)[:, lo:hi], scalar=scale(c, s),
                                                    in1=rstd[:, c // K, lo:hi], op0=ALU.mult, op1=ALU.mult)
                last.then_inc(scaled, 1)
            if mul is not None:
                for c in range(n_chunks):
                    dve.wait_ge(scaled, c + 1)
                    dve.tensor_tensor(value(c), value(c), mul(c), ALU.mult).then_inc(multiplied, 1)
            if pair is not None:
                for c in range(n_chunks):
                    dve.wait_ge(hi_done, c + 1)
                    for lo, hi, s in ranges:
                        out, high = pair(c)[1][:, lo:hi], pair(c)[0][:, lo:hi].bitcast(F32)
                        if shift is not None:
                            dve.scalar_tensor_tensor(out=out, in0=value(c)[:, lo:hi], scalar=shift(c, s), in1=high,
                                                     op0=ALU.add, op1=ALU.subtract)
                        else:
                            dve.tensor_tensor(out, value(c)[:, lo:hi], high, ALU.subtract)


class Unit:

    def __init__(self, q, k, v, nk, scale, bias=None, sink=None, weight=None, end=True, first=True, out=None):
        self.q, self.k, self.v, self.nk, self.scale = q, k, v, nk, scale
        self.bias, self.sink, self.weight = bias, sink, weight
        self.first, self.end, self.out = first, end, out


def attention(nc, name, units, ident):
    U = len(units)
    width = max(u.nk for u in units)
    group, groups = [], 0
    for u in units:
        group.append(groups)
        groups += u.end
    with stage(nc, name) as S:
        raw = S.ps("raw", [P, 3, 512])
        turned = S.ps("turned", [P, 2, 512])
        out = S.ps("out", [P, 2, 512])
        biased = S.sb("biased", [P, 3, width])
        prob = S.sb("prob", [P, 3, width])
        probT = S.sb("probT", [P, 2, width])
        low = S.sb("low", [P, 3, 4])
        scored, shifted, exped, normed, transposed, copied, summed, evacuated, v_ordered, a_ordered = (
            S.sem(n) for n in ("scored", "shifted", "exped", "normed", "transposed", "copied", "summed",
                               "evacuated", "v_ordered", "a_ordered"))
        block = S.block()

        @block.tensor
        def _(pe):
            for u in range(U + 2):
                if u < U:
                    x = units[u]
                    if u >= 3:
                        pe.wait_ge(exped, u - 2)
                    pe.matmul(raw[:, u % 3, 0:x.nk], x.q, x.k, start=True, stop=True).then_inc(scored, 1)
                if 1 <= u <= U:
                    w, x = u - 1, units[u - 1]
                    pe.wait_ge(normed, w + 1)
                    if w >= 2:
                        pe.wait_ge(copied, w - 1)
                    for b in range(x.nk // P):
                        last = pe.transpose(turned[:, w % 2, b * P:(b + 1) * P], prob[:, w % 3, b * P:(b + 1) * P], ident)
                    last.then_inc(transposed, 1)
                if u >= 2:
                    w, x = u - 2, units[u - 2]
                    pe.wait_ge(copied, w + 1)
                    if x.first and group[w] >= 2:
                        pe.wait_ge(evacuated, group[w] - 1)
                    nb = x.nk // P
                    for b in range(nb):
                        last = pe.matmul(out[:, group[w] % 2, 0:P], x.v(b), probT[:, w % 2, b * P:(b + 1) * P],
                                         start=(x.first and b == 0), stop=(x.end and b == nb - 1))
                    last.then_inc(summed, 1)

        @block.vector
        def _(dve):
            chain = Chain(dve, v_ordered)
            for u in range(U + 1):
                if u < U:
                    x, i = units[u], u % 3
                    dve.wait_ge(scored, u + 1)
                    if u >= 3:
                        dve.wait_ge(exped, u - 2)
                    src = raw[:, i, 0:x.nk]
                    if x.bias is not None:
                        chain(dve.scalar_tensor_tensor(out=biased[:, i, 0:x.nk], in0=src, scalar=x.scale,
                                                       in1=x.bias, op0=ALU.mult, op1=ALU.add))
                        src = biased[:, i, 0:x.nk]
                    chain(dve.tensor_reduce(low[:, i, 0:1], src, X_AXIS, ALU.max))
                    factor = -1.0 if x.bias is not None else -x.scale
                    if x.sink is None:
                        dve.tensor_scalar(low[:, i, 0:1], low[:, i, 0:1], factor, None, ALU.mult).then_inc(shifted, 1)
                    else:
                        chain(dve.tensor_scalar(low[:, i, 0:1], low[:, i, 0:1], x.sink, factor, ALU.max, ALU.mult))
                        dve.tensor_tensor(low[:, i, 3:4], x.sink, low[:, i, 0:1], ALU.add).then_inc(shifted, 1)
                if u >= 1:
                    w, x, i = u - 1, units[u - 1], (u - 1) % 3
                    dve.wait_ge(exped, w + 1)
                    if x.sink is not None:
                        chain(dve.tensor_tensor(low[:, i, 1:2], low[:, i, 1:2], low[:, i, 3:4], ALU.add))
                    chain(dve.reciprocal(low[:, i, 2:3], low[:, i, 1:2]))
                    if x.weight is None:
                        ins = dve.tensor_scalar(prob[:, i, 0:x.nk], prob[:, i, 0:x.nk], low[:, i, 2:3], None, ALU.mult)
                    else:
                        ins = dve.tensor_scalar(prob[:, i, 0:x.nk], prob[:, i, 0:x.nk], low[:, i, 2:3], x.weight,
                                                ALU.mult, ALU.mult)
                    ins.then_inc(normed, 1)

        @block.scalar
        def _(act):
            chain = Chain(act, a_ordered)
            for u in range(U + 2):
                if u < U:
                    x, i = units[u], u % 3
                    act.wait_ge(shifted, u + 1)
                    if u >= 3:
                        act.wait_ge(transposed, u - 2)
                    src, scale = (raw[:, i, 0:x.nk], x.scale) if x.bias is None else (biased[:, i, 0:x.nk], 1.0)
                    if x.sink is not None:
                        chain(act.activation(low[:, i, 3:4], low[:, i, 3:4], ACT.Exp))
                    act.activation(prob[:, i, 0:x.nk], src, ACT.Exp, bias=low[:, i, 0:1], scale=scale,
                                   accum_out=low[:, i, 1:2]).then_inc(exped, 1)
                if 1 <= u <= U:
                    w, x = u - 1, units[u - 1]
                    act.wait_ge(transposed, w + 1)
                    if w >= 2:
                        act.wait_ge(summed, w - 1)
                    act.activation(probT[:, w % 2, 0:x.nk], turned[:, w % 2, 0:x.nk], ACT.Copy).then_inc(copied, 1)
                if u >= 2 and units[u - 2].end:
                    w = u - 2
                    act.wait_ge(summed, w + 1)
                    lo, hi, dst = units[w].out
                    act.activation(dst, out[lo:hi, group[w] % 2, 0:P], ACT.Copy).then_inc(evacuated, 1)


def feed_forward(nc, W, seg, x, h):
    first = W.take(seg)
    order = [("gate", 0), ("up", 0)]
    for c in range(FC):
        if c + 1 < FC:
            order += [("gate", c + 1), ("up", c + 1)]
        order.append(("down", c))
    end = {key: 2 * (first + i) + 2 for i, key in enumerate(order)}
    with stage(nc, seg) as S:
        acc = S.ps("acc", [P, KD, T])
        gu = S.ps("gu", [P, 2, 2, 512])
        silu = S.sb("silu", [P, 2, T])
        hid = S.sb("hid", [P, T])
        hid_hi = S.sb("hid_hi", [P, 2, T], F32R)
        hid_lo = S.sb("hid_lo", [P, 2, T], F32R)
        silu_done, hidden, ordered = S.sem("silu_done"), S.sem("hidden"), S.sem("ordered")
        block = S.block()

        @block.sync
        def _(sync):
            W.feed(sync, first, 3 * FC)

        @block.tensor
        def _(pe):
            for kind, c in order:
                for part in (end[kind, c] - 2, end[kind, c] - 1):
                    W.wait(pe, part)
                    if kind == "down" and part % 2 == 0:
                        pe.wait_ge(hidden, c + 1)
                    if kind == "gate" and c >= 2 and part % 2 == 0:
                        pe.wait_ge(hidden, c - 1)
                    for i in range(4):
                        n = 4 * (part % 2) + i
                        if kind == "down":
                            last = run_passes(pe, acc[:, n, :],
                                              W.stationary(part, i * P, (hid_hi[:, c % 2, :], hid_lo[:, c % 2, :])),
                                              c == 0 and n % 2 == 0, c == FC - 1, skip_group_check=True)
                        else:
                            j = ("gate", "up").index(kind)
                            last = run_passes(pe, gu[:, c % 2, j, 0:T], W.stationary(part, i * P, x(n)), n == 0, n == KD - 1)
                    last.then_inc(W.used, 1)

        @block.scalar
        def _(act):
            for kind, c in order:
                for part in (end[kind, c] - 2, end[kind, c] - 1):
                    W.next_hi(act, part)
                if kind == "gate":
                    if c >= 2:
                        act.wait_ge(hidden, c - 1)
                    act.activation(silu[:, c % 2, :], gu[:, c % 2, 0, 0:T], ACT.Silu).then_inc(silu_done, 1)

        @block.vector
        def _(dve):
            chain = Chain(dve, ordered)
            for kind, c in order:
                for part in (end[kind, c] - 2, end[kind, c] - 1):
                    W.next_lo(dve, part)
                if kind == "up":
                    dve.wait_ge(W.used, end[kind, c])
                    dve.wait_ge(silu_done, c + 1)
                    chain(dve.tensor_tensor(hid[:, :], silu[:, c % 2, :], gu[:, c % 2, 1, 0:T], ALU.mult))
                    if c >= 2:
                        dve.wait_ge(W.used, end["down", c - 2])
                    chain(dve.tensor_copy(hid_hi[:, c % 2, :], hid[:, :]))
                    dve.tensor_tensor(hid_lo[:, c % 2, :], hid[:, :], hid_hi[:, c % 2, :].bitcast(F32),
                                      ALU.subtract).then_inc(hidden, 1)
                    dve.wait_ge(hidden, c + 1)
            dve.wait_ge(W.used, 2 * (first + 3 * FC))
            for n in range(KD):
                dve.scalar_tensor_tensor(out=h[:, n, 0:T], in0=acc[:, n, :], scalar=0.5, in1=h[:, n, 0:T],
                                         op0=ALU.mult, op1=ALU.add)


def peer_topk(nc, name, scores, route, const):
    ident, iota16 = const[:, 0:P], const[:, 3 * P:3 * P + 16]
    HC = PH * TOPK
    with stage(nc, name) as S:
        rest = S.sb("rest", [P, 2 * PH, NKEYS])
        best = S.sb("best", [P, 2 * PH, TOPK])
        index = S.sb("index", [P, 2 * PH, TOPK], U32)
        indexf = S.sb("indexf", [P, 2 * PH, TOPK])
        cand = S.sb("cand", [P, PH, TOPK * TOPK])
        cand2 = S.sb("cand2", [P, PH, TOPK * TOPK])
        top = S.sb("top", [P, PH, TOPK])
        where = S.sb("where", [P, PH, TOPK], U32)
        part = S.sb("part", [P, 2, HC], U32)
        partf = S.sb("partf", [P, 2, HC])
        hit = S.sb("hit", [P, HC, TOPK])
        total = S.sb("total", [P, PH])
        chosen = S.sb("chosen", [P, 2, 3, HC])
        turned = S.ps("turned", [P, 2, 512])
        ordered, exp_in, exped, ready, transposed = (
            S.sem(n) for n in ("ordered", "exp_in", "exped", "ready", "transposed"))
        block = S.block()

        @block.vector
        def _(dve):
            chain = Chain(dve, ordered)
            for tt in range(2):
                for i in range(2 * PH):
                    last = dve.max(best[:, i, 0:8], scores[:, tt, i, :])
                chain(last)
                for i in range(2 * PH):
                    dve.match_replace(out=rest[:, i, :], in_to_replace=best[:, i, 0:8], in_values=scores[:, tt, i, :],
                                      imm_value=-3e38)
                    last = dve.max_index(index[:, i, 0:8], best[:, i, 0:8], scores[:, tt, i, :])
                chain(last)
                for i in range(2 * PH):
                    last = dve.max(best[:, i, 8:16], rest[:, i, :])
                chain(last)
                for i in range(2 * PH):
                    last = dve.max_index(index[:, i, 8:16], best[:, i, 8:16], rest[:, i, :])
                chain(last)
                dve.tensor_copy(indexf[:, :, :], index[:, :, :])
                halves = best[:, :, :].rearrange("p (h two) a -> p h two a", two=2)
                chain(dve.tensor_tensor(
                    cand[:, :, :].rearrange("p h (a b) -> p h a b", a=TOPK),
                    halves[:, :, 0, :].unsqueeze(3).to_broadcast([P, PH, TOPK, TOPK]),
                    halves[:, :, 1, :].unsqueeze(2).to_broadcast([P, PH, TOPK, TOPK]), ALU.add))
                for h in range(PH):
                    last = dve.max(top[:, h, 0:8], cand[:, h, :])
                chain(last)
                for h in range(PH):
                    dve.match_replace(out=cand2[:, h, :], in_to_replace=top[:, h, 0:8], in_values=cand[:, h, :],
                                      imm_value=-3e38)
                    last = dve.max_index(where[:, h, 0:8], top[:, h, 0:8], cand[:, h, :])
                chain(last)
                for h in range(PH):
                    last = dve.max(top[:, h, 8:16], cand2[:, h, :])
                chain(last)
                for h in range(PH):
                    last = dve.max_index(where[:, h, 8:16], top[:, h, 8:16], cand2[:, h, :])
                chain(last)
                g = chosen[:, tt, 2, :].rearrange("p (h s) -> p h s", h=PH)
                dve.tensor_tensor(g, top[:, :, :], top[:, :, 0:1].to_broadcast([P, PH, TOPK]),
                                  ALU.subtract).then_inc(exp_in, 1)
                flat = where[:, :, :].rearrange("p h s -> p (h s)")
                dve.tensor_scalar(part[:, 0, :], flat, 4, None, ALU.logical_shift_right)
                chain(dve.tensor_scalar(part[:, 1, :], flat, 15, None, ALU.bitwise_and))
                chain(dve.tensor_copy(partf[:, :, :], part[:, :, :]))
                both = indexf[:, :, :].rearrange("p (h two) a -> p h two a", two=2)
                for half in range(2):
                    chain(dve.tensor_tensor(hit[:, :, :], partf[:, half, :].unsqueeze(2).to_broadcast([P, HC, TOPK]),
                                            iota16.unsqueeze(1).to_broadcast([P, HC, TOPK]), ALU.is_equal))
                    hits = hit[:, :, :].rearrange("p (h s) a -> p h s a", h=PH)
                    chain(dve.tensor_tensor(hits, hits, both[:, :, half, :].unsqueeze(2).to_broadcast([P, PH, TOPK, TOPK]),
                                            ALU.mult))
                    chain(dve.tensor_reduce(chosen[:, tt, half, :], hit[:, :, :], X_AXIS, ALU.add))
                dve.wait_ge(exped, tt + 1)
                chain(dve.tensor_reduce(total[:, :], g, X_AXIS, ALU.add))
                chain(dve.reciprocal(total[:, :], total[:, :]))
                dve.tensor_tensor(g, g, total[:, :].unsqueeze(2).to_broadcast([P, PH, TOPK]), ALU.mult).then_inc(ready, 1)
                dve.wait_ge(ready, tt + 1)

        @block.scalar
        def _(act):
            for tt in range(2):
                act.wait_ge(exp_in, tt + 1)
                act.activation(chosen[:, tt, 2, :], chosen[:, tt, 2, :], ACT.Exp).then_inc(exped, 1)
            for tt in range(2):
                act.wait_ge(transposed, tt + 1)
                for j in range(3):
                    act.activation(route[:, j, tt * P:(tt + 1) * P], turned[:, tt, j * P:(j + 1) * P], ACT.Copy)

        @block.tensor
        def _(pe):
            for tt in range(2):
                pe.wait_ge(ready, tt + 1)
                for j in range(3):
                    last = pe.transpose(turned[:, tt, j * P:(j + 1) * P], chosen[:, tt, j, :], ident)
                last.then_inc(transposed, 1)


GROUP = 4


def peer_spread(nc, name, route, G, const):
    iota = const[:, 2 * P:3 * P]
    steps = T // GROUP
    with stage(nc, name) as S:
        cur = S.sb("cur", [P, 2, 3, GROUP])
        first = S.sb("first", [P, 2, GROUP, P])
        second = S.sb("second", [P, 2, GROUP, P])
        product = S.ps("product", [P, 2, GROUP, P])
        picked, onehots, multiplied, stored = (S.sem(n) for n in ("picked", "onehots", "multiplied", "stored"))
        block = S.block()

        @block.scalar
        def _(act):
            for b in range(2):
                act.activation(cur[:, b, :, :], route[:, :, b * GROUP:(b + 1) * GROUP], ACT.Copy).then_inc(picked, 1)

            def store(at, b, done):
                act.wait_ge(multiplied, done)
                act.activation(G[:, :, bass.ds(at, GROUP)], product[:, b, :, :].rearrange("p t j -> p j t"),
                               ACT.Copy).then_inc(stored, 1)

            with act.Fori(0, steps // 2 - 1) as i:
                for b in range(2):
                    store(i * (2 * GROUP) + b * GROUP, b, i * 2 + (b + 1))
                    act.activation(cur[:, b, :, :], route[:, :, bass.ds(i * (2 * GROUP) + (b + 2) * GROUP, GROUP)],
                                   ACT.Copy).then_inc(picked, 1)
            for b in range(2):
                store(T + (b - 2) * GROUP, b, steps - 1 + b)

        @block.vector
        def _(dve):
            with dve.Fori(0, steps // 2) as i:
                for b in range(2):
                    dve.wait_ge(picked, i * 2 + (b + 1))
                    for t in range(GROUP):
                        dve.tensor_scalar(first[:, b, t, :], iota, cur[:, b, 0, t:t + 1], None, ALU.is_equal)
                        last = dve.tensor_scalar(second[:, b, t, :], iota, cur[:, b, 1, t:t + 1], cur[:, b, 2, t:t + 1],
                                                 ALU.is_equal, ALU.mult)
                    last.then_inc(onehots, 1)

        @block.tensor
        def _(pe):
            with pe.Fori(0, steps // 2) as i:
                for b in range(2):
                    pe.wait_ge(onehots, i * 2 + (b + 1))
                    for t in range(GROUP):
                        last = pe.matmul(product[:, b, t, :], first[:, b, t, :], second[:, b, t, :], start=True, stop=True)
                    last.then_inc(multiplied, 1)


def peer_scores(nc, name, q, keys, scores):
    with stage(nc, name) as S:
        acc = S.ps("acc", [P, 4, 512])
        multiplied, evacuated = S.sem("multiplied"), S.sem("evacuated")
        jobs = [(tt, quad) for tt in range(2) for quad in range(PH // 2)]
        block = S.block()

        @block.tensor
        def _(pe):
            for n, (tt, quad) in enumerate(jobs):
                if n >= 4:
                    pe.wait_ge(evacuated, n - 3)
                for j in range(4):
                    i = 4 * quad + j
                    last = pe.matmul(acc[:, n % 4, j * NKEYS:(j + 1) * NKEYS], q[:, i, tt * P:(tt + 1) * P],
                                     keys[:, i, :], start=True, stop=True)
                last.then_inc(multiplied, 1)

        @block.scalar
        def _(act):
            for n, (tt, quad) in enumerate(jobs):
                act.wait_ge(multiplied, n + 1)
                act.activation(scores[:, tt, 4 * quad:4 * quad + 4, :].rearrange("p a k -> p (a k)"), acc[:, n % 4, :],
                               ACT.Copy).then_inc(evacuated, 1)


def peer_experts(nc, W, seg, x, G, h, gate, work):
    first = W.take(seg)
    turns = (NKEYS - 1) // 2
    assert RING == 4 and PARTS == 4
    with stage(nc, seg) as S:
        acc = S.ps("acc", [P, KD, T])
        dot = S.ps("dot", [P, 2, 512])
        coef_hi = S.sb("coef_hi", [P, 2, T], F32R)
        coef_lo = S.sb("coef_lo", [P, 2, T], F32R)
        zero = S.sb("zero", [P, P])
        zero_r = S.sb("zero_r", [P, P], F32R)
        zeroed, dotted, gelued, weighed, high, weighted, finished = (
            S.sem(n) for n in ("zeroed", "dotted", "gelued", "weighed", "high", "weighted", "finished"))
        block = S.block()

        def parts_used(pos, i):
            return i * (2 * RING) + 2 * (first + pos + 1)

        @block.sync
        def _(sync):
            base = tile_bases()[0][seg] * P
            with sync.Fori(0, PEER_TILES // RING - 1) as i:
                for s in range(RING):
                    sync.wait_ge(W.lo_done, parts_used(s, i))
                    sync.dma_start(W.ring[:, (first + s) % RING, :],
                                   W.sources["peer"][bass.ds(i * (RING * P) + (base + (RING + s) * P), P), :]
                                   ).then_inc(W.arrived[(first + s) % RING], 16)
            W.feed(sync, first + PEER_TILES - RING, RING)

        @block.gpsimd
        def _(pool):
            pool.memset(zero[:, :], 0.0).then_inc(zeroed, 1)

        @block.tensor
        def _(pe):
            def dots(pos, i, j):
                for half in range(2):
                    part = 2 * (first + pos) + half
                    pe.wait_ge(W.lo_done, parts_used(pos, i) - 1 + half)
                    for k in range(4):
                        last = run_passes(pe, dot[:, j % 2, 0:T], W.stationary(part, k * P, x(4 * half + k)),
                                          half == 0 and k == 0, half == 1 and k == 3)
                    last.then_inc(W.used, 1)

            def sums(pos, i, j, count):
                pe.wait_ge(weighted, count)
                for half in range(2):
                    part = 2 * (first + pos) + half
                    pe.wait_ge(W.lo_done, parts_used(pos, i) - 1 + half)
                    for n in range(4):
                        last = run_passes(pe, acc[:, 4 * half + n, :],
                                          W.stationary(part, n * P, (coef_hi[:, j % 2, :], coef_lo[:, j % 2, :])),
                                          False, False, skip_group_check=True)
                    last.then_inc(W.used, 1)

            def zeros(start, stop):
                for n in range(KD):
                    last = pe.matmul(acc[:, n, :], zero_r[:, :], x(0)[0], start=start and n % 2 == 0, stop=stop,
                                     skip_group_check=True)
                return last

            pe.wait_ge(zeroed, 2)
            zeros(True, False)
            dots(0, 0, 0)
            with pe.Fori(0, turns) as i:
                for q in range(2):
                    dots(2 * q + 1, i, q + 1)
                    sums(2 * q + 2, i, q, i * 2 + (q + 1))
            for j in range(turns * 2, NKEYS):
                if j + 1 < NKEYS:
                    dots(2 * j + 1, 0, j + 1)
                    sums(2 * j + 2, 0, j, j + 1)
                else:
                    sums(2 * j + 1, 0, j, j + 1)
            zeros(False, True).then_inc(finished, 1)

        @block.scalar
        def _(act):
            def next_parts(pos, i):
                slot = (first + pos + 2) % RING
                act.wait_ge(W.arrived[slot], i * 16 + 16 * ((first + pos + 2) // RING + 1))
                for half in range(2):
                    act.wait_ge(W.used, parts_used(pos, i) - 1 + half)
                    act.activation(W.hi[:, (2 * (first + pos) + half) % PARTS, :],
                                   W.ring[:, slot, half * PART:(half + 1) * PART], ACT.Copy).then_inc(W.hi_done, 1)

            def gelu(b, pos, i):
                act.wait_ge(W.used, parts_used(pos, i))
                act.activation(work[:, b, :], dot[:, b, 0:T], ACT.Gelu).then_inc(gelued, 1)

            next_parts(0, 0)
            gelu(0, 0, 0)
            with act.Fori(0, turns) as i:
                for q in range(2):
                    next_parts(2 * q + 1, i)
                    gelu(1 - q, 2 * q + 1, i)
                    next_parts(2 * q + 2, i)
            for j in range(turns * 2, NKEYS):
                next_parts(2 * j + 1, 0)
                if j + 1 < NKEYS:
                    gelu((j + 1) % 2, 2 * j + 1, 0)
                    next_parts(2 * j + 2, 0)

        @block.vector
        def _(dve):
            def next_parts(pos, i):
                slot = (first + pos + 2) % RING
                for half in range(2):
                    b = (2 * (first + pos) + half) % PARTS
                    dve.wait_ge(W.hi_done, parts_used(pos, i) + 3 + half)
                    dve.tensor_tensor(W.lo[:, b, :], W.ring[:, slot, half * PART:(half + 1) * PART],
                                      W.hi[:, b, :].bitcast(F32), ALU.subtract).then_inc(W.lo_done, 1)

            def weigh(b, j, count):
                dve.wait_ge(gelued, count)
                dve.tensor_tensor(work[:, 2, :], work[:, b, :], G[:, bass.ds(j, 1), :].rearrange("p o t -> p (o t)"),
                                  ALU.mult).then_inc(weighed, 1)
                dve.wait_ge(weighed, count)
                dve.tensor_copy(coef_hi[:, b, :], work[:, 2, :]).then_inc(high, 1)
                dve.wait_ge(high, count)
                dve.tensor_tensor(coef_lo[:, b, :], work[:, 2, :], coef_hi[:, b, :].bitcast(F32),
                                  ALU.subtract).then_inc(weighted, 1)
                dve.wait_ge(weighted, count)

            dve.wait_ge(zeroed, 1)
            dve.tensor_copy(zero_r[:, :], zero[:, :]).then_inc(zeroed, 1)
            next_parts(0, 0)
            weigh(0, 0, 1)
            with dve.Fori(0, turns) as i:
                for q in range(2):
                    next_parts(2 * q + 1, i)
                    weigh(1 - q, i * 2 + (q + 1), i * 2 + (q + 2))
                    next_parts(2 * q + 2, i)
            for j in range(turns * 2, NKEYS):
                next_parts(2 * j + 1, 0)
                if j + 1 < NKEYS:
                    weigh((j + 1) % 2, j + 1, j + 2)
                    next_parts(2 * j + 2, 0)
            dve.wait_ge(finished, 1)
            for n in range(KD):
                dve.scalar_tensor_tensor(out=h[:, n, :], in0=acc[:, n, :], scalar=gate(n), in1=h[:, n, :],
                                         op0=ALU.mult, op1=ALU.add)


def peer(nc, W, layer, stream, h, scale, shift, gate, const, dram):
    name = "peer%d%d" % (layer, stream)
    with nc.sbuf_tensor(name + "_xh", [P, KD, T], F32R) as x_hi, nc.sbuf_tensor(name + "_xl", [P, KD, T], F32R) as x_lo, \
            nc.sbuf_tensor(name + "_route", [P, 3, T], F32) as route:
        x = split_pair(x_hi, x_lo)
        norm(nc, name + "n", lambda c: h[:, c, :], None, KD, T, const[:, P:2 * P],
             lambda c, s: scale(c), shift=lambda c, s: shift(c), pair=x)
        with nc.sbuf_tensor(name + "_s", [P, 2, 2 * PH, NKEYS], F32) as scores:
            with nc.sbuf_tensor(name + "_q", [P, 2 * PH, T], F32) as q, \
                    nc.sbuf_tensor(name + "_keys", [P, 2 * PH, NKEYS], F32) as keys:
                first = W.take("peer_q%d" % layer)
                products(nc, W, name + "q", first, 16, column_jobs(W, first, 16, KD, T, x),
                         lambda eng, chain, c, ps: eng.activation(q[:, c, :], ps[:, 0:T], ACT.Copy), "scalar",
                         const_load=[(keys[:, :, :].rearrange("p i k -> p (i k)"), dram["subkeys%d" % layer])])
                peer_scores(nc, name + "s", q, keys, scores)
            peer_topk(nc, name + "t", scores, route, const)
        with nc.sbuf_tensor(name + "_G", [P, NKEYS, T], F32) as G:
            peer_spread(nc, name + "g", route, G, const)
            peer_experts(nc, W, "experts%d" % layer, x, G, h, gate, route)


def even_mixer(nc, W, h, modulation, scales, cols, const, rope_dram):
    TT = 2 * T
    ones, ident = const[:, P:2 * P], const[:, 0:P]
    streams = [(0, T, LAT), (T, TT, CTX)]
    with ExitStack() as ctx:
        def sb(name, shape):
            return ctx.enter_context(nc.sbuf_tensor("even_" + name, shape, F32))

        mix = sb("mix", [P, KD, TT])
        with ExitStack() as inner:
            def tmp_sb(name, shape, dt=F32):
                return inner.enter_context(nc.sbuf_tensor("even_" + name, shape, dt))

            pq = tmp_sb("pq", [P, 2, TT])
            pkv = tmp_sb("pkv", [P, TT])
            kr = tmp_sb("kr", [P, TT])
            rope = tmp_sb("rope", [P, TT])
            with nc.sbuf_tensor("even_xh", [P, KD, TT], F32R) as x_hi, nc.sbuf_tensor("even_xl", [P, KD, TT], F32R) as x_lo:
                x = split_pair(x_hi, x_lo)
                norm(nc, "even_n", lambda c: h[:, c, :], None, KD, TT, ones,
                     lambda c, s: scales[:, 0, 0, s, c:c + 1], ranges=streams,
                     shift=lambda c, s: modulation[:, 0, c, s:s + 1], pair=x)
                first = W.take("even_in")
                with nc.sbuf_tensor("even_c", [P, TT], F32) as c_gate, nc.sbuf_tensor("even_z", [P, 2, T + 2], F32) as z, \
                        nc.sbuf_tensor("even_y", [P, 2, T], F32) as y, nc.sbuf_tensor("even_t", [P, TT], F32) as turn:
                    def prepare(dve, chain):
                        chain(dve.memset(z[:, :, :], 0.0))

                    def evacuate(dve, chain, c, ps):
                        if c < 2:
                            return dve.tensor_copy(pq[:, c, :], ps)
                        if c == 2:
                            return dve.tensor_copy(pkv[:, :], ps)
                        if c == 3:
                            chain(dve.tensor_tensor(turn[64:96, :], ps[96:128, :], rope[96:128, :], ALU.mult))
                            chain(dve.tensor_tensor(kr[64:96, :], ps[64:96, :], rope[64:96, :], ALU.mult))
                            return dve.tensor_tensor(kr[64:96, :], kr[64:96, :], turn[64:96, :], ALU.add)
                        j, kind = (c - 4) // 3, (c - 4) % 3
                        two = ps.rearrange("p (s t) -> p s t", s=2)
                        if kind == 0:
                            return dve.tensor_copy(c_gate[:, :], ps)
                        if kind == 1:
                            dve.wait_ge(*done_before(c))
                            return dve.tensor_tensor(z[:, :, 1:T + 1], two,
                                                     c_gate[:, :].rearrange("p (s t) -> p s t", s=2), ALU.mult)

                        def tap(i):
                            at = col_at("conv") + 4 * i + j
                            return cols[:, at:at + 1]

                        dve.wait_ge(*done_before(c))
                        chain(dve.tensor_scalar(y[:, :, :], z[:, :, 0:T], tap(0), None, ALU.mult))
                        for i in (1, 2):
                            chain(dve.scalar_tensor_tensor(out=y[:, :, :], in0=z[:, :, i:T + i], scalar=tap(i),
                                                           in1=y[:, :, :], op0=ALU.mult, op1=ALU.add))
                        return dve.tensor_tensor(mix[:, 4 + j, :].rearrange("p (s t) -> p s t", s=2), two, y[:, :, :],
                                                 ALU.mult)

                    done = []

                    def done_before(c):
                        return done[0], c

                    products(nc, W, "even_in", first, 16, column_jobs(W, first, 16, KD, TT, x),
                             evacuate, "vector", prepare=prepare, const_load=[(rope[:, :], rope_dram)],
                             evacuated_out=done)

            q = tmp_sb("q", [P, MLA_HEADS, TT])
            k = tmp_sb("k", [P, MLA_HEADS, TT])
            v = tmp_sb("v", [P, 4, 512])
            q_hi, q_lo = (tmp_sb("q_" + n, [P, 2, TT], F32R) for n in ("hi", "lo"))
            kv_hi, kv_lo = (tmp_sb("kv_" + n, [P, TT], F32R) for n in ("hi", "lo"))
            at = col_at("q_norm")
            norm(nc, "even_qn", lambda c: pq[:, c, :], None, 2, TT, ones,
                 lambda c, s: cols[:, at + c:at + c + 1], pair=split_pair(q_hi, q_lo))
            at_kv = col_at("kv_norm")
            norm(nc, "even_kvn", lambda c: pkv[:, :], None, 1, TT, ones,
                 lambda c, s: cols[:, at_kv:at_kv + 1], pair=lambda c: (kv_hi[:, :], kv_lo[:, :]))
            first = W.take("uq")
            with nc.sbuf_tensor("even_t2", [P, 2, TT], F32) as turn:
                def rotate(dve, chain, c, ps):
                    chain(dve.tensor_tensor(turn[64:96, c % 2, :], ps[96:128, :], rope[96:128, :], ALU.mult))
                    chain(dve.tensor_tensor(q[64:96, c, :], ps[64:96, :], rope[64:96, :], ALU.mult))
                    dve.tensor_copy(q[0:64, c, :], ps[0:64, :])
                    return dve.tensor_tensor(q[64:96, c, :], q[64:96, c, :], turn[64:96, c % 2, :], ALU.add)

                products(nc, W, "even_uq", first, 2, column_jobs(W, first, MLA_HEADS, 2, TT, split_pair(q_hi, q_lo)),
                         rotate, "vector")
            first = W.take("ukv")
            jobs = [Job([((0, TT), 2 * first, W.stationary(2 * first, j * P, (kv_hi[:, :], kv_lo[:, :])), True, True)])
                    for j in range(MLA_HEADS // 2)]
            for tt in range(4):
                tok = slice(tt * P, (tt + 1) * P)
                jobs.append(Job([((0, 512), 2 * first + 1, W.moving(2 * first + 1, (kv_hi[:, tok], kv_lo[:, tok])),
                                  True, True)]))

            def keys_values(dve, chain, c, ps):
                if c >= MLA_HEADS // 2:
                    return dve.tensor_copy(v[:, c - MLA_HEADS // 2, :], ps)
                for head in (2 * c, 2 * c + 1):
                    dve.tensor_copy(k[64:96, head, :], kr[64:96, :])
                dve.tensor_copy(k[0:64, 2 * c, :], ps[0:64, :])
                return dve.tensor_copy(k[0:64, 2 * c + 1, :], ps[64:128, :])

            products(nc, W, "even_ukv", first, 1, jobs, keys_values, "vector")
            units = []
            for head in range(MLA_HEADS):
                for tt in range(4):
                    lo = 0 if tt < 2 else 2
                    units.append(Unit(
                        q[0:96, head, tt * P:(tt + 1) * P], k[0:96, head, lo * P:TT],
                        lambda b, head=head, lo=lo: v[:, lo + b, (head // 2) * P:(head // 2 + 1) * P],
                        (4 - lo) * P, MLA_SCALE,
                        out=(64 * (head % 2), 64 * (head % 2) + 64,
                             mix[64 * (head % 2):64 * (head % 2) + 64, head // 2, tt * P:(tt + 1) * P])))
            attention(nc, "mla", units, ident)
        first = W.take("even_out")

        def residual(dve, chain, c, ps):
            for lo, hi, s in streams:
                last = dve.scalar_tensor_tensor(out=h[:, c, lo:hi], in0=ps[:, lo:hi], scalar=modulation[:, 0, 16 + c, s:s + 1],
                                                in1=h[:, c, lo:hi], op0=ALU.mult, op1=ALU.add)
            return last

        with nc.sbuf_tensor("mix_hi", [P, KD, TT], F32R) as mix_hi, nc.sbuf_tensor("mix_lo", [P, KD, TT], F32R) as mix_lo:
            split_stage(nc, "mix", *(b[:, :, :].rearrange("p k t -> p (k t)") for b in (mix, mix_hi, mix_lo)))
            products(nc, W, "even_out", first, 8, column_jobs(W, first, 8, KD, TT, split_pair(mix_hi, mix_lo)),
                     residual, "vector")


def mlstm(nc, name, gx, q, k, v, out, const, sel_dram, mask_dram):
    TT = 2 * T
    ident = const[:, 0:P]
    with stage(nc, name) as S:
        F = S.sb("F", [P, TT])
        r = S.sb("r", [P, TT])
        M = S.sb("M", [P, TT])
        neg_m = S.sb("neg_m", [P, TT])
        sel = S.sb("sel", [P, ML_HEADS, P])
        mask = S.sb("mask", [P, 2, 2, T])
        colM = S.sb("colM", [P, 2, P])
        guard = S.sb("guard", [P, 2, P])
        s_sb = S.sb("scores", [P, TT])
        w = S.sb("w", [P, 2, TT])
        sc = S.sb("sc", [P, 2, TT])
        den = S.sb("den", [P, 2, 2])
        scT = S.sb("scT", [P, 4, P])
        raw = S.ps("raw", [P, TT])
        row = S.ps("row", [P, 2, TT])
        turned = S.ps("turned", [P, 2, 512])
        o = S.ps("o", [P, 2, 512])
        (loaded, rows_ready, cols_done, guarded, scored, scores_out, row_done, shifted, exped, masked, combined,
         transposed, copied, summed, evacuated, ordered, cols_out) = (
            S.sem(n) for n in ("loaded", "rows_ready", "cols_done", "guarded", "scored", "scores_out", "row_done",
                               "shifted", "exped", "masked", "combined", "transposed", "copied", "summed",
                               "evacuated", "ordered", "cols_out"))
        steps = [(head, tt) for head in range(ML_HEADS) for tt in range(2)]
        lanes = (slice(32, 36), slice(96, 100))
        block = S.block()

        @block.sync
        def _(sync):
            sync.dma_start(sel[:, :, :].rearrange("p h m -> p (h m)"), sel_dram).then_inc(loaded, 16)
            sync.dma_start(mask[:, :, :, :].rearrange("p a b t -> p (a b t)"), mask_dram).then_inc(loaded, 16)

        @block.gpsimd
        def _(pool):
            pool.wait_ge(loaded, 32)
            for n, (head, tt) in enumerate(steps):
                for d in range(2):
                    pool.wait_ge(exped, 2 * n + d + 1)
                    pool.tensor_tensor(w[:, d, 0:T], w[:, d, 0:T], mask[:, d, tt, :], ALU.mult).then_inc(masked, 1)

        @block.vector
        def _(dve):
            chain = Chain(dve, ordered)
            for buf in (F, r, M):
                last = dve.memset(buf[:, :], 0.0)
            chain(last)
            for d, lane in enumerate(lanes):
                src = slice(64 * d, 64 * d + 4)
                dve.tensor_copy(r[lane, :], gx[src, :])
                if d == 0:
                    one, two = slice(T, TT), slice(0, T)
                    ends = (TT - 1, T - 1)
                else:
                    one, two = slice(TT - 1, T - 1, -1), slice(T - 1, None, -1)
                    ends = (T, 0)
                chain(dve.tensor_tensor_scan(F[lane, one], gx[lane, one], gx[lane, one], 0.0, ALU.add, ALU.bypass))
                chain(dve.tensor_tensor_scan(F[lane, two], gx[lane, two], gx[lane, two],
                                             F[lane, ends[0]:ends[0] + 1], ALU.add, ALU.bypass))
                chain(dve.tensor_tensor(r[lane, :], r[lane, :], F[lane, :], ALU.subtract))
                chain(dve.tensor_tensor_scan(M[lane, one], r[lane, one], r[lane, one], 0.0, ALU.max, ALU.bypass))
                chain(dve.tensor_tensor_scan(M[lane, two], r[lane, two], r[lane, two],
                                             M[lane, ends[0]:ends[0] + 1], ALU.max, ALU.bypass))
            dve.scalar_tensor_tensor(out=neg_m[:, :], in0=F[:, :], scalar=-1.0, in1=M[:, :],
                                     op0=ALU.mult, op1=ALU.subtract).then_inc(rows_ready, 1)
            dve.wait_ge(cols_done, 1)
            dve.tensor_copy(colM[:, :, :], turned[:, 0, 0:2 * P].rearrange("p (a b) -> p a b", a=2)).then_inc(cols_out, 1)
            dve.wait_ge(cols_out, 1)
            dve.wait_ge(guarded, 1)
            for n, (head, tt) in enumerate(steps):
                for d in range(2):
                    lane = 32 + 64 * d + head
                    dve.wait_ge(row_done, 2 * n + d + 1)
                    if n:
                        dve.wait_ge(combined, n)
                    dve.tensor_scalar(w[:, d, :], row[:, d, :], colM[:, tt, lane:lane + 1], 0.0,
                                      ALU.subtract, ALU.min).then_inc(shifted, 1)
                if n >= 1:
                    dve.wait_ge(transposed, n)
                dve.wait_ge(scores_out, n + 1)
                for d in range(2):
                    lane = 32 + 64 * d + head
                    dve.wait_ge(masked, 2 * n + d + 1)
                    chain(dve.tensor_tensor_reduce(sc[:, d, :], w[:, d, :], s_sb[:, :], 1.0, 0.0, ALU.mult, ALU.add,
                                                   den[:, d, 0:1]))
                    chain(dve.tensor_scalar(den[:, d, 1:2], den[:, d, 0:1], -1.0, den[:, d, 0:1], ALU.mult, ALU.max))
                    chain(dve.tensor_tensor(den[:, d, 1:2], den[:, d, 1:2], guard[:, tt, lane:lane + 1], ALU.max))
                    chain(dve.reciprocal(den[:, d, 1:2], den[:, d, 1:2]))
                chain(dve.tensor_scalar(sc[:, 0, :], sc[:, 0, :], den[:, 0, 1:2], None, ALU.mult))
                dve.scalar_tensor_tensor(out=sc[:, 1, :], in0=sc[:, 1, :], scalar=den[:, 1, 1:2], in1=sc[:, 0, :],
                                         op0=ALU.mult, op1=ALU.add).then_inc(combined, 1)

        @block.tensor
        def _(pe):
            pe.wait_ge(rows_ready, 1)
            for tt in range(2):
                pe.transpose(turned[:, 0, tt * P:(tt + 1) * P], M[:, tt * P:(tt + 1) * P], ident)
                last = pe.transpose(turned[:, 1, tt * P:(tt + 1) * P], neg_m[:, tt * P:(tt + 1) * P], ident)
            last.then_inc(cols_done, 1)
            pe.wait_ge(loaded, 32)

            def score(n):
                head, tt = steps[n]
                if n:
                    pe.wait_ge(scores_out, n)
                pe.matmul(raw[:, :], q[:, head, tt * P:(tt + 1) * P], k[:, head, :], start=True, stop=True).then_inc(scored, 1)
                for d, lane in enumerate(lanes):
                    if n:
                        pe.wait_ge(shifted, 2 * (n - 1) + d + 1)
                    pe.matmul(row[:, d, :], sel[lane, head, :], r[lane, :], start=True, stop=True,
                              tile_position=(lane.start, 0)).then_inc(row_done, 1)

            score(0)
            for n, (head, tt) in enumerate(steps):
                if n + 1 < len(steps):
                    score(n + 1)
                pe.wait_ge(combined, n + 1)
                if n == 0:
                    pe.wait_ge(cols_out, 1)
                    pe.wait_ge(guarded, 1)
                if n >= 2:
                    pe.wait_ge(copied, n - 1)
                for b in range(4):
                    last = pe.transpose(turned[:, n % 2, b * P:(b + 1) * P], sc[:, 1, b * P:(b + 1) * P], ident)
                last.then_inc(transposed, 1)
                pe.wait_ge(copied, n + 1)
                if n >= 2:
                    pe.wait_ge(evacuated, n - 1)
                for c in range(2):
                    for b in range(4):
                        at = head * ML_DV + c * P
                        last = pe.matmul(o[:, n % 2, c * P:(c + 1) * P], v[:, b, at:at + P], scT[:, b, :],
                                         start=(b == 0), stop=(b == 3))
                last.then_inc(summed, 1)

        @block.scalar
        def _(act):
            act.wait_ge(cols_done, 1)
            act.activation(guard[:, :, :], turned[:, 1, 0:2 * P].rearrange("p (a b) -> p a b", a=2),
                           ACT.Exp).then_inc(guarded, 1)
            for n, (head, tt) in enumerate(steps):
                act.wait_ge(scored, n + 1)
                if n:
                    act.wait_ge(combined, n)
                act.activation(s_sb[:, :], raw[:, :], ACT.Copy, scale=ML_SCALE).then_inc(scores_out, 1)
                for d in range(2):
                    act.wait_ge(shifted, 2 * n + d + 1)
                    act.activation(w[:, d, :], w[:, d, :], ACT.Exp).then_inc(exped, 1)
                act.wait_ge(transposed, n + 1)
                if n:
                    act.wait_ge(summed, n)
                act.activation(scT[:, :, :].rearrange("p b t -> p (b t)"), turned[:, n % 2, :], ACT.Copy).then_inc(copied, 1)
                act.wait_ge(summed, n + 1)
                act.activation(out[:, 2 * head:2 * head + 2, tt * P:(tt + 1) * P],
                               o[:, n % 2, 0:2 * P].rearrange("p (c t) -> p c t", c=2), ACT.Copy).then_inc(evacuated, 1)


def log_forget(nc, name, gx):
    with stage(nc, name) as S:
        e = S.sb("e", [P, 2 * T])
        mn = S.sb("mn", [P, 2 * T])
        exped, plus, ln_done = S.sem("exped"), S.sem("plus"), S.sem("ln_done")
        a_ordered = S.sem("a_ordered")
        block = S.block()

        @block.scalar
        def _(act):
            chain = Chain(act, a_ordered)
            chain(act.activation(e[:, :], gx[:, :], ACT.Abs))
            act.activation(e[:, :], e[:, :], ACT.Exp, scale=-1.0).then_inc(exped, 1)
            act.wait_ge(plus, 1)
            act.activation(e[:, :], e[:, :], ACT.Ln).then_inc(ln_done, 1)

        @block.vector
        def _(dve):
            dve.wait_ge(exped, 1)
            dve.tensor_scalar(mn[:, :], gx[:, :], 0.0, None, ALU.min)
            dve.tensor_scalar(e[:, :], e[:, :], 1.0, None, ALU.add).then_inc(plus, 1)
            dve.wait_ge(plus, 1)
            dve.wait_ge(ln_done, 1)
            for lo in (32, 96):
                dve.tensor_tensor(gx[lo:lo + 4, :], mn[lo:lo + 4, :], e[lo:lo + 4, :], ALU.subtract)


def odd_mixer(nc, W, h, modulation, scales, cols, const, sel_dram, mask_dram):
    TT = 2 * T
    ones = const[:, P:2 * P]
    with ExitStack() as ctx:
        def sb(name, shape):
            return ctx.enter_context(nc.sbuf_tensor("odd_" + name, shape, F32))

        gate = sb("gate", [P, KD, T])
        y = sb("y", [P, KD, T])
        y_hi, y_lo = (ctx.enter_context(nc.sbuf_tensor("odd_y_" + n, [P, KD, T], F32R)) for n in ("hi", "lo"))
        with ExitStack() as inner:
            def tmp_sb(name, shape):
                return inner.enter_context(nc.sbuf_tensor("odd_" + name, shape, F32))

            x_hi, x_lo = (inner.enter_context(nc.sbuf_tensor("odd_x_" + n, [P, KD, TT], F32R)) for n in ("hi", "lo"))
            x = split_pair(x_hi, x_lo)
            q = tmp_sb("q", [P, ML_HEADS, T])
            k = tmp_sb("k", [P, ML_HEADS, TT])
            v = tmp_sb("v", [P, 4, 1024])
            gx = tmp_sb("gx", [P, TT])
            norm(nc, "odd_n", lambda c: h[:, c, :], None, KD, TT, ones,
                 lambda c, s: scales[:, 1, 0, s, c:c + 1], ranges=[(0, T, LAT), (T, TT, CTX)],
                 shift=lambda c, s: modulation[:, 1, c, s:s + 1], pair=x)
            x_lat = split_pair(x_hi[:, :, 0:T], x_lo[:, :, 0:T])
            first = W.take("odd_qk")
            at = col_at("gate_b")

            def heads(act, chain, c, ps):
                if c < 4:
                    return act.activation(q[:, c, :], ps[:, 0:T], ACT.Copy)
                if c < 8:
                    return act.activation(k[:, c - 4, :], ps[:, :], ACT.Copy)
                return act.activation(gx[:, :], ps[:, :], ACT.Identity, bias=cols[:, at:at + 1])

            jobs = column_jobs(W, first, 4, KD, T, x_lat)
            jobs += column_jobs(W, first + 4, 5, KD, TT, x)
            products(nc, W, "odd_qk", first, 9, jobs, heads, "scalar")
            log_forget(nc, "odd_lf", gx)
            first = W.take("odd_v")
            row_products(nc, W, "odd_v", first, 2, lambda kk, tt: (x_hi[:, kk, tt * P:(tt + 1) * P], x_lo[:, kk, tt * P:(tt + 1) * P]), 4,
                         lambda act, half, tt, ps: act.activation(v[:, tt, half * 512:(half + 1) * 512], ps, ACT.Copy))
            first = W.take("odd_gate")
            products(nc, W, "odd_g", first, 8, column_jobs(W, first, 8, KD, T, x_lat),
                     lambda act, chain, c, ps: act.activation(gate[:, c, :], ps[:, 0:T], ACT.Sigmoid), "scalar")
            mlstm(nc, "mlstm", gx, q, k, v, y, const, sel_dram, mask_dram)
        at_g = col_at("head_g")
        norm(nc, "odd_hn", lambda c: y[:, c, :], None, 2, T, ones,
             lambda c, s: cols[:, at_g + c:at_g + c + 1], groups=ML_HEADS, mul=lambda c: gate[:, c, :],
             pair=split_pair(y_hi, y_lo))
        first = W.take("odd_out")
        products(nc, W, "odd_out", first, 8, column_jobs(W, first, 8, KD, T, split_pair(y_hi, y_lo)),
                 lambda dve, chain, c, ps: dve.scalar_tensor_tensor(
                     out=h[:, c, 0:T], in0=ps[:, 0:T], scalar=modulation[:, 1, 16 + c, LAT:LAT + 1],
                     in1=h[:, c, 0:T], op0=ALU.mult, op1=ALU.add), "vector")


def modulation_stage(nc, W, h, modulation, scales, cols, const, dram):
    first = W.take("mod")
    blocks = 24
    with stage(nc, "mod") as S:
        c_in = S.sb("c", [P, KD, 2])
        c_act = S.sb("c_act", [P, KD, 2])
        zero = S.sb("zero", [P, KD, P])
        c_hi = S.sb("c_hi", [P, KD, P], F32R)
        c_lo = S.sb("c_lo", [P, KD, P], F32R)
        row = S.sb("row", [2, 2, 512])
        acc = S.ps("acc", [P, 2, 512])
        turned = S.ps("turned", [P, 2 * 96])
        loaded, silu_done, ordered, h_loaded, c_split, row_out, turned_done, zeroed = (
            S.sem(n) for n in ("loaded", "silu_done", "ordered", "h_loaded", "c_split", "row_out", "turned_done", "zeroed"))
        block = S.block()

        @block.sync
        def _(sync):
            W.prime(sync)
            W.feed(sync, first, 96)

        @block.scalar
        def _(act):
            act.dma_start(c_in[:, :, :].rearrange("p k s -> p (k s)"), dram["c_cols"]).then_inc(loaded, 16)
            act.dma_start(cols[:, :], dram["cols"]).then_inc(loaded, 16)
            act.dma_start(const[:, :], dram["const"]).then_inc(loaded, 16)
            act.dma_start(h[:, :, :].rearrange("p k t -> p (k t)"), dram["tokens"]).then_inc(h_loaded, 16)
            act.wait_ge(loaded, 48)
            act.activation(c_act[:, :, :], c_in[:, :, :], ACT.Silu).then_inc(silu_done, 1)
            for part in range(PARTS):
                W.write_hi(act, part)
            for b in range(blocks):
                for k in range(KD):
                    W.next_hi(act, 2 * first + KD * b + k)
                if b >= 2:
                    act.wait_ge(turned_done, b - 1)
                act.activation(row[:, b % 2, :], acc[0:2, b % 2, :], ACT.Copy).then_inc(row_out, 1)
            act.wait_ge(h_loaded, 16)

        @block.gpsimd
        def _(pool):
            pool.memset(zero[:, :, :], 0.0).then_inc(zeroed, 1)

        @block.tensor
        def _(pe):
            pe.wait_ge(c_split, 1)

            def turn(b):
                pe.wait_ge(row_out, b + 1)
                for j in range(4):
                    at = 2 * (4 * b + j)
                    last = pe.transpose(turned[:, at:at + 2], row[:, b % 2, j * P:(j + 1) * P], const[0:2, 0:2])
                last.then_inc(turned_done, 1)

            for b in range(blocks):
                if b >= 2:
                    pe.wait_ge(row_out, b - 1)
                for k in range(KD):
                    part = 2 * first + KD * b + k
                    W.wait(pe, part)
                    run_passes(pe, acc[:, b % 2, :], W.moving(part, (c_hi[:, k, :], c_lo[:, k, :])), k == 0,
                               k == KD - 1).then_inc(W.used, 1)
                if b >= 1:
                    turn(b - 1)
            turn(blocks - 1)

        @block.vector
        def _(dve):
            chain = Chain(dve, ordered)
            dve.wait_ge(loaded, 48)
            dve.wait_ge(zeroed, 1)
            dve.tensor_copy(c_hi[:, :, :], zero[:, :, :])
            chain(dve.tensor_copy(c_lo[:, :, :], zero[:, :, :]))
            dve.wait_ge(silu_done, 1)
            chain(dve.tensor_copy(c_hi[:, :, 0:2], c_act[:, :, :]))
            dve.tensor_tensor(c_lo[:, :, 0:2], c_act[:, :, :], c_hi[:, :, 0:2].bitcast(F32), ALU.subtract).then_inc(c_split, 1)
            for part in range(PARTS):
                W.write_lo(dve, part)
            for part in range(2 * 96):
                W.next_lo(dve, 2 * first + part)
            dve.wait_ge(turned_done, blocks)
            at = col_at("b_mod")
            chain(dve.tensor_tensor(modulation[:, :, :, :], turned[:, :].rearrange("p (l c s) -> p l c s", l=2, s=2),
                                    cols[:, at:at + 96].rearrange("p (l c) -> p l c", l=2).unsqueeze(3)
                                    .to_broadcast([P, 2, 48, 2]), ALU.add))
            for layer in range(2):
                for n in range(2):
                    at = col_at("norm%d" % (n + 1)) + 8 * layer
                    for s in range(2):
                        lo = 8 + 24 * n
                        dve.scalar_tensor_tensor(out=scales[:, layer, n, s, :], in0=modulation[:, layer, lo:lo + 8, s],
                                                 scalar=1.0, in1=cols[:, at:at + 8], op0=ALU.add, op1=ALU.mult)


C_HEAD0, B_HEAD0 = 12, 4


def bias_stage(nc, bias, cmp_bias, neg_lam, cols, dram):
    PER = 16
    with stage(nc, "bias") as S:
        onehot = S.sb("onehot", [34, 4 * P])
        table = S.sb("table", [34, N_BIAS])
        acc = S.ps("acc", [P, 4, 512])
        prod = S.sb("prod", [P, 2, 2, 64])
        dots = S.sb("dots", [P, 2, 2])
        loaded, cols_loaded, filled, copied, ordered, dotted, exped = (
            S.sem(n) for n in ("loaded", "cols_loaded", "filled", "copied", "ordered", "dotted", "exped"))
        rounds = T // PER
        block = S.block()

        @block.sync
        def _(sync):
            sync.dma_start(onehot[:, :], dram["onehot"]).then_inc(loaded, 16)
            sync.dma_start(table[0:32, :], dram["rel_bias"]).then_inc(loaded, 16)
            sync.dma_start(table[32:34, :], dram["masked"]).then_inc(loaded, 16)
            sync.dma_start(cols[:, :], dram["cols2"]).then_inc(cols_loaded, 16)

        @block.tensor
        def _(pe):
            pe.wait_ge(loaded, 48)
            for r in range(rounds + 2):
                if r >= 4:
                    pe.wait_ge(copied, r - 3)
                for j in range(PER if r < rounds else N_CMP):
                    x0 = 384 - (r * PER + j) if r < rounds else 225 + P * (r - rounds) - 16 * j
                    last = pe.matmul(acc[:, r % 4, j * N_BIAS:(j + 1) * N_BIAS], onehot[:, x0:x0 + P], table[:, :],
                                     start=True, stop=True)
                last.then_inc(filled, 1)

        @block.scalar
        def _(act):
            for r in range(rounds):
                act.wait_ge(filled, r + 1)
                act.activation(bias[:, :, r * PER:(r + 1) * PER],
                               acc[:, r % 4, 0:PER * N_BIAS].rearrange("p (c h) -> p h c", h=N_BIAS),
                               ACT.Copy).then_inc(copied, 1)
            act.wait_ge(ordered, 1)
            for tt in range(2):
                act.wait_ge(filled, rounds + tt + 1)
                act.activation(cmp_bias[:, tt, :, 0:N_CMP],
                               acc[:, (rounds + tt) % 4, 0:N_CMP * N_BIAS].rearrange("p (c h) -> p h c", h=N_BIAS)
                               [:, B_HEAD0:B_HEAD0 + 8, :], ACT.Copy).then_inc(copied, 1)
            act.wait_ge(dotted, 1)
            act.activation(dots[:, :, :], dots[:, :, :], ACT.Exp).then_inc(exped, 1)

        @block.vector
        def _(dve):
            chain = Chain(dve, ordered)
            chain(dve.memset(cmp_bias[:, :, :, :], NEG))
            dve.wait_ge(cols_loaded, 16)
            at = col_at("lam")
            lam = cols[:, at:at + 512].rearrange("p (l a b d) -> p l a b d", l=2, a=2, b=2)
            for layer in range(2):
                last = dve.tensor_tensor(prod[:, layer, :, :], lam[:, layer, :, 0, :], lam[:, layer, :, 1, :], ALU.mult)
            chain(last)
            dve.tensor_reduce(dots[:, :, :], prod[:, :, :, :], X_AXIS, ALU.add).then_inc(dotted, 1)
            dve.wait_ge(exped, 1)
            for layer in range(2):
                init = 0.8 - 0.6 * math.exp(-0.3 * layer)
                dve.tensor_scalar(neg_lam[:, layer:layer + 1], dots[:, layer, 1:2], dots[:, layer, 0:1], -init,
                                  ALU.subtract, ALU.add)


def compress_stage(nc, W, layer, X, kc, vc, const):
    first = W.take("cmp%d" % layer)
    N = 3 * 16
    hid_hi_name = "cmp%d_hid" % layer
    with nc.sbuf_tensor(hid_hi_name, [P, 4, 2 * 16], F32) as hid, \
            nc.sbuf_tensor(hid_hi_name + "h", [P, 4, 2 * 16], F32R) as hid_hi, \
            nc.sbuf_tensor(hid_hi_name + "l", [P, 4, 2 * 16], F32R) as hid_lo, \
            nc.sbuf_tensor(hid_hi_name + "p", [P, 4], F32) as pos_sum:
        jobs = []
        for kv in range(2):
            for hc in range(2):
                jobs.append([])
            for pp in range(16):
                part = 2 * first + 8 * kv + pp // 2
                x = [b[:, :, 2 * pp:2 * pp + 16 * 15 + 1:16] for b in X(kv)]
                for hc in range(2):
                    jobs[2 * kv + hc].append((part, W.stationary(part, (pp % 2) * 256 + hc * P, x)))
        with stage(nc, "cmp1") as S:
            acc = S.ps("acc", [P, 4, 512])
            pos_out, geluv, hi_done = S.sem("pos_out"), S.sem("gelu"), S.sem("hi_done")
            block = S.block()

            @block.sync
            def _(sync):
                W.feed(sync, first, 8)

            @block.tensor
            def _(pe):
                for kv in range(2):
                    for pp in range(16):
                        for hc in range(2):
                            part, passes = jobs[2 * kv + hc][pp]
                            if pp % 2 == 0 and hc == 0:
                                W.wait(pe, part)
                            out = acc[:, 2 * kv + hc, 0:N].rearrange("p (g n) -> p g n", g=3)
                            last = run_passes(pe, out, passes, pp == 0, pp == 15)
                        if pp % 2 == 1:
                            last.then_inc(W.used, 1)

            @block.vector
            def _(dve):
                for part in range(16):
                    W.next_lo(dve, 2 * first + part)
                dve.wait_ge(W.used, 2 * first + 16)
                dve.tensor_copy(pos_sum[:, :], acc[:, :, 2 * 16]).then_inc(pos_out, 1)
                dve.wait_ge(hi_done, 1)
                dve.tensor_tensor(hid_lo[:, :, :], hid[:, :, :], hid_hi[:, :, :].bitcast(F32), ALU.subtract)

            @block.scalar
            def _(act):
                for part in range(16):
                    W.next_hi(act, 2 * first + part)
                act.wait_ge(pos_out, 1)
                for i in range(4):
                    last = act.activation(hid[:, i, :], acc[:, i, 0:2 * 16], ACT.Gelu_apprx_tanh,
                                          bias=pos_sum[:, i:i + 1])
                last.then_inc(geluv, 1)
                act.wait_ge(geluv, 1)
                act.activation(hid_hi[:, :, :], hid[:, :, :], ACT.Copy).then_inc(hi_done, 1)

        with stage(nc, "cmp2") as S:
            acc = S.ps("acc", [P, 2, 512])
            turned = S.ps("turned", [P, 2, P])
            vT = S.sb("vT", [P, 2, P])
            cleared, vT_done, v_turned = S.sem("cleared"), S.sem("vT_done"), S.sem("v_turned")
            block = S.block()
            part0 = 2 * (first + 8)

            @block.sync
            def _(sync):
                W.feed(sync, first + 8, 1)

            @block.scalar
            def _(act):
                for kv in range(2):
                    W.next_hi(act, part0 + kv)

            @block.tensor
            def _(pe):
                for kv in range(2):
                    W.wait(pe, part0 + kv)
                    for hc in range(2):
                        i = 2 * kv + hc
                        last = run_passes(pe, acc[:, kv, 0:2 * 16],
                                          W.stationary(part0 + kv, hc * P, (hid_hi[:, i, :], hid_lo[:, i, :])),
                                          hc == 0, hc == 1)
                    last.then_inc(W.used, 1)
                pe.wait_ge(vT_done, 1)
                for grp in range(2):
                    last = pe.transpose(turned[:, grp, :], vT[:, grp, :], const[:, 0:P])
                last.then_inc(v_turned, 1)

            @block.vector
            def _(dve):
                dve.memset(kc[:, :], 0.0)
                dve.memset(vT[:, :, :], 0.0).then_inc(cleared, 1)
                for kv in range(2):
                    W.next_lo(dve, part0 + kv)
                dve.wait_ge(cleared, 1)
                dve.wait_ge(W.used, part0 + 2)
                for grp in range(2):
                    mine = slice(grp * 16, grp * 16 + N_CMP)
                    dve.tensor_copy(kc[64 * grp:64 * grp + 64, 0:N_CMP], acc[64 * grp:64 * grp + 64, 0, mine])
                    last = dve.tensor_copy(vT[:, grp, 0:N_CMP], acc[:, 1, mine])
                last.then_inc(vT_done, 1)
                dve.wait_ge(v_turned, 1)
                dve.tensor_copy(vc[:, :, :], turned[:, :, :])


def small_gates(nc, name, rows, gates, cmp_gates, valid, X, pos):
    with stage(nc, name) as S:
        done, cleared = S.sem("done"), S.sem("cleared")
        block = S.block()

        @block.scalar
        def _(act):
            act.activation(gates[:, :, :], rows[:, :, 384:408], ACT.Sigmoid).then_inc(done, 1)

        @block.vector
        def _(dve):
            dve.memset(X[:, :, 0:2, T:XT], 0.0)
            dve.memset(X[64:128, :, 0:2, T - 1:T], 0.0)
            dve.memset(X[:, :, 2, :], 0.0).then_inc(cleared, 1)
            dve.wait_ge(cleared, 1)
            dve.tensor_copy(X[:, :, 2, 0:31:2], pos.rearrange("p (kv pp) -> p kv pp", kv=2))
            dve.wait_ge(done, 1)
            by = gates[:, :, :].rearrange("p t (h b) -> p t h b", b=3)
            dve.tensor_scalar(cmp_gates[:, 0, :], by[:, 0, :, 0], valid, None, ALU.mult)
            dve.tensor_copy(cmp_gates[:, 1, :], by[:, 1, :, 0])


def causal_units(q, k, v, bias, tt, **more):
    nk = P * (tt + 1)
    return Unit(q[:, tt * P:(tt + 1) * P], k[:, 0:nk], v, nk, 64 ** -0.5, bias=bias[:, 2 * P - nk:2 * P], **more)


def second_layer(nc, W, layer, h, bias, cmp_bias, neg_lam, cols, const, dram):
    ones, ident = const[:, P:2 * P], const[:, 0:P]
    n = str(layer)

    def norm_to(dst, which, name):
        at = col_at("norms") + 32 * layer + 8 * which
        norm(nc, name, lambda c: h[:, c, 0:T], None, KD, T, ones, lambda c, s: cols[:, at + c:at + c + 1], pair=dst)

    with ExitStack() as ctx:
        def sb(name, shape, dt=F32):
            return ctx.enter_context(nc.sbuf_tensor("second%d_%s" % (layer, name), shape, dt))

        x_hi, x_lo = sb("x_hi", [P, KD, T], F32R), sb("x_lo", [P, KD, T], F32R)
        x = split_pair(x_hi, x_lo)
        norm_to(x, 0, "ffn1n")
        feed_forward(nc, W, "ffn1_" + n, x, h)
        norm_to(x, 1, "attn_n")
        merged = sb("merged", [P, KD, T])
        with ExitStack() as inner:
            def tmp_sb(name, shape, dt=F32):
                return inner.enter_context(nc.sbuf_tensor("second%d_%s" % (layer, name), shape, dt))

            y = tmp_sb("y", [P, 3, 4, T])
            with ExitStack() as attn:
                def at_sb(name, shape, dt=F32):
                    return attn.enter_context(nc.sbuf_tensor("second%d_%s" % (layer, name), shape, dt))

                heads = at_sb("heads", [P, 19, T])
                X = at_sb("X", [P, 2, 3, XT])
                X_hi, X_lo = at_sb("X_hi", [P, 2, 3, XT], F32R), at_sb("X_lo", [P, 2, 3, XT], F32R)
                av = at_sb("av", [P, 2, 512])
                rows = at_sb("rows", [P, 2, 512])
                kc = at_sb("kc", [P, P])
                vc = at_sb("vc", [P, 2, P])
                gates = at_sb("gates", [P, 2, 24])
                cmp_gates = at_sb("cmp_gates", [P, 2, 8])
                first = W.take("in_cols" + n)

                def evacuate(act, chain, c, ps):
                    if c < 19:
                        return act.activation(heads[:, c, :], ps[:, 0:T], ACT.Copy)
                    for g in range(2):
                        act.activation(X[0:64, c - 19, g, 0:T], ps[64 * g:64 * g + 64, 0:T], ACT.Copy)
                        last = act.activation(X[64:128, c - 19, g, 0:T - 1], ps[64 * g:64 * g + 64, 1:T], ACT.Copy)
                    return last

                products(nc, W, "in_cols", first, 21, column_jobs(W, first, 21, KD, T, x),
                         evacuate, "scalar")
                first = W.take("in_rows" + n)
                row_products(nc, W, "in_rows", first, 2, lambda k, tt: (x_hi[:, k, tt * P:(tt + 1) * P], x_lo[:, k, tt * P:(tt + 1) * P]), 2,
                             lambda act, half, tt, ps: act.activation((av, rows)[half][:, tt, :], ps, ACT.Copy))
                pos_at = col_at("pos") + 32 * layer
                small_gates(nc, "small_gates", rows, gates, cmp_gates, cols[:, col_at("valid"):col_at("valid") + 1],
                            X, cols[:, pos_at:pos_at + 32])
                split_stage(nc, "X_split", *(b[:, :, :, :].rearrange("p a g t -> p (a g t)") for b in (X, X_hi, X_lo)))
                compress_stage(nc, W, layer, lambda kv: (X_hi[:, kv, :, :], X_lo[:, kv, :, :]), kc, vc, const)

                units = []
                for head in range(4):
                    for tt in range(2):
                        for c in range(2):
                            half = slice(64 * c, 64 * c + 64)
                            units.append(causal_units(
                                heads[half, head, :], heads[half, 4 + head, :],
                                lambda b, head=head: av[:, b, head * P:(head + 1) * P], bias[:, head, :], tt,
                                weight=neg_lam[:, layer:layer + 1] if c else None, first=c == 0, end=c == 1,
                                out=(0, P, y[:, 0, head, tt * P:(tt + 1) * P])))
                for g in range(2):
                    half = slice(64 * g, 64 * g + 64)
                    for r in range(4):
                        head = 4 * g + r
                        for tt in range(2):
                            tok = slice(tt * P, (tt + 1) * P)
                            out = (64 * g, 64 * g + 64, y[half, 1, r, tok])
                            units.append(Unit(heads[half, 8 + r, tok], kc[half, :], lambda b, g=g: vc[:, g, :], P,
                                              64 ** -0.5, bias=cmp_bias[:, tt, head, :],
                                              weight=cmp_gates[:, tt, head:head + 1], first=True, end=False))
                            for br in (1, 2):
                                gate = gates[:, tt, 3 * head + br:3 * head + br + 1]
                                units.append(causal_units(
                                    heads[half, 8 + r, :], heads[half, 11 + br, :],
                                    lambda b, br=br: rows[:, b, (br - 1) * P:br * P], bias[:, B_HEAD0 + head, :], tt,
                                    weight=gate, first=False, end=br == 2, out=out))
                    for r in range(4):
                        head = 4 * g + r
                        at = col_at("sinks") + 8 * layer + head
                        for tt in range(2):
                            units.append(causal_units(
                                heads[half, 14 + r, :], heads[half, 18, :], lambda b: rows[:, b, 2 * P:3 * P],
                                bias[:, C_HEAD0 + head, :], tt, sink=cols[:, at:at + 1],
                                out=(64 * g, 64 * g + 64, y[half, 2, r, tt * P:(tt + 1) * P])))
                attention(nc, "attn", units, ident)
            at = col_at("subln") + layer
            norm(nc, "subln", lambda c: y[:, 0, c, :], lambda c: y[:, 0, c, :], 1, T, ones, lambda c, s: cols[:, at:at + 1],
                 groups=4, post=0.2 + 0.6 * math.exp(-0.3 * layer))
            y_hi, y_lo = tmp_sb("y_hi", [P, 3, 4, T], F32R), tmp_sb("y_lo", [P, 3, 4, T], F32R)
            split_stage(nc, "y_split", *(b[:, :, :, :].rearrange("p b k t -> p (b k t)") for b in (y, y_hi, y_lo)))
            sig = tmp_sb("sig", [P, 3, KD, T])
            term = tmp_sb("term", [P, 2, T])
            first = W.take("gates" + n)
            products(nc, W, "gates", first, 24, column_jobs(W, first, 24, KD, T, x),
                     lambda act, chain, c, ps: act.activation(sig[:, c // 8, c % 8, :], ps[:, 0:T], ACT.Sigmoid), "scalar")
            first = W.take("branch" + n)
            jobs = []
            for br in range(3):
                jobs += column_jobs(W, first + 4 * br, 8, 4, T, split_pair(y_hi[:, br, :, :], y_lo[:, br, :, :]))

            def merge(dve, chain, c, ps):
                br, j = c // 8, c % 8
                if br == 0:
                    return dve.tensor_tensor(merged[:, j, :], ps[:, 0:T], sig[:, br, j, :], ALU.mult)
                chain(dve.tensor_tensor(term[:, c % 2, :], ps[:, 0:T], sig[:, br, j, :], ALU.mult))
                return dve.tensor_tensor(merged[:, j, :], merged[:, j, :], term[:, c % 2, :], ALU.add)

            products(nc, W, "branch", first, 12, jobs, merge, "vector")
        first = W.take("out" + n)
        m_hi, m_lo = sb("merged_hi", [P, KD, T], F32R), sb("merged_lo", [P, KD, T], F32R)
        split_stage(nc, "merged_split", *(b[:, :, :].rearrange("p k t -> p (k t)") for b in (merged, m_hi, m_lo)))
        products(nc, W, "out", first, 8, column_jobs(W, first, 8, KD, T, split_pair(m_hi, m_lo)),
                 lambda dve, chain, c, ps: dve.tensor_tensor(h[:, c, 0:T], h[:, c, 0:T], ps[:, 0:T], ALU.add), "vector")
        norm_to(x, 2, "ffn2n")
        feed_forward(nc, W, "ffn2_" + n, x, h)
        norm_to(x, 3, "ple_n")
        p_in = sb("p", [P, 2, T])
        p_hi, p_lo = sb("p_hi", [P, 2, T], F32R), sb("p_lo", [P, 2, T], F32R)
        split_stage(nc, "p_split", *(b[:, :, :].rearrange("p k t -> p (k t)") for b in (p_in, p_hi, p_lo)),
                    load=dram["p" + n], pieces=1)
        pw = sb("pw", [P, KD, T])
        first = W.take("ple_w" + n)
        products(nc, W, "ple_w", first, 2, column_jobs(W, first, 8, 2, T, split_pair(p_hi, p_lo)),
                 lambda act, chain, c, ps: act.activation(pw[:, c, :], ps[:, 0:T], ACT.Copy), "scalar")
        first = W.take("ple_gate" + n)
        products(nc, W, "ple_gate", first, 8, column_jobs(W, first, 8, KD, T, x),
                 lambda act, chain, c, ps: act.activation(merged[:, c, :], ps[:, 0:T], ACT.Sigmoid), "scalar")
        with stage(nc, "ple_add") as S:
            done = S.sem("done")
            block = S.block()

            @block.vector
            def _(dve):
                dve.tensor_tensor(pw[:, :, :], pw[:, :, :], merged[:, :, :], ALU.mult).then_inc(done, 1)
                dve.wait_ge(done, 1)
                dve.tensor_tensor(h[:, :, 0:T], h[:, :, 0:T], pw[:, :, :], ALU.add)


def store_stage(nc, y, out):
    with stage(nc, "store") as S:
        stored = S.sem("stored")
        block = S.block()

        @block.sync
        def _(sync):
            sync.dma_start(out, y[:, :, :].rearrange("p k t -> p (k t)")).then_inc(stored, 16)
            sync.wait_ge(stored, 16)


def build(nc, dram, out, debug=None, upto=99):
    def dump(name, ap):
        if debug is not None:
            debug(name, ap)

    STAGES[0] = 0
    cols = nc.alloc_sbuf_tensor("cols_sb", [P, N_COLS], F32)
    const = nc.alloc_sbuf_tensor("const_sb", [P, N_CONST], F32)
    modulation = nc.alloc_sbuf_tensor("modulation", [P, 2, 48, 2], F32)
    scales = nc.alloc_sbuf_tensor("scales", [P, 2, 2, 2, KD], F32)
    h = nc.alloc_sbuf_tensor("h", [P, KD, 2 * T], F32)
    W = Weights(nc, dram["w_tiles"], dram["peer_tiles"])
    modulation_stage(nc, W, h, modulation, scales, cols, const, dram)
    even_mixer(nc, W, h, modulation, scales, cols, const, dram["rope"])
    dump("h_even", h)
    if upto <= 1:
        return
    for s in (LAT, CTX):
        peer(nc, W, 0, s, h[:, :, s * T:(s + 1) * T], lambda c, s=s: scales[:, 0, 1, s, c:c + 1],
             lambda c, s=s: modulation[:, 0, 24 + c, s:s + 1], lambda c, s=s: modulation[:, 0, 40 + c, s:s + 1], const, dram)
        if upto <= 2:
            dump("h_peer", h)
            return
    dump("h_peer0", h)
    odd_mixer(nc, W, h, modulation, scales, cols, const, dram["select"], dram["masks"])
    dump("h_odd", h)
    peer(nc, W, 1, LAT, h[:, :, 0:T], lambda c: scales[:, 1, 1, LAT, c:c + 1],
         lambda c: modulation[:, 1, 24 + c, LAT:LAT + 1], lambda c: modulation[:, 1, 40 + c, LAT:LAT + 1], const, dram)
    ones = const[:, P:2 * P]
    at = col_at("norm_f")
    norm(nc, "norm_f", lambda c: h[:, c, 0:T], lambda c: h[:, c, 0:T], KD, T, ones, lambda c, s: cols[:, at + c:at + c + 1])
    dump("h_first", h)
    with nc.sbuf_tensor("cols2_sb", [P, N_COLS2], F32) as cols2:
        with nc.sbuf_tensor("bias_sb", [P, N_BIAS, T], F32) as bias, \
                nc.sbuf_tensor("cmp_bias", [P, 2, 8, P], F32) as cmp_bias, nc.sbuf_tensor("neg_lam", [P, 2], F32) as neg_lam:
            bias_stage(nc, bias, cmp_bias, neg_lam, cols2, dram)
            for layer in range(2):
                second_layer(nc, W, layer, h, bias, cmp_bias, neg_lam, cols2, const, dram)
                dump("h_second%d" % layer, h)
        with nc.sbuf_tensor("y_out", [P, KD, T], F32) as y:
            at2 = col_at("final")
            norm(nc, "final", lambda c: h[:, c, 0:T], lambda c: y[:, c, :], KD, T, ones,
                 lambda c, s: cols2[:, at2 + c:at2 + c + 1])
            store_stage(nc, y, out)


def column_tiles(w):
    k = w.shape[0] // P
    per = KD // k
    n = -(-w.shape[1] // (P * per)) * per
    full = np.zeros((k * P, n * P), w.dtype)
    full[:, :w.shape[1]] = w
    a = full.reshape(k, P, n // per, per, P).transpose(2, 1, 3, 0, 4)
    return a.reshape(n // per, P, TILE)


def row_tiles(w):
    n = -(-w.shape[1] // 512)
    full = np.zeros((w.shape[0], n * 512), w.dtype)
    full[:, :w.shape[1]] = w
    return full.reshape(4, 2, P, n, 512).transpose(3, 0, 2, 1, 4).reshape(4 * n, P, TILE)


def padded_tile(a):
    a = a.reshape(P, -1)
    out = np.zeros((1, P, TILE), a.dtype)
    out[0, :, :a.shape[1]] = a
    return out


def swapped_rope(w):
    return np.concatenate([w[..., 16:32], w[..., 0:16]], axis=-1)


def pair_heads(w, axis):
    w = np.moveaxis(w, axis, 0)
    rest = w.shape[1:]
    w = w.reshape((2, 4, 64) + rest).transpose((1, 0, 2) + tuple(range(3, 3 + len(rest)))).reshape((512,) + rest)
    return np.moveaxis(w, 0, axis)


def feed_forward_tiles(wi, wo):
    gate, up = column_tiles(wi[:, :D_FF]), column_tiles(wi[:, D_FF:])
    down = wo.reshape(FC, P, D)
    out = [gate[0], up[0]]
    for c in range(FC):
        if c + 1 < FC:
            out += [gate[c + 1], up[c + 1]]
        out.append(down[c])
    return np.stack(out)


def layout_weights(a):
    f = {}
    f["mod"] = np.concatenate([row_tiles(a["w_mod"][i]) for i in range(2)])
    w = a["even_w_in"][0]
    kr = w[:, 384:416]
    conv = [w[:, 416 + 512 * i:928 + 512 * i].reshape(D, 4, P) for i in range(3)]
    triples = np.stack([conv[1], conv[2], conv[0]], axis=2).reshape(D, 1536)
    f["even_in"] = column_tiles(np.concatenate([w[:, :384], np.zeros((D, 64), w.dtype), kr, swapped_rope(kr), triples], 1))
    uq = a["mla_w_uq"][0].reshape(256, MLA_HEADS, 96)
    f["uq"] = column_tiles(np.concatenate([uq, swapped_rope(uq[..., 64:])], -1).reshape(256, 1024))
    f["ukv"] = a["mla_w_ukv"][0].reshape(P, MLA_HEADS, 2, 64).transpose(0, 2, 1, 3).reshape(1, P, TILE)
    f["even_out"] = column_tiles(a["even_w_out"][0])
    for layer in range(2):
        f["peer_q%d" % layer] = column_tiles(a["peer_w_q"][layer])
    w = a["odd_w_in"][0]
    gates = np.zeros((D, 4, 32), w.dtype)
    gates[:, :, :4] = w[:, 2048:2064].reshape(D, 4, 4)
    f["odd_qk"] = column_tiles(np.concatenate([w[:, :1024], gates.reshape(D, P)], 1))
    f["odd_v"] = row_tiles(w[:, 1024:2048])
    f["odd_gate"] = column_tiles(w[:, 2064:])
    f["odd_out"] = column_tiles(a["odd_w_out"][0])
    for i in range(2):
        w, n = a["w_in_2"][i], str(i)
        f["ffn1_" + n] = feed_forward_tiles(a["ffn1_wi_2"][i], a["ffn1_wo_2"][i])
        f["ffn2_" + n] = feed_forward_tiles(a["ffn2_wi_2"][i], a["ffn2_wo_2"][i])
        f["in_cols" + n] = column_tiles(np.concatenate([
            w[:, 0:1024], pair_heads(w[:, 1536:2048], 1), w[:, 2304:2432], w[:, 2560:2688],
            pair_heads(w[:, 2840:3352], 1), w[:, 3352:3480], w[:, 2048:2304]], 1))
        f["in_rows" + n] = row_tiles(np.concatenate([
            w[:, 1024:1536], w[:, 2432:2560], w[:, 2688:2816], w[:, 3480:3608], w[:, 2816:2840]], 1))
        w1 = a["nsa_cmp_w1_2"][i].reshape(2, 4, 4, P, 256).transpose(0, 1, 3, 2, 4).reshape(8, P, TILE)
        w2 = a["nsa_cmp_w2_2"][i].reshape(2, 2, P, 64)
        w2 = np.concatenate([w2, w2], -1).transpose(2, 0, 1, 3).reshape(P, 2, 2 * P)
        w2 = np.concatenate([w2, np.zeros_like(w2)], -1)
        f["cmp" + n] = np.concatenate([w1, padded_tile(w2)])
        f["gates" + n] = column_tiles(w[:, 3608:])
        wb = a["w_branch_2"][i]
        f["branch" + n] = np.concatenate([column_tiles(x) for x in (wb[0], pair_heads(wb[1], 0), pair_heads(wb[2], 0))])
        f["out" + n] = column_tiles(a["w_out_2"][i])
        f["ple_w" + n] = column_tiles(a["w_ple_2"][i])
        f["ple_gate" + n] = column_tiles(a["w_ple_gate_2"][i])
    bases, size = tile_bases()
    out = np.empty((size["w"], P, TILE), np.float32)
    for name, n, source in stream_plan():
        if source == "w":
            assert f[name].shape == (n, P, TILE), (name, f[name].shape)
            out[bases[name]:bases[name] + n] = f[name]
    return out.reshape(-1, TILE)


def layout_experts(u, v):
    out = np.empty((2, PEER_TILES, P, TILE), u.dtype)
    for layer in range(2):
        ut = u[layer].reshape(NKEYS, NKEYS, KD, P).transpose(1, 3, 2, 0).reshape(NKEYS, P, TILE)
        vt = v[layer].reshape(NKEYS, NKEYS, D).transpose(1, 0, 2)
        out[layer, 0] = ut[0]
        out[layer, 1:-1:2] = ut[1:]
        out[layer, 2:-1:2] = vt[:-1]
        out[layer, -1] = vt[-1]
    return out.reshape(-1, TILE)


def features(v):
    return np.ascontiguousarray(v.reshape(-1, P).T)


def spread(v):
    return np.broadcast_to(v.reshape(1, -1), (P, v.size))


def layout_columns(a):
    gate_b = np.zeros((4, 32), np.float32)
    gate_b[:, :4] = a["mlstm_gate_b"][0].reshape(4, 4)
    pos = a["nsa_cmp_pos_2"].reshape(4, 16, P)
    parts = {
        "norm1": features(a["norm1_g"]), "norm2": features(a["norm2_g"]), "b_mod": features(a["b_mod"]),
        "q_norm": features(a["mla_q_norm"]), "kv_norm": features(a["mla_kv_norm"]), "conv": features(a["conv_w"]),
        "head_g": features(a["mlstm_head_g"]), "norm_f": features(a["norm_f_g"]), "norms": features(a["norm_g_2"]),
        "subln": features(a["diff_subln_2"]), "final": features(a["final_norm_2"]), "gate_b": gate_b.reshape(P, 1),
        "pos": pos.reshape(64, P).T, "lam": spread(a["diff_lambda_2"]), "sinks": spread(a["swa_sinks_2"]),
        "valid": (np.arange(P) >= 31).astype(np.float32).reshape(P, 1),
    }
    for name, width in COLS + COLS2:
        assert parts[name].shape == (P, width), (name, parts[name].shape)
    return [np.concatenate([parts[name] for name, _ in columns], 1) for columns in (COLS, COLS2)]


def constants():
    const = np.concatenate([np.eye(P), np.ones((P, P)), np.tile(np.arange(P), (P, 1)), np.tile(np.arange(16), (P, 1))],
                           1).astype(np.float32)
    inv = np.float32(10000.0) ** (-np.arange(8, dtype=np.float32) / np.float32(8))
    t = np.arange(T)
    ang = np.concatenate([(t // 64).astype(np.float32)[:, None] * inv, (t % 64).astype(np.float32)[:, None] * inv], -1)
    cos, sin = np.cos(ang).T, np.sin(ang).T
    rope = np.zeros((P, 2 * T), np.float32)
    rope[64:96, T:] = 1.0
    rope[64:96, :T] = np.concatenate([cos, cos])
    rope[96:128, :T] = np.concatenate([-sin, sin])
    dist = np.arange(512) - 256
    n = np.maximum(dist, 0)
    nf = np.maximum(n, 1).astype(np.float32)
    large = 16 + (np.log(nf / 16) / np.float32(math.log(8)) * 16).astype(np.int32)
    bucket = np.where(n < 16, n, np.minimum(large, 31))
    onehot = np.zeros((34, 512), np.float32)
    seen = dist >= 0
    onehot[bucket[seen], np.nonzero(seen)[0]] = 1.0
    onehot[32] = ~seen
    onehot[33] = dist >= 128
    masked = np.zeros((2, N_BIAS), np.float32)
    masked[0] = NEG
    masked[1, C_HEAD0:] = NEG
    select = np.zeros((P, ML_HEADS, P), np.float32)
    for hd in range(ML_HEADS):
        select[32 + hd, hd] = select[96 + hd, hd] = 1.0
    q = np.arange(T).reshape(2, P).T[:, :, None]
    s = np.arange(T)[None, None, :]
    masks = np.stack([s <= q, s >= q], 1).astype(np.float32)
    return {"const": const, "rope": rope, "onehot": onehot, "masked": masked, "select": select.reshape(P, -1),
            "masks": masks.reshape(P, -1)}


def layout(inputs):
    a = {k: np.asarray(v) for k, v in inputs.items()}

    def tokens(x):
        return x.T.reshape(-1, P, x.shape[0]).transpose(1, 0, 2)

    arrays = constants()
    arrays["w_tiles"] = layout_weights(a)
    arrays["peer_tiles"] = layout_experts(a["peer_u"], a["peer_v"])
    arrays["cols"], arrays["cols2"] = layout_columns(a)
    for layer in range(2):
        arrays["subkeys%d" % layer] = a["peer_subkeys"][layer].reshape(2 * PH, NKEYS, P).transpose(2, 0, 1).reshape(P, -1)
    arrays["tokens"] = np.concatenate([tokens(a["x"][0]), tokens(a["ctx"][0])], 2).reshape(P, -1)
    arrays["c_cols"] = np.stack([features(a["c"][0]), features(a["c_ctx"])], 2).reshape(P, -1)
    arrays["rel_bias"] = a["rel_bias_2"]
    for i in range(2):
        arrays["p%d" % i] = tokens(a["p_2"][i, 0]).reshape(P, -1)
    return {k: np.ascontiguousarray(v) for k, v in arrays.items()}


def kernel(**inputs):
    import concourse.bacc as bacc
    from concourse.bass_utils import run_bass_kernel_spmd

    arrays = layout(inputs)
    nc = bacc.Bacc("TRN2", target_bir_lowering=False, num_devices=1)
    dram = {name: nc.dram_tensor("in_" + name, x.shape, mybir.dt.from_np(x.dtype), kind="ExternalInput").ap()
            for name, x in arrays.items()}
    out = nc.dram_tensor("out_y", (P, KD * T), F32, kind="ExternalOutput").ap()
    build(nc, dram, out)
    r = run_bass_kernel_spmd(nc, [{"in_" + name: x for name, x in arrays.items()}], core_ids=[0])
    y = r.results[0]["out_y"].reshape(P, KD, T)
    return y.transpose(2, 1, 0).reshape(1, T, D)
```

```python
import math
from contextlib import ExitStack, contextmanager

import numpy as np

import concourse.bass as bass
from concourse import mybir

F32 = mybir.dt.float32
U32 = mybir.dt.uint32
F32R = mybir.dt.float32r
ALU = mybir.AluOpType
ACT = mybir.ActivationFunctionType
X_AXIS = mybir.AxisListType.X

P = 128
D = 1024
KD = D // P
T = 256
LAT, CTX = 0, 1
RING = 4
TILE = 1024
PARTS = 4
PART = TILE // 2
EPS = 1e-6
NEG = -1e30

MLA_HEADS, MLA_NOPE, MLA_ROPE = 8, 64, 32
MLA_SCALE = (MLA_NOPE + MLA_ROPE) ** -0.5
ML_HEADS, ML_DV = 4, 256
ML_SCALE = 128 ** -0.5
PH, NKEYS, TOPK = 8, 128, 16
PEER_TILES = 2 * NKEYS
D_FF = 2816
FC = D_FF // P
N_BIAS = 20
N_CMP = 15
XT = T + 16


def stream_plan():
    def route(layer):
        return [("peer_q%d" % layer, 16, "w"), ("experts%d" % layer, PEER_TILES, "peer")]

    plan = [("mod", 96, "w"), ("even_in", 16, "w"), ("uq", 2, "w"), ("ukv", 1, "w"), ("even_out", 8, "w")]
    plan += route(0) + route(0)
    plan += [("odd_qk", 9, "w"), ("odd_v", 8, "w"), ("odd_gate", 8, "w"), ("odd_out", 8, "w")] + route(1)
    for i in range(2):
        plan += [(name + str(i), n, "w") for name, n in (
            ("ffn1_", 3 * FC), ("in_cols", 21), ("in_rows", 8), ("cmp", 9), ("gates", 24), ("branch", 12),
            ("out", 8), ("ffn2_", 3 * FC), ("ple_w", 2), ("ple_gate", 8))]
    return plan


def tile_bases():
    bases, nxt = {}, {"w": 0, "peer": 0}
    for name, n, source in stream_plan():
        if name not in bases:
            bases[name] = nxt[source]
            nxt[source] += n
    return bases, nxt


COLS = [("norm1", 16), ("norm2", 16), ("b_mod", 96), ("q_norm", 2), ("kv_norm", 1), ("conv", 12), ("head_g", 8),
        ("norm_f", 8), ("gate_b", 1)]
COLS2 = [("norms", 64), ("subln", 2), ("final", 8), ("pos", 64), ("lam", 512), ("sinks", 16), ("valid", 1)]


def col_at(name):
    for columns in (COLS, COLS2):
        at = 0
        for n, w in columns:
            if n == name:
                return at
            at += w
    raise KeyError(name)


N_COLS = sum(w for _, w in COLS)
N_COLS2 = sum(w for _, w in COLS2)
N_CONST = 3 * P + 16


class Weights:

    def __init__(self, nc, w_tiles, peer_tiles):
        self.sources = {"w": w_tiles, "peer": peer_tiles}
        self.ring = nc.alloc_sbuf_tensor("weight_ring", [P, RING, TILE], F32)
        self.hi = nc.alloc_sbuf_tensor("weight_hi", [P, PARTS, PART], F32R)
        self.lo = nc.alloc_sbuf_tensor("weight_lo", [P, PARTS, PART], F32R)
        self.arrived = [nc.alloc_semaphore("tile_arrived%d" % i) for i in range(RING)]
        self.hi_done = nc.alloc_semaphore("parts_hi_done")
        self.lo_done = nc.alloc_semaphore("parts_lo_done")
        self.used = nc.alloc_semaphore("parts_used")
        self.plan = stream_plan()
        bases, _ = tile_bases()
        self.tiles = []
        for name, n, source in self.plan:
            self.tiles += [(source, bases[name] + i) for i in range(n)]
        self.at = 0
        self.seg = 0

    def take(self, name):
        got, n, _ = self.plan[self.seg]
        assert got == name, (got, name)
        first = self.at
        self.at += n
        self.seg += 1
        return first

    def wait(self, pe, part):
        pe.wait_ge(self.lo_done, part + 1)

    def load(self, sync, g):
        source, i = self.tiles[g]
        sync.dma_start(self.ring[:, g % RING, :], self.sources[source][i * P:(i + 1) * P, :]
                       ).then_inc(self.arrived[g % RING], 16)

    def prime(self, sync):
        for g in range(RING):
            self.load(sync, g)

    def feed(self, sync, first, n):
        for g in range(first + RING, min(first + n + RING, len(self.tiles))):
            sync.wait_ge(self.lo_done, 2 * (g - RING) + 2)
            self.load(sync, g)

    def write_hi(self, act, part):
        if part < 2 * len(self.tiles):
            g = part // 2
            act.wait_ge(self.arrived[g % RING], 16 * (g // RING + 1))
            act.activation(self.hi[:, part % PARTS, :], self.ring[:, g % RING, (part % 2) * PART:(part % 2 + 1) * PART],
                           ACT.Copy).then_inc(self.hi_done, 1)

    def write_lo(self, dve, part):
        if part < 2 * len(self.tiles):
            g = part // 2
            dve.wait_ge(self.hi_done, part + 1)
            dve.tensor_tensor(self.lo[:, part % PARTS, :], self.ring[:, g % RING, (part % 2) * PART:(part % 2 + 1) * PART],
                              self.hi[:, part % PARTS, :].bitcast(F32), ALU.subtract).then_inc(self.lo_done, 1)

    def next_hi(self, act, part):
        act.wait_ge(self.used, part + 1)
        self.write_hi(act, part + PARTS)

    def next_lo(self, dve, part):
        self.write_lo(dve, part + PARTS)

    def stationary(self, part, at, x):
        w_hi, w_lo = (w[:, part % PARTS, at:at + P] for w in (self.hi, self.lo))
        return [(w_hi, x[0]), (w_hi, x[1]), (w_lo, x[0])]

    def moving(self, part, x):
        w_hi, w_lo = (w[:, part % PARTS, :] for w in (self.hi, self.lo))
        return [(x[0], w_hi), (x[0], w_lo), (x[1], w_hi)]


def run_passes(pe, out, passes, start, stop, **more):
    for i, (lhsT, rhs) in enumerate(passes):
        last = pe.matmul(out, lhsT, rhs, start=start and i == 0, stop=stop and i == len(passes) - 1, **more)
    return last


def split_pair(hi, lo):
    return lambda k: (hi[:, k, :], lo[:, k, :])


class Stage:
    def __init__(self, nc, name, ctx):
        self.nc, self.name, self.ctx = nc, name, ctx

    def sem(self, name):
        return self.nc.alloc_semaphore("%s_%s" % (self.name, name))

    def sb(self, name, shape, dt=F32):
        return self.ctx.enter_context(self.nc.sbuf_tensor("%s_%s" % (self.name, name), shape, dt))

    def ps(self, name, shape):
        return self.ctx.enter_context(self.nc.psum_tensor("%s_%s" % (self.name, name), shape, F32))

    def block(self):
        return self.ctx.enter_context(self.nc.Block())


STAGES = [0]


@contextmanager
def stage(nc, name):
    STAGES[0] += 1
    with nc.cleanup_on_exit():
        with ExitStack() as ctx:
            yield Stage(nc, "%s_%d" % (name, STAGES[0]), ctx)


class Chain:

    def __init__(self, eng, sem):
        self.eng, self.sem, self.n = eng, sem, 0

    def __call__(self, ins):
        self.n += 1
        ins.then_inc(self.sem, 1)
        self.eng.wait_ge(self.sem, self.n)


class Job:

    def __init__(self, mms):
        self.mms = mms
        self.part = mms[-1][1]


def column_jobs(W, first, n_chunks, K, N, x):
    jobs = []
    for c in range(n_chunks):
        mms = []
        for k in range(K):
            at = (c * K + k) * P
            part = 2 * first + at // PART
            mms.append(((0, N), part, W.stationary(part, at % PART, x(k)), k == 0, k == K - 1))
        jobs.append(Job(mms))
    return jobs


def products(nc, W, name, first, n_tiles, jobs, evacuate, who, prepare=None, const_load=None,
             evacuated_out=None, banks=4):
    with stage(nc, name) as S:
        acc = S.ps("acc", [P, banks, 512])
        job_done = S.sem("job_done")
        evacuated = S.sem("evacuated")
        ordered = S.sem("ordered")
        const_in = S.sem("const_in")
        if evacuated_out is not None:
            evacuated_out.append(evacuated)
        last_mm = {mm[1]: (c, i) for c, j in enumerate(jobs) for i, mm in enumerate(j.mms)}
        ready, within = [], 0
        for c, j in enumerate(jobs):
            if last_mm[j.part] == (c, len(j.mms) - 1):
                ready.append((W.used, j.part + 1))
            else:
                within += 1
                ready.append((job_done, within))
        parts = range(2 * first, 2 * (first + n_tiles))
        assert sorted(last_mm) == list(parts)
        block = S.block()

        @block.sync
        def _(sync):
            if const_load is not None:
                for dst, src in const_load:
                    sync.dma_start(dst, src).then_inc(const_in, 16)
            W.feed(sync, first, n_tiles)

        @block.tensor
        def _(pe):
            seen = None
            for c, j in enumerate(jobs):
                if c >= banks:
                    pe.wait_ge(evacuated, c - banks + 1)
                for i, ((lo, hi), part, passes, start, stop) in enumerate(j.mms):
                    if part != seen:
                        W.wait(pe, part)
                        seen = part
                    last = run_passes(pe, acc[:, c % banks, lo:hi], passes, start, stop)
                    if last_mm[part] == (c, i):
                        last.then_inc(W.used, 1)
                    elif i == len(j.mms) - 1:
                        last.then_inc(job_done, 1)

        def read_out(eng, chain, part):
            for c, j in enumerate(jobs):
                if j.part == part:
                    eng.wait_ge(*ready[c])
                    evacuate(eng, chain, c, acc[:, c % banks, :]).then_inc(evacuated, 1)

        def start(eng):
            chain = Chain(eng, ordered)
            if const_load is not None:
                eng.wait_ge(const_in, 16 * len(const_load))
            if prepare is not None:
                prepare(eng, chain)
            return chain

        @block.scalar
        def _(act):
            chain = start(act) if who == "scalar" else None
            for part in parts:
                W.next_hi(act, part)
                if who == "scalar":
                    read_out(act, chain, part)

        @block.vector
        def _(dve):
            chain = start(dve) if who == "vector" else None
            for part in parts:
                W.next_lo(dve, part)
                if who == "vector":
                    read_out(dve, chain, part)


def row_products(nc, W, name, first, halves, x, n_tt, evacuate):
    with stage(nc, name) as S:
        acc = S.ps("acc", [P, halves * n_tt, 512])
        block = S.block()

        @block.sync
        def _(sync):
            W.feed(sync, first, 4 * halves)

        @block.tensor
        def _(pe):
            for half in range(halves):
                for k in range(KD):
                    part = 2 * first + KD * half + k
                    W.wait(pe, part)
                    for tt in range(n_tt):
                        last = run_passes(pe, acc[:, half * n_tt + tt, :], W.moving(part, x(k, tt)), k == 0, k == KD - 1)
                    last.then_inc(W.used, 1)

        @block.vector
        def _(dve):
            for k in range(KD * halves):
                W.next_lo(dve, 2 * first + k)

        @block.scalar
        def _(act):
            for half in range(halves):
                for k in range(KD):
                    W.next_hi(act, 2 * first + KD * half + k)
                for tt in range(n_tt):
                    evacuate(act, half, tt, acc[:, half * n_tt + tt, :])


def split_stage(nc, name, src, hi, lo, load=None, pieces=4):
    n = src.shape[1] // pieces
    with stage(nc, name) as S:
        hi_done, loaded = S.sem("hi_done"), S.sem("loaded")
        block = S.block()
        if load is not None:
            @block.sync
            def _(sync):
                sync.dma_start(src, load).then_inc(loaded, 16)

        @block.scalar
        def _(act):
            if load is not None:
                act.wait_ge(loaded, 16)
            for i in range(pieces):
                act.activation(hi[:, i * n:(i + 1) * n], src[:, i * n:(i + 1) * n], ACT.Copy).then_inc(hi_done, 1)

        @block.vector
        def _(dve):
            if load is not None:
                dve.wait_ge(loaded, 16)
            for i in range(pieces):
                dve.wait_ge(hi_done, i + 1)
                dve.tensor_tensor(lo[:, i * n:(i + 1) * n], src[:, i * n:(i + 1) * n],
                                  hi[:, i * n:(i + 1) * n].bitcast(F32), ALU.subtract)


def norm(nc, name, src, dst, K, N, ones, scale, groups=1, post=1.0, shift=None, mul=None, ranges=None, pair=None):
    ranges = ranges or [(0, N, 0)]
    n_chunks = K * groups
    with stage(nc, name) as S:
        sq = S.sb("sq", [P, n_chunks, N])
        root = S.sb("root", [P, groups, N])
        rstd = S.sb("rstd", [P, groups, N])
        total = S.ps("total", [P, groups, N])
        squared, summed, meaned, rooted, ordered, scaled, multiplied, hi_done = (
            S.sem(n) for n in ("squared", "summed", "meaned", "rooted", "ordered", "scaled", "multiplied", "hi_done"))
        value = dst if dst is not None else (lambda c: sq[:, c, :])
        valued = multiplied if mul is not None else scaled
        block = S.block()

        @block.scalar
        def _(act):
            for c in range(n_chunks):
                act.activation(sq[:, c, :], src(c), ACT.Square).then_inc(squared, 1)
            act.wait_ge(meaned, 1)
            act.activation(root[:, :, :], root[:, :, :], ACT.Sqrt).then_inc(rooted, 1)
            if pair is not None:
                for c in range(n_chunks):
                    act.wait_ge(valued, c + 1)
                    for lo, hi, s in ranges:
                        if shift is not None:
                            last = act.activation(pair(c)[0][:, lo:hi], value(c)[:, lo:hi], ACT.Identity, bias=shift(c, s))
                        else:
                            last = act.activation(pair(c)[0][:, lo:hi], value(c)[:, lo:hi], ACT.Copy)
                    last.then_inc(hi_done, 1)

        @block.tensor
        def _(pe):
            for c in range(n_chunks):
                pe.wait_ge(squared, c + 1)
                last = pe.matmul(total[:, c // K, :], ones, sq[:, c, :], start=(c % K == 0), stop=(c % K == K - 1))
            last.then_inc(summed, 1)

        @block.vector
        def _(dve):
            chain = Chain(dve, ordered)
            dve.wait_ge(summed, 1)
            dve.tensor_scalar(root[:, :, :], total[:, :, :], 1.0 / (K * P * post * post), EPS / (post * post),
                              ALU.mult, ALU.add).then_inc(meaned, 1)
            dve.wait_ge(rooted, 1)
            chain(dve.reciprocal(rstd[:, :, :], root[:, :, :]))
            for c in range(n_chunks):
                for lo, hi, s in ranges:
                    last = dve.scalar_tensor_tensor(out=value(c)[:, lo:hi], in0=src(c)[:, lo:hi], scalar=scale(c, s),
                                                    in1=rstd[:, c // K, lo:hi], op0=ALU.mult, op1=ALU.mult)
                last.then_inc(scaled, 1)
            if mul is not None:
                for c in range(n_chunks):
                    dve.wait_ge(scaled, c + 1)
                    dve.tensor_tensor(value(c), value(c), mul(c), ALU.mult).then_inc(multiplied, 1)
            if pair is not None:
                for c in range(n_chunks):
                    dve.wait_ge(hi_done, c + 1)
                    for lo, hi, s in ranges:
                        out, high = pair(c)[1][:, lo:hi], pair(c)[0][:, lo:hi].bitcast(F32)
                        if shift is not None:
                            dve.scalar_tensor_tensor(out=out, in0=value(c)[:, lo:hi], scalar=shift(c, s), in1=high,
                                                     op0=ALU.add, op1=ALU.subtract)
                        else:
                            dve.tensor_tensor(out, value(c)[:, lo:hi], high, ALU.subtract)


class Unit:

    def __init__(self, q, k, v, nk, scale, bias=None, sink=None, weight=None, end=True, first=True, out=None):
        self.q, self.k, self.v, self.nk, self.scale = q, k, v, nk, scale
        self.bias, self.sink, self.weight = bias, sink, weight
        self.first, self.end, self.out = first, end, out


def attention(nc, name, units, ident):
    U = len(units)
    width = max(u.nk for u in units)
    B = 1024 // width
    H = B // 2
    steps = U // B
    assert steps * B == U
    group, groups = [], 0
    for u in units:
        group.append(groups)
        groups += u.end

    def batch(s):
        return [(s * B + i, i, units[s * B + i]) for i in range(B)] if 0 <= s < steps else []

    def place(i):
        return (i % 2) * H + i // 2

    with stage(nc, name) as S:
        raw = S.ps("raw", [P, 2, B, width])
        turned = S.ps("turned", [P, B, width])
        out = S.ps("out", [P, 2, 512])
        biased = S.sb("biased", [P, 2, B, width])
        prob = S.sb("prob", [P, 2, B, width])
        probT = S.sb("probT", [P, 2, B, width])
        low, total, inverse, sunk = (S.sb(n, [P, 2, B]) for n in ("low", "total", "inverse", "sunk"))
        scored, shifted, exped, normed, transposed, copied, summed, evacuated, v_ordered, a_ordered = (
            S.sem(n) for n in ("scored", "shifted", "exped", "normed", "transposed", "copied", "summed",
                               "evacuated", "v_ordered", "a_ordered"))
        block = S.block()

        @block.tensor
        def _(pe):
            def scores(s):
                for u, i, x in batch(s):
                    if i == 0 and s >= 2:
                        pe.wait_ge(exped, (s - 1) * B)
                    last = pe.matmul(raw[:, s % 2, place(i), 0:x.nk], x.q, x.k, start=True, stop=True)
                    if i == B - 1:
                        last.then_inc(scored, 1)

            scores(0)
            for s in range(steps + 2):
                scores(s + 1)
                for u, i, x in batch(s - 1):
                    pe.wait_ge(normed, u + 1)
                    if i % H == 0 and s >= 2:
                        pe.wait_ge(copied, u - B + H)
                    for b in range(x.nk // P):
                        last = pe.transpose(turned[:, i, b * P:(b + 1) * P], prob[:, (s - 1) % 2, i, b * P:(b + 1) * P], ident)
                    last.then_inc(transposed, 1)
                for u, i, x in batch(s - 2):
                    pe.wait_ge(copied, u + 1)
                    if x.first and group[u] >= 2:
                        pe.wait_ge(evacuated, group[u] - 1)
                    nb = x.nk // P
                    for b in range(nb):
                        last = pe.matmul(out[:, group[u] % 2, 0:P], x.v(b), probT[:, s % 2, i, b * P:(b + 1) * P],
                                         start=(x.first and b == 0), stop=(x.end and b == nb - 1))
                    last.then_inc(summed, 1)

        @block.vector
        def _(dve):
            chain = Chain(dve, v_ordered)
            for s in range(steps + 1):
                now, b = batch(s), s % 2
                if now:
                    dve.wait_ge(scored, s + 1)
                    for u, i, x in now:
                        if x.bias is not None:
                            last = dve.scalar_tensor_tensor(out=biased[:, b, i, 0:x.nk], in0=raw[:, b, place(i), 0:x.nk],
                                                            scalar=x.scale, in1=x.bias, op0=ALU.mult, op1=ALU.add)
                    if now[0][2].bias is not None:
                        chain(last)
                    for u, i, x in now:
                        src = raw[:, b, place(i), 0:x.nk] if x.bias is None else biased[:, b, i, 0:x.nk]
                        last = dve.tensor_reduce(low[:, b, i:i + 1], src, X_AXIS, ALU.max)
                    chain(last)
                    factor = -1.0 if now[0][2].bias is not None else -now[0][2].scale
                    if now[0][2].sink is None:
                        dve.tensor_scalar(low[:, b, :], low[:, b, :], factor, None, ALU.mult).then_inc(shifted, 1)
                    else:
                        for u, i, x in now:
                            last = dve.tensor_scalar(low[:, b, i:i + 1], low[:, b, i:i + 1], x.sink, factor, ALU.max, ALU.mult)
                        chain(last)
                        for u, i, x in now:
                            last = dve.tensor_tensor(sunk[:, b, i:i + 1], x.sink, low[:, b, i:i + 1], ALU.add)
                        last.then_inc(shifted, 1)
                before, b = batch(s - 1), (s - 1) % 2
                if before:
                    dve.wait_ge(exped, s * B)
                    if before[0][2].sink is not None:
                        chain(dve.tensor_tensor(total[:, b, :], total[:, b, :], sunk[:, b, :], ALU.add))
                    chain(dve.reciprocal(inverse[:, b, :], total[:, b, :]))
                    for u, i, x in before:
                        p, by = prob[:, b, i, 0:x.nk], inverse[:, b, i:i + 1]
                        if x.weight is None:
                            ins = dve.tensor_scalar(p, p, by, None, ALU.mult)
                        else:
                            ins = dve.tensor_scalar(p, p, by, x.weight, ALU.mult, ALU.mult)
                        ins.then_inc(normed, 1)

        @block.scalar
        def _(act):
            chain = Chain(act, a_ordered)
            for s in range(steps + 2):
                for u, i, x in batch(s):
                    if i == 0:
                        act.wait_ge(shifted, s + 1)
                        if s >= 2:
                            act.wait_ge(transposed, (s - 1) * B)
                        if x.sink is not None:
                            chain(act.activation(sunk[:, s % 2, :], sunk[:, s % 2, :], ACT.Exp))
                    src, scale = (raw[:, s % 2, place(i), 0:x.nk], x.scale) if x.bias is None else (biased[:, s % 2, i, 0:x.nk], 1.0)
                    act.activation(prob[:, s % 2, i, 0:x.nk], src, ACT.Exp,
                                   bias=low[:, s % 2, i:i + 1], scale=scale,
                                   accum_out=total[:, s % 2, i:i + 1]).then_inc(exped, 1)
                for u, i, x in batch(s - 1):
                    if i % H == 0:
                        act.wait_ge(transposed, u + H)
                    if i == 0 and s >= 3:
                        act.wait_ge(summed, (s - 2) * B)
                    act.activation(probT[:, (s - 1) % 2, i, 0:x.nk], turned[:, i, 0:x.nk], ACT.Copy).then_inc(copied, 1)
                for u, i, x in batch(s - 2):
                    if x.end:
                        act.wait_ge(summed, u + 1)
                        lo, hi, dst = x.out
                        act.activation(dst, out[lo:hi, group[u] % 2, 0:P], ACT.Copy).then_inc(evacuated, 1)


def feed_forward(nc, W, seg, x, h):
    first = W.take(seg)
    order = [("gate", 0), ("up", 0)]
    for c in range(FC):
        if c + 1 < FC:
            order += [("gate", c + 1), ("up", c + 1)]
        order.append(("down", c))
    end = {key: 2 * (first + i) + 2 for i, key in enumerate(order)}
    with stage(nc, seg) as S:
        acc = S.ps("acc", [P, KD, T])
        gu = S.ps("gu", [P, 2, 2, 512])
        silu = S.sb("silu", [P, 2, T])
        hid = S.sb("hid", [P, T])
        hid_hi = S.sb("hid_hi", [P, 2, T], F32R)
        hid_lo = S.sb("hid_lo", [P, 2, T], F32R)
        silu_done, hidden, ordered = S.sem("silu_done"), S.sem("hidden"), S.sem("ordered")
        block = S.block()

        @block.sync
        def _(sync):
            W.feed(sync, first, 3 * FC)

        @block.tensor
        def _(pe):
            for kind, c in order:
                for part in (end[kind, c] - 2, end[kind, c] - 1):
                    W.wait(pe, part)
                    if kind == "down" and part % 2 == 0:
                        pe.wait_ge(hidden, c + 1)
                    if kind == "gate" and c >= 2 and part % 2 == 0:
                        pe.wait_ge(hidden, c - 1)
                    for i in range(4):
                        n = 4 * (part % 2) + i
                        if kind == "down":
                            last = run_passes(pe, acc[:, n, :],
                                              W.stationary(part, i * P, (hid_hi[:, c % 2, :], hid_lo[:, c % 2, :])),
                                              c == 0 and n % 2 == 0, c == FC - 1, skip_group_check=True)
                        else:
                            j = ("gate", "up").index(kind)
                            last = run_passes(pe, gu[:, c % 2, j, 0:T], W.stationary(part, i * P, x(n)), n == 0, n == KD - 1)
                    last.then_inc(W.used, 1)

        @block.scalar
        def _(act):
            for kind, c in order:
                for part in (end[kind, c] - 2, end[kind, c] - 1):
                    W.next_hi(act, part)
                if kind == "gate":
                    if c >= 2:
                        act.wait_ge(hidden, c - 1)
                    act.activation(silu[:, c % 2, :], gu[:, c % 2, 0, 0:T], ACT.Silu).then_inc(silu_done, 1)

        @block.vector
        def _(dve):
            chain = Chain(dve, ordered)
            for kind, c in order:
                for part in (end[kind, c] - 2, end[kind, c] - 1):
                    W.next_lo(dve, part)
                if kind == "up":
                    dve.wait_ge(W.used, end[kind, c])
                    dve.wait_ge(silu_done, c + 1)
                    chain(dve.tensor_tensor(hid[:, :], silu[:, c % 2, :], gu[:, c % 2, 1, 0:T], ALU.mult))
                    if c >= 2:
                        dve.wait_ge(W.used, end["down", c - 2])
                    chain(dve.tensor_copy(hid_hi[:, c % 2, :], hid[:, :]))
                    dve.tensor_tensor(hid_lo[:, c % 2, :], hid[:, :], hid_hi[:, c % 2, :].bitcast(F32),
                                      ALU.subtract).then_inc(hidden, 1)
                    dve.wait_ge(hidden, c + 1)
            dve.wait_ge(W.used, 2 * (first + 3 * FC))
            for n in range(KD):
                dve.scalar_tensor_tensor(out=h[:, n, 0:T], in0=acc[:, n, :], scalar=0.5, in1=h[:, n, 0:T],
                                         op0=ALU.mult, op1=ALU.add)


def peer_queries(nc, W, name, seg, x, keys_dram, best, index):
    first = W.take(seg)
    with stage(nc, name) as S:
        keys = S.sb("keys", [P, 2 * PH, NKEYS])
        q = S.sb("q", [P, 2, T])
        rest = S.sb("rest", [P, 2, NKEYS])
        acc = S.ps("acc", [P, 2, 512])
        scores = S.ps("scores", [P, 4, 512])
        keys_in, q_out, scored, read, ordered = (S.sem(n) for n in ("keys_in", "q_out", "scored", "read", "ordered"))
        block = S.block()

        @block.sync
        def _(sync):
            sync.dma_start(keys[:, :, :].rearrange("p i k -> p (i k)"), keys_dram).then_inc(keys_in, 16)
            W.feed(sync, first, 2 * PH)

        @block.tensor
        def _(pe):
            def score(c):
                pe.wait_ge(q_out, c + 1)
                if c >= 4:
                    pe.wait_ge(read, c - 3)
                for tt in range(2):
                    last = pe.matmul(scores[:, c % 4, tt * NKEYS:(tt + 1) * NKEYS], q[:, c % 2, tt * P:(tt + 1) * P],
                                     keys[:, c, :], start=True, stop=True)
                last.then_inc(scored, 1)

            for c in range(2 * PH):
                for half in range(2):
                    part = 2 * (first + c) + half
                    W.wait(pe, part)
                    if half == 0 and c >= 2:
                        pe.wait_ge(q_out, c - 1)
                    for k in range(4):
                        last = run_passes(pe, acc[:, c % 2, 0:T], W.stationary(part, k * P, x(4 * half + k)),
                                          half == 0 and k == 0, half == 1 and k == 3)
                    last.then_inc(W.used, 1)
                if c == 0:
                    pe.wait_ge(keys_in, 16)
                else:
                    score(c - 1)
            score(2 * PH - 1)

        @block.scalar
        def _(act):
            for c in range(2 * PH):
                for half in range(2):
                    W.next_hi(act, 2 * (first + c) + half)
                if c >= 2:
                    act.wait_ge(scored, c - 1)
                act.activation(q[:, c % 2, :], acc[:, c % 2, 0:T], ACT.Copy).then_inc(q_out, 1)

        @block.vector
        def _(dve):
            chain = Chain(dve, ordered)
            tiles = range(2)

            def choose(c):
                dve.wait_ge(scored, c + 1)
                sc = [scores[:, c % 4, tt * NKEYS:(tt + 1) * NKEYS] for tt in tiles]
                for tt in tiles:
                    last = dve.max(best[:, tt, c, 0:8], sc[tt])
                chain(last)
                for tt in tiles:
                    dve.match_replace(out=rest[:, tt, :], in_to_replace=best[:, tt, c, 0:8], in_values=sc[tt], imm_value=-3e38)
                for tt in tiles:
                    last = dve.max_index(index[:, tt, c, 0:8], best[:, tt, c, 0:8], sc[tt])
                last.then_inc(read, 1)
                dve.wait_ge(read, c + 1)
                for tt in tiles:
                    last = dve.max(best[:, tt, c, 8:16], rest[:, tt, :])
                chain(last)
                for tt in tiles:
                    last = dve.max_index(index[:, tt, c, 8:16], best[:, tt, c, 8:16], rest[:, tt, :])
                chain(last)

            for c in range(2 * PH):
                for half in range(2):
                    W.next_lo(dve, 2 * (first + c) + half)
                if c >= 2:
                    choose(c - 2)
            for c in (2 * PH - 2, 2 * PH - 1):
                choose(c)


def peer_topk(nc, name, best, index, route, const):
    ident, iota16 = const[:, 0:P], const[:, 3 * P:3 * P + 16]
    HC = PH * TOPK
    with stage(nc, name) as S:
        indexf = S.sb("indexf", [P, 2 * PH, TOPK])
        cand = S.sb("cand", [P, PH, TOPK * TOPK])
        cand2 = S.sb("cand2", [P, PH, TOPK * TOPK])
        top = S.sb("top", [P, PH, TOPK])
        where = S.sb("where", [P, PH, TOPK], U32)
        part = S.sb("part", [P, 2, HC], U32)
        partf = S.sb("partf", [P, 2, HC])
        hit = S.sb("hit", [P, HC, TOPK])
        total = S.sb("total", [P, PH])
        chosen = S.sb("chosen", [P, 2, 3, HC])
        turned = S.ps("turned", [P, 2, 512])
        ordered, exp_in, exped, ready, transposed = (
            S.sem(n) for n in ("ordered", "exp_in", "exped", "ready", "transposed"))
        block = S.block()

        @block.vector
        def _(dve):
            chain = Chain(dve, ordered)
            for tt in range(2):
                dve.tensor_copy(indexf[:, :, :], index[:, tt, :, :])
                halves = best[:, tt, :, :].rearrange("p (h two) a -> p h two a", two=2)
                chain(dve.tensor_tensor(
                    cand[:, :, :].rearrange("p h (a b) -> p h a b", a=TOPK),
                    halves[:, :, 0, :].unsqueeze(3).to_broadcast([P, PH, TOPK, TOPK]),
                    halves[:, :, 1, :].unsqueeze(2).to_broadcast([P, PH, TOPK, TOPK]), ALU.add))
                for h in range(PH):
                    last = dve.max(top[:, h, 0:8], cand[:, h, :])
                chain(last)
                for h in range(PH):
                    dve.match_replace(out=cand2[:, h, :], in_to_replace=top[:, h, 0:8], in_values=cand[:, h, :],
                                      imm_value=-3e38)
                    last = dve.max_index(where[:, h, 0:8], top[:, h, 0:8], cand[:, h, :])
                chain(last)
                for h in range(PH):
                    last = dve.max(top[:, h, 8:16], cand2[:, h, :])
                chain(last)
                for h in range(PH):
                    last = dve.max_index(where[:, h, 8:16], top[:, h, 8:16], cand2[:, h, :])
                chain(last)
                g = chosen[:, tt, 2, :].rearrange("p (h s) -> p h s", h=PH)
                dve.tensor_tensor(g, top[:, :, :], top[:, :, 0:1].to_broadcast([P, PH, TOPK]),
                                  ALU.subtract).then_inc(exp_in, 1)
                flat = where[:, :, :].rearrange("p h s -> p (h s)")
                dve.tensor_scalar(part[:, 0, :], flat, 4, None, ALU.logical_shift_right)
                chain(dve.tensor_scalar(part[:, 1, :], flat, 15, None, ALU.bitwise_and))
                chain(dve.tensor_copy(partf[:, :, :], part[:, :, :]))
                both = indexf[:, :, :].rearrange("p (h two) a -> p h two a", two=2)
                for half in range(2):
                    chain(dve.tensor_tensor(hit[:, :, :], partf[:, half, :].unsqueeze(2).to_broadcast([P, HC, TOPK]),
                                            iota16.unsqueeze(1).to_broadcast([P, HC, TOPK]), ALU.is_equal))
                    hits = hit[:, :, :].rearrange("p (h s) a -> p h s a", h=PH)
                    chain(dve.tensor_tensor(hits, hits, both[:, :, half, :].unsqueeze(2).to_broadcast([P, PH, TOPK, TOPK]),
                                            ALU.mult))
                    chain(dve.tensor_reduce(chosen[:, tt, half, :], hit[:, :, :], X_AXIS, ALU.add))
                dve.wait_ge(exped, tt + 1)
                chain(dve.tensor_reduce(total[:, :], g, X_AXIS, ALU.add))
                chain(dve.reciprocal(total[:, :], total[:, :]))
                dve.tensor_tensor(g, g, total[:, :].unsqueeze(2).to_broadcast([P, PH, TOPK]), ALU.mult).then_inc(ready, 1)
                dve.wait_ge(ready, tt + 1)

        @block.scalar
        def _(act):
            for tt in range(2):
                act.wait_ge(exp_in, tt + 1)
                act.activation(chosen[:, tt, 2, :], chosen[:, tt, 2, :], ACT.Exp).then_inc(exped, 1)
            for tt in range(2):
                act.wait_ge(transposed, tt + 1)
                for j in range(3):
                    act.activation(route[:, j, tt * P:(tt + 1) * P], turned[:, tt, j * P:(j + 1) * P], ACT.Copy)

        @block.tensor
        def _(pe):
            for tt in range(2):
                pe.wait_ge(ready, tt + 1)
                for j in range(3):
                    last = pe.transpose(turned[:, tt, j * P:(j + 1) * P], chosen[:, tt, j, :], ident)
                last.then_inc(transposed, 1)


GROUP = 4
ON_ACT = 1


def peer_spread(nc, name, route, G, const):
    iota, ones = const[:, 2 * P:3 * P], const[:, P:2 * P]
    steps = T // GROUP
    with stage(nc, name) as S:
        cur = S.sb("cur", [P, 2, 3, GROUP])
        first = S.sb("first", [P, 2, GROUP, P])
        second = S.sb("second", [P, 2, GROUP, P])
        product = S.ps("product", [P, 2, GROUP, P])
        apart = S.sb("apart", [P, ON_ACT, P])
        picked, apart_done, act_onehots, onehots, multiplied = (
            S.sem(n) for n in ("picked", "apart_done", "act_onehots", "onehots", "multiplied"))
        block = S.block()

        @block.scalar
        def _(act):
            def pick(b, at):
                act.activation(cur[:, b, :, :], route[:, :, bass.ds(at, GROUP)], ACT.Copy).then_inc(picked, 1)

            def one_hots(b, count):
                act.wait_ge(picked, count)
                for t in range(ON_ACT):
                    last = act.activation(apart[:, t, :], iota, ACT.Abs, bias=cur[:, b, 0, t:t + 1], scale=-1.0)
                last.then_inc(apart_done, 1)
                act.wait_ge(apart_done, count)
                act.activation(first[:, b, 0:ON_ACT, :], apart[:, :, :], ACT.Relu, bias=ones[:, 0:1],
                               scale=-1.0).then_inc(act_onehots, 1)

            def store(at, b, done):
                act.wait_ge(multiplied, done)
                act.activation(G[:, :, bass.ds(at, GROUP)], product[:, b, :, :].rearrange("p t j -> p j t"), ACT.Copy)

            pick(0, 0)
            one_hots(0, 1)
            pick(1, GROUP)
            with act.Fori(0, steps // 2 - 1) as i:
                for b in range(2):
                    one_hots(1 - b, i * 2 + (b + 2))
                    act.wait_ge(onehots, i * 2 + (b + 1))
                    pick(b, i * (2 * GROUP) + (b + 2) * GROUP)
                    store(i * (2 * GROUP) + b * GROUP, b, i * 2 + (b + 1))
            one_hots(1, steps)
            for b in range(2):
                store(T + (b - 2) * GROUP, b, steps - 1 + b)

        @block.vector
        def _(dve):
            others = GROUP - ON_ACT

            def one_hots(b, count):
                dve.wait_ge(picked, count)
                dve.tensor_tensor(first[:, b, ON_ACT:, :], iota.unsqueeze(1).to_broadcast([P, others, P]),
                                  cur[:, b, 0, ON_ACT:].unsqueeze(2).to_broadcast([P, others, P]), ALU.is_equal)
                for t in range(GROUP):
                    last = dve.tensor_scalar(second[:, b, t, :], iota, cur[:, b, 1, t:t + 1], cur[:, b, 2, t:t + 1],
                                             ALU.is_equal, ALU.mult)
                last.then_inc(onehots, 1)

            for b in range(2):
                one_hots(b, b + 1)
            with dve.Fori(1, steps // 2) as i:
                for b in range(2):
                    dve.wait_ge(multiplied, i * 2 + (b - 1))
                    one_hots(b, i * 2 + (b + 1))

        @block.tensor
        def _(pe):
            with pe.Fori(0, steps // 2) as i:
                for b in range(2):
                    pe.wait_ge(onehots, i * 2 + (b + 1))
                    pe.wait_ge(act_onehots, i * 2 + (b + 1))
                    for t in range(GROUP):
                        last = pe.matmul(product[:, b, t, :], first[:, b, t, :], second[:, b, t, :], start=True, stop=True)
                    last.then_inc(multiplied, 1)


def peer_experts(nc, W, seg, x, G, h, gate, work):
    first = W.take(seg)
    turns = (NKEYS - 1) // 2
    assert RING == 4 and PARTS == 4
    with stage(nc, seg) as S:
        acc = S.ps("acc", [P, KD, T])
        dot = S.ps("dot", [P, 2, 512])
        coef_hi = S.sb("coef_hi", [P, 2, T], F32R)
        coef_lo = S.sb("coef_lo", [P, 2, T], F32R)
        zero = S.sb("zero", [P, P])
        zero_r = S.sb("zero_r", [P, P], F32R)
        zeroed, gelued, weighed, high, weighted, finished = (
            S.sem(n) for n in ("zeroed", "gelued", "weighed", "high", "weighted", "finished"))
        block = S.block()

        def parts_used(pos, i):
            return i * (2 * RING) + 2 * (first + pos + 1)

        @block.sync
        def _(sync):
            base = tile_bases()[0][seg] * P
            with sync.Fori(0, PEER_TILES // RING - 1) as i:
                for s in range(RING):
                    sync.wait_ge(W.lo_done, parts_used(s, i))
                    sync.dma_start(W.ring[:, (first + s) % RING, :],
                                   W.sources["peer"][bass.ds(i * (RING * P) + (base + (RING + s) * P), P), :]
                                   ).then_inc(W.arrived[(first + s) % RING], 16)
            W.feed(sync, first + PEER_TILES - RING, RING)

        @block.gpsimd
        def _(pool):
            pool.memset(zero[:, :], 0.0).then_inc(zeroed, 1)

        @block.tensor
        def _(pe):
            def dots(pos, i, j):
                for half in range(2):
                    part = 2 * (first + pos) + half
                    pe.wait_ge(W.lo_done, parts_used(pos, i) - 1 + half)
                    for k in range(4):
                        last = run_passes(pe, dot[:, j % 2, 0:T], W.stationary(part, k * P, x(4 * half + k)),
                                          half == 0 and k == 0, half == 1 and k == 3)
                    last.then_inc(W.used, 1)

            def sums(pos, i, j, count):
                pe.wait_ge(weighted, count)
                for half in range(2):
                    part = 2 * (first + pos) + half
                    pe.wait_ge(W.lo_done, parts_used(pos, i) - 1 + half)
                    for n in range(4):
                        last = run_passes(pe, acc[:, 4 * half + n, :],
                                          W.stationary(part, n * P, (coef_hi[:, j % 2, :], coef_lo[:, j % 2, :])),
                                          False, False, skip_group_check=True)
                    last.then_inc(W.used, 1)

            def zeros(start, stop):
                for n in range(KD):
                    last = pe.matmul(acc[:, n, :], zero_r[:, :], x(0)[0], start=start and n % 2 == 0, stop=stop,
                                     skip_group_check=True)
                return last

            pe.wait_ge(zeroed, 2)
            zeros(True, False)
            dots(0, 0, 0)
            with pe.Fori(0, turns) as i:
                for q in range(2):
                    dots(2 * q + 1, i, q + 1)
                    sums(2 * q + 2, i, q, i * 2 + (q + 1))
            for j in range(turns * 2, NKEYS):
                if j + 1 < NKEYS:
                    dots(2 * j + 1, 0, j + 1)
                    sums(2 * j + 2, 0, j, j + 1)
                else:
                    sums(2 * j + 1, 0, j, j + 1)
            zeros(False, True).then_inc(finished, 1)

        @block.scalar
        def _(act):
            def next_parts(pos, i):
                slot = (first + pos + 2) % RING
                act.wait_ge(W.arrived[slot], i * 16 + 16 * ((first + pos + 2) // RING + 1))
                for half in range(2):
                    act.wait_ge(W.used, parts_used(pos, i) - 1 + half)
                    act.activation(W.hi[:, (2 * (first + pos) + half) % PARTS, :],
                                   W.ring[:, slot, half * PART:(half + 1) * PART], ACT.Copy).then_inc(W.hi_done, 1)

            def gelu(b, pos, i):
                act.wait_ge(W.used, parts_used(pos, i))
                act.activation(work[:, b, :], dot[:, b, 0:T], ACT.Gelu).then_inc(gelued, 1)

            next_parts(0, 0)
            gelu(0, 0, 0)
            with act.Fori(0, turns) as i:
                for q in range(2):
                    next_parts(2 * q + 1, i)
                    gelu(1 - q, 2 * q + 1, i)
                    next_parts(2 * q + 2, i)
            for j in range(turns * 2, NKEYS):
                next_parts(2 * j + 1, 0)
                if j + 1 < NKEYS:
                    gelu((j + 1) % 2, 2 * j + 1, 0)
                    next_parts(2 * j + 2, 0)

        @block.vector
        def _(dve):
            def next_parts(pos, i):
                slot = (first + pos + 2) % RING
                for half in range(2):
                    b = (2 * (first + pos) + half) % PARTS
                    dve.wait_ge(W.hi_done, parts_used(pos, i) + 3 + half)
                    dve.tensor_tensor(W.lo[:, b, :], W.ring[:, slot, half * PART:(half + 1) * PART],
                                      W.hi[:, b, :].bitcast(F32), ALU.subtract).then_inc(W.lo_done, 1)

            def weigh(b, j, count):
                dve.wait_ge(gelued, count)
                dve.tensor_tensor(work[:, 2, :], work[:, b, :], G[:, bass.ds(j, 1), :].rearrange("p o t -> p (o t)"),
                                  ALU.mult).then_inc(weighed, 1)
                dve.wait_ge(weighed, count)
                dve.tensor_copy(coef_hi[:, b, :], work[:, 2, :]).then_inc(high, 1)
                dve.wait_ge(high, count)
                dve.tensor_tensor(coef_lo[:, b, :], work[:, 2, :], coef_hi[:, b, :].bitcast(F32),
                                  ALU.subtract).then_inc(weighted, 1)
                dve.wait_ge(weighted, count)

            dve.wait_ge(zeroed, 1)
            dve.tensor_copy(zero_r[:, :], zero[:, :]).then_inc(zeroed, 1)
            next_parts(0, 0)
            weigh(0, 0, 1)
            with dve.Fori(0, turns) as i:
                for q in range(2):
                    next_parts(2 * q + 1, i)
                    weigh(1 - q, i * 2 + (q + 1), i * 2 + (q + 2))
                    next_parts(2 * q + 2, i)
            for j in range(turns * 2, NKEYS):
                next_parts(2 * j + 1, 0)
                if j + 1 < NKEYS:
                    weigh((j + 1) % 2, j + 1, j + 2)
                    next_parts(2 * j + 2, 0)
            dve.wait_ge(finished, 1)
            for n in range(KD):
                dve.scalar_tensor_tensor(out=h[:, n, :], in0=acc[:, n, :], scalar=gate(n), in1=h[:, n, :],
                                         op0=ALU.mult, op1=ALU.add)


def peer(nc, W, layer, stream, h, scale, shift, gate, const, dram):
    name = "peer%d%d" % (layer, stream)
    with nc.sbuf_tensor(name + "_xh", [P, KD, T], F32R) as x_hi, nc.sbuf_tensor(name + "_xl", [P, KD, T], F32R) as x_lo, \
            nc.sbuf_tensor(name + "_route", [P, 3, T], F32) as route:
        x = split_pair(x_hi, x_lo)
        norm(nc, name + "n", lambda c: h[:, c, :], None, KD, T, const[:, P:2 * P],
             lambda c, s: scale(c), shift=lambda c, s: shift(c), pair=x)
        with nc.sbuf_tensor(name + "_best", [P, 2, 2 * PH, TOPK], F32) as best, \
                nc.sbuf_tensor(name + "_index", [P, 2, 2 * PH, TOPK], U32) as index:
            peer_queries(nc, W, name + "q", "peer_q%d" % layer, x, dram["subkeys%d" % layer], best, index)
            peer_topk(nc, name + "t", best, index, route, const)
        with nc.sbuf_tensor(name + "_G", [P, NKEYS, T], F32) as G:
            peer_spread(nc, name + "g", route, G, const)
            peer_experts(nc, W, "experts%d" % layer, x, G, h, gate, route)


def even_mixer(nc, W, h, modulation, scales, cols, const, rope_dram):
    TT = 2 * T
    ones, ident = const[:, P:2 * P], const[:, 0:P]
    streams = [(0, T, LAT), (T, TT, CTX)]
    with ExitStack() as ctx:
        def sb(name, shape):
            return ctx.enter_context(nc.sbuf_tensor("even_" + name, shape, F32))

        mix = sb("mix", [P, KD, TT])
        with ExitStack() as inner:
            def tmp_sb(name, shape, dt=F32):
                return inner.enter_context(nc.sbuf_tensor("even_" + name, shape, dt))

            pq = tmp_sb("pq", [P, 2, TT])
            pkv = tmp_sb("pkv", [P, TT])
            kr = tmp_sb("kr", [P, TT])
            rope = tmp_sb("rope", [P, TT])
            with nc.sbuf_tensor("even_xh", [P, KD, TT], F32R) as x_hi, nc.sbuf_tensor("even_xl", [P, KD, TT], F32R) as x_lo:
                x = split_pair(x_hi, x_lo)
                norm(nc, "even_n", lambda c: h[:, c, :], None, KD, TT, ones,
                     lambda c, s: scales[:, 0, 0, s, c:c + 1], ranges=streams,
                     shift=lambda c, s: modulation[:, 0, c, s:s + 1], pair=x)
                first = W.take("even_in")
                with nc.sbuf_tensor("even_c", [P, TT], F32) as c_gate, nc.sbuf_tensor("even_z", [P, 2, T + 2], F32) as z, \
                        nc.sbuf_tensor("even_y", [P, 2, T], F32) as y, nc.sbuf_tensor("even_t", [P, TT], F32) as turn:
                    def prepare(dve, chain):
                        chain(dve.memset(z[:, :, :], 0.0))

                    def evacuate(dve, chain, c, ps):
                        if c < 2:
                            return dve.tensor_copy(pq[:, c, :], ps)
                        if c == 2:
                            return dve.tensor_copy(pkv[:, :], ps)
                        if c == 3:
                            chain(dve.tensor_tensor(turn[64:96, :], ps[96:128, :], rope[96:128, :], ALU.mult))
                            chain(dve.tensor_tensor(kr[64:96, :], ps[64:96, :], rope[64:96, :], ALU.mult))
                            return dve.tensor_tensor(kr[64:96, :], kr[64:96, :], turn[64:96, :], ALU.add)
                        j, kind = (c - 4) // 3, (c - 4) % 3
                        two = ps.rearrange("p (s t) -> p s t", s=2)
                        if kind == 0:
                            return dve.tensor_copy(c_gate[:, :], ps)
                        if kind == 1:
                            dve.wait_ge(*done_before(c))
                            return dve.tensor_tensor(z[:, :, 1:T + 1], two,
                                                     c_gate[:, :].rearrange("p (s t) -> p s t", s=2), ALU.mult)

                        def tap(i):
                            at = col_at("conv") + 4 * i + j
                            return cols[:, at:at + 1]

                        dve.wait_ge(*done_before(c))
                        chain(dve.tensor_scalar(y[:, :, :], z[:, :, 0:T], tap(0), None, ALU.mult))
                        for i in (1, 2):
                            chain(dve.scalar_tensor_tensor(out=y[:, :, :], in0=z[:, :, i:T + i], scalar=tap(i),
                                                           in1=y[:, :, :], op0=ALU.mult, op1=ALU.add))
                        return dve.tensor_tensor(mix[:, 4 + j, :].rearrange("p (s t) -> p s t", s=2), two, y[:, :, :],
                                                 ALU.mult)

                    done = []

                    def done_before(c):
                        return done[0], c

                    products(nc, W, "even_in", first, 16, column_jobs(W, first, 16, KD, TT, x),
                             evacuate, "vector", prepare=prepare, const_load=[(rope[:, :], rope_dram)],
                             evacuated_out=done)

            q = tmp_sb("q", [P, MLA_HEADS, TT])
            k = tmp_sb("k", [P, MLA_HEADS, TT])
            v = tmp_sb("v", [P, 4, 512])
            q_hi, q_lo = (tmp_sb("q_" + n, [P, 2, TT], F32R) for n in ("hi", "lo"))
            kv_hi, kv_lo = (tmp_sb("kv_" + n, [P, TT], F32R) for n in ("hi", "lo"))
            at = col_at("q_norm")
            norm(nc, "even_qn", lambda c: pq[:, c, :], None, 2, TT, ones,
                 lambda c, s: cols[:, at + c:at + c + 1], pair=split_pair(q_hi, q_lo))
            at_kv = col_at("kv_norm")
            norm(nc, "even_kvn", lambda c: pkv[:, :], None, 1, TT, ones,
                 lambda c, s: cols[:, at_kv:at_kv + 1], pair=lambda c: (kv_hi[:, :], kv_lo[:, :]))
            first = W.take("uq")
            with nc.sbuf_tensor("even_t2", [P, 2, TT], F32) as turn:
                def rotate(dve, chain, c, ps):
                    chain(dve.tensor_tensor(turn[64:96, c % 2, :], ps[96:128, :], rope[96:128, :], ALU.mult))
                    chain(dve.tensor_tensor(q[64:96, c, :], ps[64:96, :], rope[64:96, :], ALU.mult))
                    dve.tensor_copy(q[0:64, c, :], ps[0:64, :])
                    return dve.tensor_tensor(q[64:96, c, :], q[64:96, c, :], turn[64:96, c % 2, :], ALU.add)

                products(nc, W, "even_uq", first, 2, column_jobs(W, first, MLA_HEADS, 2, TT, split_pair(q_hi, q_lo)),
                         rotate, "vector")
            first = W.take("ukv")
            jobs = [Job([((0, TT), 2 * first, W.stationary(2 * first, j * P, (kv_hi[:, :], kv_lo[:, :])), True, True)])
                    for j in range(MLA_HEADS // 2)]
            for tt in range(4):
                tok = slice(tt * P, (tt + 1) * P)
                jobs.append(Job([((0, 512), 2 * first + 1, W.moving(2 * first + 1, (kv_hi[:, tok], kv_lo[:, tok])),
                                  True, True)]))

            def keys_values(dve, chain, c, ps):
                if c >= MLA_HEADS // 2:
                    return dve.tensor_copy(v[:, c - MLA_HEADS // 2, :], ps)
                for head in (2 * c, 2 * c + 1):
                    dve.tensor_copy(k[64:96, head, :], kr[64:96, :])
                dve.tensor_copy(k[0:64, 2 * c, :], ps[0:64, :])
                return dve.tensor_copy(k[0:64, 2 * c + 1, :], ps[64:128, :])

            products(nc, W, "even_ukv", first, 1, jobs, keys_values, "vector")
            units = []
            for tiles in ((0, 1), (2, 3)):
                for head, tt in ((head, tt) for head in range(MLA_HEADS) for tt in tiles):
                    lo = 0 if tt < 2 else 2
                    units.append(Unit(
                        q[0:96, head, tt * P:(tt + 1) * P], k[0:96, head, lo * P:TT],
                        lambda b, head=head, lo=lo: v[:, lo + b, (head // 2) * P:(head // 2 + 1) * P],
                        (4 - lo) * P, MLA_SCALE,
                        out=(64 * (head % 2), 64 * (head % 2) + 64,
                             mix[64 * (head % 2):64 * (head % 2) + 64, head // 2, tt * P:(tt + 1) * P])))
            attention(nc, "mla", units, ident)
        first = W.take("even_out")

        def residual(dve, chain, c, ps):
            for lo, hi, s in streams:
                last = dve.scalar_tensor_tensor(out=h[:, c, lo:hi], in0=ps[:, lo:hi], scalar=modulation[:, 0, 16 + c, s:s + 1],
                                                in1=h[:, c, lo:hi], op0=ALU.mult, op1=ALU.add)
            return last

        with nc.sbuf_tensor("mix_hi", [P, KD, TT], F32R) as mix_hi, nc.sbuf_tensor("mix_lo", [P, KD, TT], F32R) as mix_lo:
            split_stage(nc, "mix", *(b[:, :, :].rearrange("p k t -> p (k t)") for b in (mix, mix_hi, mix_lo)))
            products(nc, W, "even_out", first, 8, column_jobs(W, first, 8, KD, TT, split_pair(mix_hi, mix_lo)),
                     residual, "vector")


def mlstm(nc, name, gx, q, k, v, out, const, sel_dram, mask_dram):
    TT = 2 * T
    ident = const[:, 0:P]
    with stage(nc, name) as S:
        F = S.sb("F", [P, TT])
        r = S.sb("r", [P, TT])
        M = S.sb("M", [P, TT])
        neg_m = S.sb("neg_m", [P, TT])
        sel = S.sb("sel", [P, ML_HEADS, P])
        mask = S.sb("mask", [P, 2, 2, T])
        colM = S.sb("colM", [P, 2, P])
        guard = S.sb("guard", [P, 2, P])
        s_sb = S.sb("scores", [P, 2, TT])
        w = S.sb("w", [P, 2, 2, TT])
        sc = S.sb("sc", [P, 2, TT])
        den = S.sb("den", [P, 2, 2])
        scT = S.sb("scT", [P, 4, P])
        raw = S.ps("raw", [P, TT])
        row = S.ps("row", [P, 2, TT])
        turned = S.ps("turned", [P, 2, 512])
        o = S.ps("o", [P, 2, 512])
        (loaded, rows_ready, cols_done, guarded, scored, scores_out, row_done, shifted, exped, masked, combined,
         transposed, copied, summed, evacuated, ordered, cols_out) = (
            S.sem(n) for n in ("loaded", "rows_ready", "cols_done", "guarded", "scored", "scores_out", "row_done",
                               "shifted", "exped", "masked", "combined", "transposed", "copied", "summed",
                               "evacuated", "ordered", "cols_out"))
        steps = [(head, tt) for head in range(ML_HEADS) for tt in range(2)]
        lanes = (slice(32, 36), slice(96, 100))
        block = S.block()

        @block.sync
        def _(sync):
            sync.dma_start(sel[:, :, :].rearrange("p h m -> p (h m)"), sel_dram).then_inc(loaded, 16)
            sync.dma_start(mask[:, :, :, :].rearrange("p a b t -> p (a b t)"), mask_dram).then_inc(loaded, 16)

        @block.gpsimd
        def _(pool):
            pool.wait_ge(loaded, 32)
            for n, (head, tt) in enumerate(steps):
                for d in range(2):
                    pool.wait_ge(exped, 2 * n + d + 1)
                    pool.tensor_tensor(w[:, n % 2, d, 0:T], w[:, n % 2, d, 0:T], mask[:, d, tt, :], ALU.mult).then_inc(masked, 1)

        @block.vector
        def _(dve):
            chain = Chain(dve, ordered)
            for buf in (F, r, M):
                last = dve.memset(buf[:, :], 0.0)
            chain(last)
            for d, lane in enumerate(lanes):
                src = slice(64 * d, 64 * d + 4)
                dve.tensor_copy(r[lane, :], gx[src, :])
                if d == 0:
                    one, two = slice(T, TT), slice(0, T)
                    ends = (TT - 1, T - 1)
                else:
                    one, two = slice(TT - 1, T - 1, -1), slice(T - 1, None, -1)
                    ends = (T, 0)
                chain(dve.tensor_tensor_scan(F[lane, one], gx[lane, one], gx[lane, one], 0.0, ALU.add, ALU.bypass))
                chain(dve.tensor_tensor_scan(F[lane, two], gx[lane, two], gx[lane, two],
                                             F[lane, ends[0]:ends[0] + 1], ALU.add, ALU.bypass))
                chain(dve.tensor_tensor(r[lane, :], r[lane, :], F[lane, :], ALU.subtract))
                chain(dve.tensor_tensor_scan(M[lane, one], r[lane, one], r[lane, one], 0.0, ALU.max, ALU.bypass))
                chain(dve.tensor_tensor_scan(M[lane, two], r[lane, two], r[lane, two],
                                             M[lane, ends[0]:ends[0] + 1], ALU.max, ALU.bypass))
            dve.scalar_tensor_tensor(out=neg_m[:, :], in0=F[:, :], scalar=-1.0, in1=M[:, :],
                                     op0=ALU.mult, op1=ALU.subtract).then_inc(rows_ready, 1)
            dve.wait_ge(cols_done, 1)
            dve.tensor_copy(colM[:, :, :], turned[:, 0, 0:2 * P].rearrange("p (a b) -> p a b", a=2)).then_inc(cols_out, 1)
            dve.wait_ge(cols_out, 1)
            dve.wait_ge(guarded, 1)

            def shift(n):
                head, tt = steps[n]
                for d in range(2):
                    lane = 32 + 64 * d + head
                    dve.wait_ge(row_done, 2 * n + d + 1)
                    if n >= 2:
                        dve.wait_ge(combined, n - 1)
                    dve.tensor_scalar(w[:, n % 2, d, :], row[:, d, :], colM[:, tt, lane:lane + 1], 0.0,
                                      ALU.subtract, ALU.min).then_inc(shifted, 1)

            shift(0)
            for n, (head, tt) in enumerate(steps):
                if n + 1 < len(steps):
                    shift(n + 1)
                if n >= 1:
                    dve.wait_ge(transposed, n)
                dve.wait_ge(scores_out, n + 1)
                for d in range(2):
                    lane = 32 + 64 * d + head
                    dve.wait_ge(masked, 2 * n + d + 1)
                    chain(dve.tensor_tensor_reduce(sc[:, d, :], w[:, n % 2, d, :], s_sb[:, n % 2, :], 1.0, 0.0, ALU.mult, ALU.add,
                                                   den[:, d, 0:1]))
                    chain(dve.tensor_scalar(den[:, d, 1:2], den[:, d, 0:1], -1.0, den[:, d, 0:1], ALU.mult, ALU.max))
                    chain(dve.tensor_tensor(den[:, d, 1:2], den[:, d, 1:2], guard[:, tt, lane:lane + 1], ALU.max))
                    chain(dve.reciprocal(den[:, d, 1:2], den[:, d, 1:2]))
                chain(dve.tensor_scalar(sc[:, 0, :], sc[:, 0, :], den[:, 0, 1:2], None, ALU.mult))
                dve.scalar_tensor_tensor(out=sc[:, 1, :], in0=sc[:, 1, :], scalar=den[:, 1, 1:2], in1=sc[:, 0, :],
                                         op0=ALU.mult, op1=ALU.add).then_inc(combined, 1)

        @block.tensor
        def _(pe):
            pe.wait_ge(rows_ready, 1)
            for tt in range(2):
                pe.transpose(turned[:, 0, tt * P:(tt + 1) * P], M[:, tt * P:(tt + 1) * P], ident)
                last = pe.transpose(turned[:, 1, tt * P:(tt + 1) * P], neg_m[:, tt * P:(tt + 1) * P], ident)
            last.then_inc(cols_done, 1)
            pe.wait_ge(loaded, 32)

            def score(n):
                head, tt = steps[n]
                if n:
                    pe.wait_ge(scores_out, n)
                pe.matmul(raw[:, :], q[:, head, tt * P:(tt + 1) * P], k[:, head, :], start=True, stop=True).then_inc(scored, 1)
                for d, lane in enumerate(lanes):
                    if n:
                        pe.wait_ge(shifted, 2 * (n - 1) + d + 1)
                    pe.matmul(row[:, d, :], sel[lane, head, :], r[lane, :], start=True, stop=True,
                              tile_position=(lane.start, 0)).then_inc(row_done, 1)

            score(0)
            score(1)
            for n, (head, tt) in enumerate(steps):
                pe.wait_ge(combined, n + 1)
                if n == 0:
                    pe.wait_ge(cols_out, 1)
                    pe.wait_ge(guarded, 1)
                if n >= 2:
                    pe.wait_ge(copied, n - 1)
                for b in range(4):
                    last = pe.transpose(turned[:, n % 2, b * P:(b + 1) * P], sc[:, 1, b * P:(b + 1) * P], ident)
                last.then_inc(transposed, 1)
                if n + 2 < len(steps):
                    score(n + 2)
                pe.wait_ge(copied, n + 1)
                if n >= 2:
                    pe.wait_ge(evacuated, n - 1)
                for c in range(2):
                    for b in range(4):
                        at = head * ML_DV + c * P
                        last = pe.matmul(o[:, n % 2, c * P:(c + 1) * P], v[:, b, at:at + P], scT[:, b, :],
                                         start=(b == 0), stop=(b == 3))
                last.then_inc(summed, 1)

        @block.scalar
        def _(act):
            act.wait_ge(cols_done, 1)
            act.activation(guard[:, :, :], turned[:, 1, 0:2 * P].rearrange("p (a b) -> p a b", a=2),
                           ACT.Exp).then_inc(guarded, 1)

            def weigh(n):
                act.wait_ge(scored, n + 1)
                if n >= 2:
                    act.wait_ge(combined, n - 1)
                act.activation(s_sb[:, n % 2, :], raw[:, :], ACT.Copy, scale=ML_SCALE).then_inc(scores_out, 1)
                for d in range(2):
                    act.wait_ge(shifted, 2 * n + d + 1)
                    act.activation(w[:, n % 2, d, :], w[:, n % 2, d, :], ACT.Exp).then_inc(exped, 1)

            weigh(0)
            for n, (head, tt) in enumerate(steps):
                if n + 1 < len(steps):
                    weigh(n + 1)
                act.wait_ge(transposed, n + 1)
                if n:
                    act.wait_ge(summed, n)
                act.activation(scT[:, :, :].rearrange("p b t -> p (b t)"), turned[:, n % 2, :], ACT.Copy).then_inc(copied, 1)
                act.wait_ge(summed, n + 1)
                act.activation(out[:, 2 * head:2 * head + 2, tt * P:(tt + 1) * P],
                               o[:, n % 2, 0:2 * P].rearrange("p (c t) -> p c t", c=2), ACT.Copy).then_inc(evacuated, 1)


def log_forget(nc, name, gx):
    with stage(nc, name) as S:
        e = S.sb("e", [P, 2 * T])
        mn = S.sb("mn", [P, 2 * T])
        exped, plus, ln_done = S.sem("exped"), S.sem("plus"), S.sem("ln_done")
        a_ordered = S.sem("a_ordered")
        block = S.block()

        @block.scalar
        def _(act):
            chain = Chain(act, a_ordered)
            chain(act.activation(e[:, :], gx[:, :], ACT.Abs))
            act.activation(e[:, :], e[:, :], ACT.Exp, scale=-1.0).then_inc(exped, 1)
            act.wait_ge(plus, 1)
            act.activation(e[:, :], e[:, :], ACT.Ln).then_inc(ln_done, 1)

        @block.vector
        def _(dve):
            dve.wait_ge(exped, 1)
            dve.tensor_scalar(mn[:, :], gx[:, :], 0.0, None, ALU.min)
            dve.tensor_scalar(e[:, :], e[:, :], 1.0, None, ALU.add).then_inc(plus, 1)
            dve.wait_ge(plus, 1)
            dve.wait_ge(ln_done, 1)
            for lo in (32, 96):
                dve.tensor_tensor(gx[lo:lo + 4, :], mn[lo:lo + 4, :], e[lo:lo + 4, :], ALU.subtract)


def odd_mixer(nc, W, h, modulation, scales, cols, const, sel_dram, mask_dram):
    TT = 2 * T
    ones = const[:, P:2 * P]
    with ExitStack() as ctx:
        def sb(name, shape):
            return ctx.enter_context(nc.sbuf_tensor("odd_" + name, shape, F32))

        gate = sb("gate", [P, KD, T])
        y = sb("y", [P, KD, T])
        y_hi, y_lo = (ctx.enter_context(nc.sbuf_tensor("odd_y_" + n, [P, KD, T], F32R)) for n in ("hi", "lo"))
        with ExitStack() as inner:
            def tmp_sb(name, shape):
                return inner.enter_context(nc.sbuf_tensor("odd_" + name, shape, F32))

            x_hi, x_lo = (inner.enter_context(nc.sbuf_tensor("odd_x_" + n, [P, KD, TT], F32R)) for n in ("hi", "lo"))
            x = split_pair(x_hi, x_lo)
            q = tmp_sb("q", [P, ML_HEADS, T])
            k = tmp_sb("k", [P, ML_HEADS, TT])
            v = tmp_sb("v", [P, 4, 1024])
            gx = tmp_sb("gx", [P, TT])
            norm(nc, "odd_n", lambda c: h[:, c, :], None, KD, TT, ones,
                 lambda c, s: scales[:, 1, 0, s, c:c + 1], ranges=[(0, T, LAT), (T, TT, CTX)],
                 shift=lambda c, s: modulation[:, 1, c, s:s + 1], pair=x)
            x_lat = split_pair(x_hi[:, :, 0:T], x_lo[:, :, 0:T])
            first = W.take("odd_qk")
            at = col_at("gate_b")

            def heads(act, chain, c, ps):
                if c < 4:
                    return act.activation(q[:, c, :], ps[:, 0:T], ACT.Copy)
                if c < 8:
                    return act.activation(k[:, c - 4, :], ps[:, :], ACT.Copy)
                return act.activation(gx[:, :], ps[:, :], ACT.Identity, bias=cols[:, at:at + 1])

            jobs = column_jobs(W, first, 4, KD, T, x_lat)
            jobs += column_jobs(W, first + 4, 5, KD, TT, x)
            products(nc, W, "odd_qk", first, 9, jobs, heads, "scalar")
            log_forget(nc, "odd_lf", gx)
            first = W.take("odd_v")
            row_products(nc, W, "odd_v", first, 2, lambda kk, tt: (x_hi[:, kk, tt * P:(tt + 1) * P], x_lo[:, kk, tt * P:(tt + 1) * P]), 4,
                         lambda act, half, tt, ps: act.activation(v[:, tt, half * 512:(half + 1) * 512], ps, ACT.Copy))
            first = W.take("odd_gate")
            products(nc, W, "odd_g", first, 8, column_jobs(W, first, 8, KD, T, x_lat),
                     lambda act, chain, c, ps: act.activation(gate[:, c, :], ps[:, 0:T], ACT.Sigmoid), "scalar")
            mlstm(nc, "mlstm", gx, q, k, v, y, const, sel_dram, mask_dram)
        at_g = col_at("head_g")
        norm(nc, "odd_hn", lambda c: y[:, c, :], None, 2, T, ones,
             lambda c, s: cols[:, at_g + c:at_g + c + 1], groups=ML_HEADS, mul=lambda c: gate[:, c, :],
             pair=split_pair(y_hi, y_lo))
        first = W.take("odd_out")
        products(nc, W, "odd_out", first, 8, column_jobs(W, first, 8, KD, T, split_pair(y_hi, y_lo)),
                 lambda dve, chain, c, ps: dve.scalar_tensor_tensor(
                     out=h[:, c, 0:T], in0=ps[:, 0:T], scalar=modulation[:, 1, 16 + c, LAT:LAT + 1],
                     in1=h[:, c, 0:T], op0=ALU.mult, op1=ALU.add), "vector")


def modulation_stage(nc, W, h, modulation, scales, cols, const, dram):
    first = W.take("mod")
    blocks = 24
    with stage(nc, "mod") as S:
        c_in = S.sb("c", [P, KD, 2])
        c_act = S.sb("c_act", [P, KD, 2])
        zero = S.sb("zero", [P, KD, P])
        c_hi = S.sb("c_hi", [P, KD, P], F32R)
        c_lo = S.sb("c_lo", [P, KD, P], F32R)
        row = S.sb("row", [2, 2, 512])
        acc = S.ps("acc", [P, 2, 512])
        turned = S.ps("turned", [P, 2 * 96])
        loaded, silu_done, ordered, h_loaded, c_split, row_out, turned_done, zeroed = (
            S.sem(n) for n in ("loaded", "silu_done", "ordered", "h_loaded", "c_split", "row_out", "turned_done", "zeroed"))
        block = S.block()

        @block.sync
        def _(sync):
            W.prime(sync)
            W.feed(sync, first, 96)

        @block.scalar
        def _(act):
            act.dma_start(c_in[:, :, :].rearrange("p k s -> p (k s)"), dram["c_cols"]).then_inc(loaded, 16)
            act.dma_start(cols[:, :], dram["cols"]).then_inc(loaded, 16)
            act.dma_start(const[:, :], dram["const"]).then_inc(loaded, 16)
            act.dma_start(h[:, :, :].rearrange("p k t -> p (k t)"), dram["tokens"]).then_inc(h_loaded, 16)
            act.wait_ge(loaded, 48)
            act.activation(c_act[:, :, :], c_in[:, :, :], ACT.Silu).then_inc(silu_done, 1)
            for part in range(PARTS):
                W.write_hi(act, part)
            for b in range(blocks):
                for k in range(KD):
                    W.next_hi(act, 2 * first + KD * b + k)
                if b >= 2:
                    act.wait_ge(turned_done, b - 1)
                act.activation(row[:, b % 2, :], acc[0:2, b % 2, :], ACT.Copy).then_inc(row_out, 1)
            act.wait_ge(h_loaded, 16)

        @block.gpsimd
        def _(pool):
            pool.memset(zero[:, :, :], 0.0).then_inc(zeroed, 1)

        @block.tensor
        def _(pe):
            pe.wait_ge(c_split, 1)

            def turn(b):
                pe.wait_ge(row_out, b + 1)
                for j in range(4):
                    at = 2 * (4 * b + j)
                    last = pe.transpose(turned[:, at:at + 2], row[:, b % 2, j * P:(j + 1) * P], const[0:2, 0:2])
                last.then_inc(turned_done, 1)

            for b in range(blocks):
                if b >= 2:
                    pe.wait_ge(row_out, b - 1)
                for k in range(KD):
                    part = 2 * first + KD * b + k
                    W.wait(pe, part)
                    run_passes(pe, acc[:, b % 2, :], W.moving(part, (c_hi[:, k, :], c_lo[:, k, :])), k == 0,
                               k == KD - 1).then_inc(W.used, 1)
                if b >= 1:
                    turn(b - 1)
            turn(blocks - 1)

        @block.vector
        def _(dve):
            chain = Chain(dve, ordered)
            dve.wait_ge(loaded, 48)
            dve.wait_ge(zeroed, 1)
            dve.tensor_copy(c_hi[:, :, :], zero[:, :, :])
            chain(dve.tensor_copy(c_lo[:, :, :], zero[:, :, :]))
            dve.wait_ge(silu_done, 1)
            chain(dve.tensor_copy(c_hi[:, :, 0:2], c_act[:, :, :]))
            dve.tensor_tensor(c_lo[:, :, 0:2], c_act[:, :, :], c_hi[:, :, 0:2].bitcast(F32), ALU.subtract).then_inc(c_split, 1)
            for part in range(PARTS):
                W.write_lo(dve, part)
            for part in range(2 * 96):
                W.next_lo(dve, 2 * first + part)
            dve.wait_ge(turned_done, blocks)
            at = col_at("b_mod")
            chain(dve.tensor_tensor(modulation[:, :, :, :], turned[:, :].rearrange("p (l c s) -> p l c s", l=2, s=2),
                                    cols[:, at:at + 96].rearrange("p (l c) -> p l c", l=2).unsqueeze(3)
                                    .to_broadcast([P, 2, 48, 2]), ALU.add))
            for layer in range(2):
                for n in range(2):
                    at = col_at("norm%d" % (n + 1)) + 8 * layer
                    for s in range(2):
                        lo = 8 + 24 * n
                        dve.scalar_tensor_tensor(out=scales[:, layer, n, s, :], in0=modulation[:, layer, lo:lo + 8, s],
                                                 scalar=1.0, in1=cols[:, at:at + 8], op0=ALU.add, op1=ALU.mult)


C_HEAD0, B_HEAD0 = 12, 4


def bias_stage(nc, bias, cmp_bias, neg_lam, cols, dram):
    with stage(nc, "bias") as S:
        onehot = S.sb("onehot", [34, 512])
        table = S.sb("table", [34, N_BIAS])
        exchange = S.sb("exchange", [P, P])
        line = S.sb("line", [N_BIAS, 512])
        shifted = S.sb("shifted", [P, N_BIAS, T])
        scratch = nc.dram_tensor("bias_lines", (N_BIAS, 512), F32)
        acc = S.ps("acc", [P, 4, 2, T])
        line_acc = S.ps("line_acc", [N_BIAS, 512])
        prod = S.sb("prod", [P, 2, 2, 64])
        dots = S.sb("dots", [P, 2, 2])
        loaded, exchange_in, cols_loaded, lined, line_out, stored, back, filled, copied, ordered, dotted, exped = (
            S.sem(n) for n in ("loaded", "exchange_in", "cols_loaded", "lined", "line_out", "stored", "back", "filled",
                               "copied", "ordered", "dotted", "exped"))
        pairs = N_BIAS // 2
        block = S.block()

        @block.sync
        def _(sync):
            sync.dma_start(onehot[:, :], dram["onehot"]).then_inc(loaded, 16)
            sync.dma_start(table[0:32, :], dram["rel_bias"]).then_inc(loaded, 16)
            sync.dma_start(table[32:34, :], dram["masked"]).then_inc(loaded, 16)
            sync.dma_start(cols[:, :], dram["cols2"]).then_inc(cols_loaded, 16)
            sync.dma_start(exchange[:, :], dram["exchange"]).then_inc(exchange_in, 16)
            sync.wait_ge(line_out, 1)
            sync.dma_start(scratch.ap(), line[:, :]).then_inc(stored, 16)
            sync.wait_ge(stored, 16)
            for half in range(2):
                lo = half * pairs
                sync.dma_start(shifted[:, lo:lo + pairs, :],
                               bass.AP(tensor=scratch, offset=lo * 512, ap=[[1, P], [512, pairs], [1, T]])).then_inc(back, 16)

        @block.tensor
        def _(pe):
            pe.wait_ge(loaded, 48)
            pe.matmul(line_acc[:, :], table[:, :], onehot[:, :], start=True, stop=True).then_inc(lined, 1)
            pe.wait_ge(exchange_in, 16)
            pe.wait_ge(back, 32)
            for n in range(pairs):
                if n >= 4:
                    pe.wait_ge(copied, n - 3)
                pe.matmul(acc[:, n % 4, :, :], exchange[:, :], shifted[:, 2 * n:2 * n + 2, :],
                          start=True, stop=True).then_inc(filled, 1)

        @block.scalar
        def _(act):
            act.wait_ge(lined, 1)
            act.activation(line[:, :], line_acc[:, :], ACT.Copy).then_inc(line_out, 1)
            act.wait_ge(dotted, 1)
            act.activation(dots[:, :, :], dots[:, :, :], ACT.Exp).then_inc(exped, 1)
            for n in range(pairs):
                act.wait_ge(filled, n + 1)
                act.activation(bias[:, 2 * n:2 * n + 2, :], acc[:, n % 4, :, :], ACT.Copy).then_inc(copied, 1)

        @block.vector
        def _(dve):
            chain = Chain(dve, ordered)
            chain(dve.memset(cmp_bias[:, :, :, :], NEG))
            dve.wait_ge(cols_loaded, 16)
            at = col_at("lam")
            lam = cols[:, at:at + 512].rearrange("p (l a b d) -> p l a b d", l=2, a=2, b=2)
            for layer in range(2):
                last = dve.tensor_tensor(prod[:, layer, :, :], lam[:, layer, :, 0, :], lam[:, layer, :, 1, :], ALU.mult)
            chain(last)
            dve.tensor_reduce(dots[:, :, :], prod[:, :, :, :], X_AXIS, ALU.add).then_inc(dotted, 1)
            dve.wait_ge(exped, 1)
            for layer in range(2):
                init = 0.8 - 0.6 * math.exp(-0.3 * layer)
                dve.tensor_scalar(neg_lam[:, layer:layer + 1], dots[:, layer, 1:2], dots[:, layer, 0:1], -init,
                                  ALU.subtract, ALU.add)
            dve.wait_ge(copied, pairs)
            heads = slice(B_HEAD0, B_HEAD0 + 8)
            dve.tensor_copy(cmp_bias[:, 0, :, 0:7], bias[:, heads, 159:159 + 16 * 6 + 1:16])
            dve.tensor_copy(cmp_bias[:, 1, :, 0:N_CMP], bias[:, heads, 31:31 + 16 * 14 + 1:16])


def compress_stage(nc, W, layer, X, kc, vc, const):
    first = W.take("cmp%d" % layer)
    N = 3 * 16
    hid_hi_name = "cmp%d_hid" % layer
    with nc.sbuf_tensor(hid_hi_name, [P, 4, 2 * 16], F32) as hid, \
            nc.sbuf_tensor(hid_hi_name + "h", [P, 4, 2 * 16], F32R) as hid_hi, \
            nc.sbuf_tensor(hid_hi_name + "l", [P, 4, 2 * 16], F32R) as hid_lo, \
            nc.sbuf_tensor(hid_hi_name + "p", [P, 4], F32) as pos_sum:
        jobs = []
        for kv in range(2):
            for hc in range(2):
                jobs.append([])
            for pp in range(16):
                part = 2 * first + 8 * kv + pp // 2
                x = [b[:, :, 2 * pp:2 * pp + 16 * 15 + 1:16] for b in X(kv)]
                for hc in range(2):
                    jobs[2 * kv + hc].append((part, W.stationary(part, (pp % 2) * 256 + hc * P, x)))
        with stage(nc, "cmp1") as S:
            acc = S.ps("acc", [P, 4, 512])
            pos_out, geluv, hi_done = S.sem("pos_out"), S.sem("gelu"), S.sem("hi_done")
            block = S.block()

            @block.sync
            def _(sync):
                W.feed(sync, first, 8)

            @block.tensor
            def _(pe):
                for kv in range(2):
                    for pp in range(16):
                        for hc in range(2):
                            part, passes = jobs[2 * kv + hc][pp]
                            if pp % 2 == 0 and hc == 0:
                                W.wait(pe, part)
                            out = acc[:, 2 * kv + hc, 0:N].rearrange("p (g n) -> p g n", g=3)
                            last = run_passes(pe, out, passes, pp == 0, pp == 15)
                        if pp % 2 == 1:
                            last.then_inc(W.used, 1)

            @block.vector
            def _(dve):
                for part in range(16):
                    W.next_lo(dve, 2 * first + part)
                dve.wait_ge(W.used, 2 * first + 16)
                dve.tensor_copy(pos_sum[:, :], acc[:, :, 2 * 16]).then_inc(pos_out, 1)
                dve.wait_ge(hi_done, 1)
                dve.tensor_tensor(hid_lo[:, :, :], hid[:, :, :], hid_hi[:, :, :].bitcast(F32), ALU.subtract)

            @block.scalar
            def _(act):
                for part in range(16):
                    W.next_hi(act, 2 * first + part)
                act.wait_ge(pos_out, 1)
                for i in range(4):
                    last = act.activation(hid[:, i, :], acc[:, i, 0:2 * 16], ACT.Gelu_apprx_tanh,
                                          bias=pos_sum[:, i:i + 1])
                last.then_inc(geluv, 1)
                act.wait_ge(geluv, 1)
                act.activation(hid_hi[:, :, :], hid[:, :, :], ACT.Copy).then_inc(hi_done, 1)

        with stage(nc, "cmp2") as S:
            acc = S.ps("acc", [P, 2, 512])
            turned = S.ps("turned", [P, 2, P])
            vT = S.sb("vT", [P, 2, P])
            cleared, vT_done, v_turned = S.sem("cleared"), S.sem("vT_done"), S.sem("v_turned")
            block = S.block()
            part0 = 2 * (first + 8)

            @block.sync
            def _(sync):
                W.feed(sync, first + 8, 1)

            @block.scalar
            def _(act):
                for kv in range(2):
                    W.next_hi(act, part0 + kv)

            @block.tensor
            def _(pe):
                for kv in range(2):
                    W.wait(pe, part0 + kv)
                    for hc in range(2):
                        i = 2 * kv + hc
                        last = run_passes(pe, acc[:, kv, 0:2 * 16],
                                          W.stationary(part0 + kv, hc * P, (hid_hi[:, i, :], hid_lo[:, i, :])),
                                          hc == 0, hc == 1)
                    last.then_inc(W.used, 1)
                pe.wait_ge(vT_done, 1)
                for grp in range(2):
                    last = pe.transpose(turned[:, grp, :], vT[:, grp, :], const[:, 0:P])
                last.then_inc(v_turned, 1)

            @block.vector
            def _(dve):
                dve.memset(kc[:, :], 0.0)
                dve.memset(vT[:, :, :], 0.0).then_inc(cleared, 1)
                for kv in range(2):
                    W.next_lo(dve, part0 + kv)
                dve.wait_ge(cleared, 1)
                dve.wait_ge(W.used, part0 + 2)
                for grp in range(2):
                    mine = slice(grp * 16, grp * 16 + N_CMP)
                    dve.tensor_copy(kc[64 * grp:64 * grp + 64, 0:N_CMP], acc[64 * grp:64 * grp + 64, 0, mine])
                    last = dve.tensor_copy(vT[:, grp, 0:N_CMP], acc[:, 1, mine])
                last.then_inc(vT_done, 1)
                dve.wait_ge(v_turned, 1)
                dve.tensor_copy(vc[:, :, :], turned[:, :, :])


def small_gates(nc, name, rows, gates, cmp_gates, valid, X, pos):
    with stage(nc, name) as S:
        done, cleared = S.sem("done"), S.sem("cleared")
        block = S.block()

        @block.scalar
        def _(act):
            act.activation(gates[:, :, :], rows[:, :, 384:408], ACT.Sigmoid).then_inc(done, 1)

        @block.vector
        def _(dve):
            dve.memset(X[:, :, 0:2, T:XT], 0.0)
            dve.memset(X[64:128, :, 0:2, T - 1:T], 0.0)
            dve.memset(X[:, :, 2, :], 0.0).then_inc(cleared, 1)
            dve.wait_ge(cleared, 1)
            dve.tensor_copy(X[:, :, 2, 0:31:2], pos.rearrange("p (kv pp) -> p kv pp", kv=2))
            dve.wait_ge(done, 1)
            by = gates[:, :, :].rearrange("p t (h b) -> p t h b", b=3)
            dve.tensor_scalar(cmp_gates[:, 0, :], by[:, 0, :, 0], valid, None, ALU.mult)
            dve.tensor_copy(cmp_gates[:, 1, :], by[:, 1, :, 0])


def causal_units(q, k, v, bias, tt, **more):
    nk = P * (tt + 1)
    return Unit(q[:, tt * P:(tt + 1) * P], k[:, 0:nk], v, nk, 64 ** -0.5, bias=bias[:, 2 * P - nk:2 * P], **more)


def second_layer(nc, W, layer, h, bias, cmp_bias, neg_lam, cols, const, dram):
    ones, ident = const[:, P:2 * P], const[:, 0:P]
    n = str(layer)

    def norm_to(dst, which, name):
        at = col_at("norms") + 32 * layer + 8 * which
        norm(nc, name, lambda c: h[:, c, 0:T], None, KD, T, ones, lambda c, s: cols[:, at + c:at + c + 1], pair=dst)

    with ExitStack() as ctx:
        def sb(name, shape, dt=F32):
            return ctx.enter_context(nc.sbuf_tensor("second%d_%s" % (layer, name), shape, dt))

        x_hi, x_lo = sb("x_hi", [P, KD, T], F32R), sb("x_lo", [P, KD, T], F32R)
        x = split_pair(x_hi, x_lo)
        norm_to(x, 0, "ffn1n")
        feed_forward(nc, W, "ffn1_" + n, x, h)
        norm_to(x, 1, "attn_n")
        merged = sb("merged", [P, KD, T])
        with ExitStack() as inner:
            def tmp_sb(name, shape, dt=F32):
                return inner.enter_context(nc.sbuf_tensor("second%d_%s" % (layer, name), shape, dt))

            y = tmp_sb("y", [P, 3, 4, T])
            with ExitStack() as attn:
                def at_sb(name, shape, dt=F32):
                    return attn.enter_context(nc.sbuf_tensor("second%d_%s" % (layer, name), shape, dt))

                heads = at_sb("heads", [P, 19, T])
                X = at_sb("X", [P, 2, 3, XT])
                X_hi, X_lo = at_sb("X_hi", [P, 2, 3, XT], F32R), at_sb("X_lo", [P, 2, 3, XT], F32R)
                av = at_sb("av", [P, 2, 512])
                rows = at_sb("rows", [P, 2, 512])
                kc = at_sb("kc", [P, P])
                vc = at_sb("vc", [P, 2, P])
                gates = at_sb("gates", [P, 2, 24])
                cmp_gates = at_sb("cmp_gates", [P, 2, 8])
                first = W.take("in_cols" + n)

                def evacuate(act, chain, c, ps):
                    if c < 19:
                        return act.activation(heads[:, c, :], ps[:, 0:T], ACT.Copy)
                    for g in range(2):
                        act.activation(X[0:64, c - 19, g, 0:T], ps[64 * g:64 * g + 64, 0:T], ACT.Copy)
                        last = act.activation(X[64:128, c - 19, g, 0:T - 1], ps[64 * g:64 * g + 64, 1:T], ACT.Copy)
                    return last

                products(nc, W, "in_cols", first, 21, column_jobs(W, first, 21, KD, T, x),
                         evacuate, "scalar")
                first = W.take("in_rows" + n)
                row_products(nc, W, "in_rows", first, 2, lambda k, tt: (x_hi[:, k, tt * P:(tt + 1) * P], x_lo[:, k, tt * P:(tt + 1) * P]), 2,
                             lambda act, half, tt, ps: act.activation((av, rows)[half][:, tt, :], ps, ACT.Copy))
                pos_at = col_at("pos") + 32 * layer
                small_gates(nc, "small_gates", rows, gates, cmp_gates, cols[:, col_at("valid"):col_at("valid") + 1],
                            X, cols[:, pos_at:pos_at + 32])
                split_stage(nc, "X_split", *(b[:, :, :, :].rearrange("p a g t -> p (a g t)") for b in (X, X_hi, X_lo)))
                compress_stage(nc, W, layer, lambda kv: (X_hi[:, kv, :, :], X_lo[:, kv, :, :]), kc, vc, const)

                units = []
                for head in range(4):
                    for tt in range(2):
                        for c in range(2):
                            half = slice(64 * c, 64 * c + 64)
                            units.append(causal_units(
                                heads[half, head, :], heads[half, 4 + head, :],
                                lambda b, head=head: av[:, b, head * P:(head + 1) * P], bias[:, head, :], tt,
                                weight=neg_lam[:, layer:layer + 1] if c else None, first=c == 0, end=c == 1,
                                out=(0, P, y[:, 0, head, tt * P:(tt + 1) * P])))
                for g in range(2):
                    half = slice(64 * g, 64 * g + 64)
                    for r in range(4):
                        head = 4 * g + r
                        for tt in range(2):
                            tok = slice(tt * P, (tt + 1) * P)
                            out = (64 * g, 64 * g + 64, y[half, 1, r, tok])
                            units.append(Unit(heads[half, 8 + r, tok], kc[half, :], lambda b, g=g: vc[:, g, :], P,
                                              64 ** -0.5, bias=cmp_bias[:, tt, head, :],
                                              weight=cmp_gates[:, tt, head:head + 1], first=True, end=False))
                            for br in (1, 2):
                                gate = gates[:, tt, 3 * head + br:3 * head + br + 1]
                                units.append(causal_units(
                                    heads[half, 8 + r, :], heads[half, 11 + br, :],
                                    lambda b, br=br: rows[:, b, (br - 1) * P:br * P], bias[:, B_HEAD0 + head, :], tt,
                                    weight=gate, first=False, end=br == 2, out=out))
                    for r in range(4):
                        head = 4 * g + r
                        at = col_at("sinks") + 8 * layer + head
                        for tt in range(2):
                            units.append(causal_units(
                                heads[half, 14 + r, :], heads[half, 18, :], lambda b: rows[:, b, 2 * P:3 * P],
                                bias[:, C_HEAD0 + head, :], tt, sink=cols[:, at:at + 1],
                                out=(64 * g, 64 * g + 64, y[half, 2, r, tt * P:(tt + 1) * P])))
                attention(nc, "attn", units, ident)
            at = col_at("subln") + layer
            norm(nc, "subln", lambda c: y[:, 0, c, :], lambda c: y[:, 0, c, :], 1, T, ones, lambda c, s: cols[:, at:at + 1],
                 groups=4, post=0.2 + 0.6 * math.exp(-0.3 * layer))
            y_hi, y_lo = tmp_sb("y_hi", [P, 3, 4, T], F32R), tmp_sb("y_lo", [P, 3, 4, T], F32R)
            split_stage(nc, "y_split", *(b[:, :, :, :].rearrange("p b k t -> p (b k t)") for b in (y, y_hi, y_lo)))
            sig = tmp_sb("sig", [P, 3, KD, T])
            term = tmp_sb("term", [P, 2, T])
            first = W.take("gates" + n)
            products(nc, W, "gates", first, 24, column_jobs(W, first, 24, KD, T, x),
                     lambda act, chain, c, ps: act.activation(sig[:, c // 8, c % 8, :], ps[:, 0:T], ACT.Sigmoid), "scalar")
            first = W.take("branch" + n)
            jobs = []
            for br in range(3):
                jobs += column_jobs(W, first + 4 * br, 8, 4, T, split_pair(y_hi[:, br, :, :], y_lo[:, br, :, :]))

            def merge(dve, chain, c, ps):
                br, j = c // 8, c % 8
                if br == 0:
                    return dve.tensor_tensor(merged[:, j, :], ps[:, 0:T], sig[:, br, j, :], ALU.mult)
                chain(dve.tensor_tensor(term[:, c % 2, :], ps[:, 0:T], sig[:, br, j, :], ALU.mult))
                return dve.tensor_tensor(merged[:, j, :], merged[:, j, :], term[:, c % 2, :], ALU.add)

            products(nc, W, "branch", first, 12, jobs, merge, "vector")
        first = W.take("out" + n)
        m_hi, m_lo = sb("merged_hi", [P, KD, T], F32R), sb("merged_lo", [P, KD, T], F32R)
        split_stage(nc, "merged_split", *(b[:, :, :].rearrange("p k t -> p (k t)") for b in (merged, m_hi, m_lo)))
        products(nc, W, "out", first, 8, column_jobs(W, first, 8, KD, T, split_pair(m_hi, m_lo)),
                 lambda dve, chain, c, ps: dve.tensor_tensor(h[:, c, 0:T], h[:, c, 0:T], ps[:, 0:T], ALU.add), "vector")
        norm_to(x, 2, "ffn2n")
        feed_forward(nc, W, "ffn2_" + n, x, h)
        norm_to(x, 3, "ple_n")
        p_in = sb("p", [P, 2, T])
        p_hi, p_lo = sb("p_hi", [P, 2, T], F32R), sb("p_lo", [P, 2, T], F32R)
        split_stage(nc, "p_split", *(b[:, :, :].rearrange("p k t -> p (k t)") for b in (p_in, p_hi, p_lo)),
                    load=dram["p" + n], pieces=1)
        pw = sb("pw", [P, KD, T])
        first = W.take("ple_w" + n)
        products(nc, W, "ple_w", first, 2, column_jobs(W, first, 8, 2, T, split_pair(p_hi, p_lo)),
                 lambda act, chain, c, ps: act.activation(pw[:, c, :], ps[:, 0:T], ACT.Copy), "scalar")
        first = W.take("ple_gate" + n)
        products(nc, W, "ple_gate", first, 8, column_jobs(W, first, 8, KD, T, x),
                 lambda act, chain, c, ps: act.activation(merged[:, c, :], ps[:, 0:T], ACT.Sigmoid), "scalar")
        with stage(nc, "ple_add") as S:
            done = S.sem("done")
            block = S.block()

            @block.vector
            def _(dve):
                dve.tensor_tensor(pw[:, :, :], pw[:, :, :], merged[:, :, :], ALU.mult).then_inc(done, 1)
                dve.wait_ge(done, 1)
                dve.tensor_tensor(h[:, :, 0:T], h[:, :, 0:T], pw[:, :, :], ALU.add)


def store_stage(nc, y, out):
    with stage(nc, "store") as S:
        stored = S.sem("stored")
        block = S.block()

        @block.sync
        def _(sync):
            sync.dma_start(out, y[:, :, :].rearrange("p k t -> p (k t)")).then_inc(stored, 16)
            sync.wait_ge(stored, 16)


def build(nc, dram, out, debug=None, upto=99):
    def dump(name, ap):
        if debug is not None:
            debug(name, ap)

    STAGES[0] = 0
    cols = nc.alloc_sbuf_tensor("cols_sb", [P, N_COLS], F32)
    const = nc.alloc_sbuf_tensor("const_sb", [P, N_CONST], F32)
    modulation = nc.alloc_sbuf_tensor("modulation", [P, 2, 48, 2], F32)
    scales = nc.alloc_sbuf_tensor("scales", [P, 2, 2, 2, KD], F32)
    h = nc.alloc_sbuf_tensor("h", [P, KD, 2 * T], F32)
    W = Weights(nc, dram["w_tiles"], dram["peer_tiles"])
    modulation_stage(nc, W, h, modulation, scales, cols, const, dram)
    even_mixer(nc, W, h, modulation, scales, cols, const, dram["rope"])
    dump("h_even", h)
    if upto <= 1:
        return
    for s in (LAT, CTX):
        peer(nc, W, 0, s, h[:, :, s * T:(s + 1) * T], lambda c, s=s: scales[:, 0, 1, s, c:c + 1],
             lambda c, s=s: modulation[:, 0, 24 + c, s:s + 1], lambda c, s=s: modulation[:, 0, 40 + c, s:s + 1], const, dram)
        if upto <= 2:
            dump("h_peer", h)
            return
    dump("h_peer0", h)
    odd_mixer(nc, W, h, modulation, scales, cols, const, dram["select"], dram["masks"])
    dump("h_odd", h)
    peer(nc, W, 1, LAT, h[:, :, 0:T], lambda c: scales[:, 1, 1, LAT, c:c + 1],
         lambda c: modulation[:, 1, 24 + c, LAT:LAT + 1], lambda c: modulation[:, 1, 40 + c, LAT:LAT + 1], const, dram)
    ones = const[:, P:2 * P]
    at = col_at("norm_f")
    norm(nc, "norm_f", lambda c: h[:, c, 0:T], lambda c: h[:, c, 0:T], KD, T, ones, lambda c, s: cols[:, at + c:at + c + 1])
    dump("h_first", h)
    with nc.sbuf_tensor("cols2_sb", [P, N_COLS2], F32) as cols2:
        with nc.sbuf_tensor("bias_sb", [P, N_BIAS, T], F32) as bias, \
                nc.sbuf_tensor("cmp_bias", [P, 2, 8, P], F32) as cmp_bias, nc.sbuf_tensor("neg_lam", [P, 2], F32) as neg_lam:
            bias_stage(nc, bias, cmp_bias, neg_lam, cols2, dram)
            for layer in range(2):
                second_layer(nc, W, layer, h, bias, cmp_bias, neg_lam, cols2, const, dram)
                dump("h_second%d" % layer, h)
        with nc.sbuf_tensor("y_out", [P, KD, T], F32) as y:
            at2 = col_at("final")
            norm(nc, "final", lambda c: h[:, c, 0:T], lambda c: y[:, c, :], KD, T, ones,
                 lambda c, s: cols2[:, at2 + c:at2 + c + 1])
            store_stage(nc, y, out)


def column_tiles(w):
    k = w.shape[0] // P
    per = KD // k
    n = -(-w.shape[1] // (P * per)) * per
    full = np.zeros((k * P, n * P), w.dtype)
    full[:, :w.shape[1]] = w
    a = full.reshape(k, P, n // per, per, P).transpose(2, 1, 3, 0, 4)
    return a.reshape(n // per, P, TILE)


def row_tiles(w):
    n = -(-w.shape[1] // 512)
    full = np.zeros((w.shape[0], n * 512), w.dtype)
    full[:, :w.shape[1]] = w
    return full.reshape(4, 2, P, n, 512).transpose(3, 0, 2, 1, 4).reshape(4 * n, P, TILE)


def padded_tile(a):
    a = a.reshape(P, -1)
    out = np.zeros((1, P, TILE), a.dtype)
    out[0, :, :a.shape[1]] = a
    return out


def swapped_rope(w):
    return np.concatenate([w[..., 16:32], w[..., 0:16]], axis=-1)


def pair_heads(w, axis):
    w = np.moveaxis(w, axis, 0)
    rest = w.shape[1:]
    w = w.reshape((2, 4, 64) + rest).transpose((1, 0, 2) + tuple(range(3, 3 + len(rest)))).reshape((512,) + rest)
    return np.moveaxis(w, 0, axis)


def feed_forward_tiles(wi, wo):
    gate, up = column_tiles(wi[:, :D_FF]), column_tiles(wi[:, D_FF:])
    down = wo.reshape(FC, P, D)
    out = [gate[0], up[0]]
    for c in range(FC):
        if c + 1 < FC:
            out += [gate[c + 1], up[c + 1]]
        out.append(down[c])
    return np.stack(out)


def layout_weights(a):
    f = {}
    f["mod"] = np.concatenate([row_tiles(a["w_mod"][i]) for i in range(2)])
    w = a["even_w_in"][0]
    kr = w[:, 384:416]
    conv = [w[:, 416 + 512 * i:928 + 512 * i].reshape(D, 4, P) for i in range(3)]
    triples = np.stack([conv[1], conv[2], conv[0]], axis=2).reshape(D, 1536)
    f["even_in"] = column_tiles(np.concatenate([w[:, :384], np.zeros((D, 64), w.dtype), kr, swapped_rope(kr), triples], 1))
    uq = a["mla_w_uq"][0].reshape(256, MLA_HEADS, 96)
    f["uq"] = column_tiles(np.concatenate([uq, swapped_rope(uq[..., 64:])], -1).reshape(256, 1024))
    f["ukv"] = a["mla_w_ukv"][0].reshape(P, MLA_HEADS, 2, 64).transpose(0, 2, 1, 3).reshape(1, P, TILE)
    f["even_out"] = column_tiles(a["even_w_out"][0])
    for layer in range(2):
        f["peer_q%d" % layer] = column_tiles(a["peer_w_q"][layer])
    w = a["odd_w_in"][0]
    gates = np.zeros((D, 4, 32), w.dtype)
    gates[:, :, :4] = w[:, 2048:2064].reshape(D, 4, 4)
    f["odd_qk"] = column_tiles(np.concatenate([w[:, :1024], gates.reshape(D, P)], 1))
    f["odd_v"] = row_tiles(w[:, 1024:2048])
    f["odd_gate"] = column_tiles(w[:, 2064:])
    f["odd_out"] = column_tiles(a["odd_w_out"][0])
    for i in range(2):
        w, n = a["w_in_2"][i], str(i)
        f["ffn1_" + n] = feed_forward_tiles(a["ffn1_wi_2"][i], a["ffn1_wo_2"][i])
        f["ffn2_" + n] = feed_forward_tiles(a["ffn2_wi_2"][i], a["ffn2_wo_2"][i])
        f["in_cols" + n] = column_tiles(np.concatenate([
            w[:, 0:1024], pair_heads(w[:, 1536:2048], 1), w[:, 2304:2432], w[:, 2560:2688],
            pair_heads(w[:, 2840:3352], 1), w[:, 3352:3480], w[:, 2048:2304]], 1))
        f["in_rows" + n] = row_tiles(np.concatenate([
            w[:, 1024:1536], w[:, 2432:2560], w[:, 2688:2816], w[:, 3480:3608], w[:, 2816:2840]], 1))
        w1 = a["nsa_cmp_w1_2"][i].reshape(2, 4, 4, P, 256).transpose(0, 1, 3, 2, 4).reshape(8, P, TILE)
        w2 = a["nsa_cmp_w2_2"][i].reshape(2, 2, P, 64)
        w2 = np.concatenate([w2, w2], -1).transpose(2, 0, 1, 3).reshape(P, 2, 2 * P)
        w2 = np.concatenate([w2, np.zeros_like(w2)], -1)
        f["cmp" + n] = np.concatenate([w1, padded_tile(w2)])
        f["gates" + n] = column_tiles(w[:, 3608:])
        wb = a["w_branch_2"][i]
        f["branch" + n] = np.concatenate([column_tiles(x) for x in (wb[0], pair_heads(wb[1], 0), pair_heads(wb[2], 0))])
        f["out" + n] = column_tiles(a["w_out_2"][i])
        f["ple_w" + n] = column_tiles(a["w_ple_2"][i])
        f["ple_gate" + n] = column_tiles(a["w_ple_gate_2"][i])
    bases, size = tile_bases()
    out = np.empty((size["w"], P, TILE), np.float32)
    for name, n, source in stream_plan():
        if source == "w":
            assert f[name].shape == (n, P, TILE), (name, f[name].shape)
            out[bases[name]:bases[name] + n] = f[name]
    return out.reshape(-1, TILE)


def layout_experts(u, v):
    out = np.empty((2, PEER_TILES, P, TILE), u.dtype)
    for layer in range(2):
        ut = u[layer].reshape(NKEYS, NKEYS, KD, P).transpose(1, 3, 2, 0).reshape(NKEYS, P, TILE)
        vt = v[layer].reshape(NKEYS, NKEYS, D).transpose(1, 0, 2)
        out[layer, 0] = ut[0]
        out[layer, 1:-1:2] = ut[1:]
        out[layer, 2:-1:2] = vt[:-1]
        out[layer, -1] = vt[-1]
    return out.reshape(-1, TILE)


def features(v):
    return np.ascontiguousarray(v.reshape(-1, P).T)


def spread(v):
    return np.broadcast_to(v.reshape(1, -1), (P, v.size))


def layout_columns(a):
    gate_b = np.zeros((4, 32), np.float32)
    gate_b[:, :4] = a["mlstm_gate_b"][0].reshape(4, 4)
    pos = a["nsa_cmp_pos_2"].reshape(4, 16, P)
    parts = {
        "norm1": features(a["norm1_g"]), "norm2": features(a["norm2_g"]), "b_mod": features(a["b_mod"]),
        "q_norm": features(a["mla_q_norm"]), "kv_norm": features(a["mla_kv_norm"]), "conv": features(a["conv_w"]),
        "head_g": features(a["mlstm_head_g"]), "norm_f": features(a["norm_f_g"]), "norms": features(a["norm_g_2"]),
        "subln": features(a["diff_subln_2"]), "final": features(a["final_norm_2"]), "gate_b": gate_b.reshape(P, 1),
        "pos": pos.reshape(64, P).T, "lam": spread(a["diff_lambda_2"]), "sinks": spread(a["swa_sinks_2"]),
        "valid": (np.arange(P) >= 31).astype(np.float32).reshape(P, 1),
    }
    for name, width in COLS + COLS2:
        assert parts[name].shape == (P, width), (name, parts[name].shape)
    return [np.concatenate([parts[name] for name, _ in columns], 1) for columns in (COLS, COLS2)]


def constants():
    const = np.concatenate([np.eye(P), np.ones((P, P)), np.tile(np.arange(P), (P, 1)), np.tile(np.arange(16), (P, 1))],
                           1).astype(np.float32)
    inv = np.float32(10000.0) ** (-np.arange(8, dtype=np.float32) / np.float32(8))
    t = np.arange(T)
    ang = np.concatenate([(t // 64).astype(np.float32)[:, None] * inv, (t % 64).astype(np.float32)[:, None] * inv], -1)
    cos, sin = np.cos(ang).T, np.sin(ang).T
    rope = np.zeros((P, 2 * T), np.float32)
    rope[64:96, T:] = 1.0
    rope[64:96, :T] = np.concatenate([cos, cos])
    rope[96:128, :T] = np.concatenate([-sin, sin])
    dist = 255 - np.arange(512)
    n = np.maximum(dist, 0)
    nf = np.maximum(n, 1).astype(np.float32)
    large = 16 + (np.log(nf / 16) / np.float32(math.log(8)) * 16).astype(np.int32)
    bucket = np.where(n < 16, n, np.minimum(large, 31))
    onehot = np.zeros((34, 512), np.float32)
    seen = dist >= 0
    onehot[bucket[seen], np.nonzero(seen)[0]] = 1.0
    onehot[32] = ~seen
    onehot[33] = dist >= 128
    masked = np.zeros((2, N_BIAS), np.float32)
    masked[0] = NEG
    masked[1, C_HEAD0:] = NEG
    select = np.zeros((P, ML_HEADS, P), np.float32)
    for hd in range(ML_HEADS):
        select[32 + hd, hd] = select[96 + hd, hd] = 1.0
    q = np.arange(T).reshape(2, P).T[:, :, None]
    s = np.arange(T)[None, None, :]
    masks = np.stack([s <= q, s >= q], 1).astype(np.float32)
    return {"const": const, "rope": rope, "onehot": onehot,
            "exchange": np.eye(P, dtype=np.float32)[::-1], "masked": masked, "select": select.reshape(P, -1),
            "masks": masks.reshape(P, -1)}


def layout(inputs):
    a = {k: np.asarray(v) for k, v in inputs.items()}

    def tokens(x):
        return x.T.reshape(-1, P, x.shape[0]).transpose(1, 0, 2)

    arrays = constants()
    arrays["w_tiles"] = layout_weights(a)
    arrays["peer_tiles"] = layout_experts(a["peer_u"], a["peer_v"])
    arrays["cols"], arrays["cols2"] = layout_columns(a)
    for layer in range(2):
        arrays["subkeys%d" % layer] = a["peer_subkeys"][layer].reshape(2 * PH, NKEYS, P).transpose(2, 0, 1).reshape(P, -1)
    arrays["tokens"] = np.concatenate([tokens(a["x"][0]), tokens(a["ctx"][0])], 2).reshape(P, -1)
    arrays["c_cols"] = np.stack([features(a["c"][0]), features(a["c_ctx"])], 2).reshape(P, -1)
    arrays["rel_bias"] = a["rel_bias_2"]
    for i in range(2):
        arrays["p%d" % i] = tokens(a["p_2"][i, 0]).reshape(P, -1)
    return {k: np.ascontiguousarray(v) for k, v in arrays.items()}


def kernel(**inputs):
    import concourse.bacc as bacc
    from concourse.bass_utils import run_bass_kernel_spmd

    arrays = layout(inputs)
    nc = bacc.Bacc("TRN2", target_bir_lowering=False, num_devices=1)
    dram = {name: nc.dram_tensor("in_" + name, x.shape, mybir.dt.from_np(x.dtype), kind="ExternalInput").ap()
            for name, x in arrays.items()}
    out = nc.dram_tensor("out_y", (P, KD * T), F32, kind="ExternalOutput").ap()
    build(nc, dram, out)
    r = run_bass_kernel_spmd(nc, [{"in_" + name: x for name, x in arrays.items()}], core_ids=[0])
    y = r.results[0]["out_y"].reshape(P, KD, T)
    return y.transpose(2, 1, 0).reshape(1, T, D)
```
